# Optimizing a Trainium2 kernel written in Bass

```python
import jax, jax.numpy as jnp
from jax import lax
import numpy as np

D_MODEL = 1024
BATCH = 1
SEQ = 512
DEPTH = 2

CHUNK = 64
N_MIXERS = 2
N_CONV_LAYERS = (DEPTH + 1) // 2
N_SSD_LAYERS = DEPTH // 2
N_MOD = 6
EPS = 1e-6

SC_WIDTH = 3

M_EXPAND = 2
M_D_INNER = M_EXPAND * D_MODEL
M_HEAD_DIM = 64
M_N_HEADS = M_D_INNER // M_HEAD_DIM
M_N_GROUPS = 8
M_HEADS_PER_GROUP = M_N_HEADS // M_N_GROUPS
M_D_STATE = 128
M_CONV_WIDTH = 4
M_CONV_DIM = M_D_INNER + 2 * M_N_GROUPS * M_D_STATE
M_IN_DIM = M_D_INNER + M_CONV_DIM + M_N_HEADS
SSD_CHUNK = CHUNK

D_FF = -(-8 * D_MODEL // (3 * 256)) * 256


def rms_normalize(x):
    xf = x.astype(jnp.float32)
    xf = xf * lax.rsqrt(jnp.mean(xf * xf, axis=-1, keepdims=True) + EPS)
    return xf.astype(x.dtype)

def rmsnorm(x, g):
    return rms_normalize(x) * g

def causal_depthwise_conv(x, w):
    k_width = w.shape[0]
    s = x.shape[1]
    xp = jnp.pad(x, ((0, 0), (k_width - 1, 0), (0, 0)))
    y = w[0] * xp[:, 0:s]
    for k in range(1, k_width):
        y = y + w[k] * xp[:, k:k + s]
    return y

def short_conv_mixer(h, w_in, conv_w, w_out):
    b_gate, c_gate, v = jnp.split(h @ w_in, 3, axis=-1)
    u = causal_depthwise_conv(c_gate * v, conv_w)
    return (b_gate * u) @ w_out

def ssd_chunked(xh, dt, a, bm, cm):
    bsz, s, g, r, p = xh.shape
    n = bm.shape[-1]
    nc, l = s // SSD_CHUNK, SSD_CHUNK
    dtype = xh.dtype
    xdt = (xh * dt[..., None].astype(dtype)).reshape(bsz, nc, l, g, r, p)
    bm = bm.reshape(bsz, nc, l, g, n)
    cm = cm.reshape(bsz, nc, l, g, n)
    cs = jnp.cumsum((dt * a).reshape(bsz, nc, l, g, r), axis=2)
    causal = jnp.tril(jnp.ones((l, l), dtype=bool))[None, None, :, :, None, None]
    seg = cs[:, :, :, None] - cs[:, :, None]
    decay = jnp.exp(jnp.where(causal, seg, -jnp.inf)).astype(dtype)
    cb = jnp.einsum('bclgn,bcsgn->bclsg', cm, bm)
    y_diag = jnp.einsum('bclsgr,bcsgrp->bclgrp', cb[..., None] * decay, xdt)
    decay_to_end = jnp.exp(cs[:, :, -1:] - cs).astype(dtype)
    states = jnp.einsum('bclgn,bclgr,bclgrp->bcgrpn', bm, decay_to_end, xdt)
    chunk_decay = jnp.exp(cs[:, :, -1]).astype(dtype)

    def step(state, inp):
        st, dec = inp
        return state * dec[..., None, None] + st, state

    h0 = jnp.zeros((bsz, g, r, p, n), dtype)
    _, prev = lax.scan(step, h0, (jnp.moveaxis(states, 1, 0), jnp.moveaxis(chunk_decay, 1, 0)))
    prev = jnp.moveaxis(prev, 0, 1)
    y_off = jnp.einsum('bclgn,bcgrpn,bclgr->bclgrp', cm, prev, jnp.exp(cs).astype(dtype))
    return (y_diag + y_off).reshape(bsz, s, g, r, p)

def ssd_mixer(h, w_in, conv_w, conv_b, dt_bias, a_log, d_skip, norm_g, w_out):
    bsz, s, _ = h.shape
    g, r, p, n = M_N_GROUPS, M_HEADS_PER_GROUP, M_HEAD_DIM, M_D_STATE
    z, xbc, dt_raw = jnp.split(h @ w_in, [M_D_INNER, M_D_INNER + M_CONV_DIM], axis=-1)
    xbc = jax.nn.silu(causal_depthwise_conv(xbc, conv_w) + conv_b)
    xs, bm, cm = jnp.split(xbc, [M_D_INNER, M_D_INNER + g * n], axis=-1)
    xs = xs.reshape(bsz, s, g, r, p)
    bm = bm.reshape(bsz, s, g, n)
    cm = cm.reshape(bsz, s, g, n)
    dt = jax.nn.softplus(dt_raw.astype(jnp.float32) + dt_bias.astype(jnp.float32)).reshape(bsz, s, g, r)
    a = -jnp.exp(a_log.astype(jnp.float32)).reshape(g, r)
    y = ssd_chunked(xs, dt, a, bm, cm) + d_skip.reshape(g, r)[:, :, None] * xs
    y = y.reshape(bsz, s, M_D_INNER) * jax.nn.silu(z)
    y = rms_normalize(y.reshape(bsz, s, g, M_D_INNER // g)).reshape(bsz, s, M_D_INNER) * norm_g
    return y @ w_out

def swiglu_ffn(h, w_in, w_out):
    gate, up = jnp.split(h @ w_in, 2, axis=-1)
    return (jax.nn.silu(gate) * up) @ w_out

def first_inputs(seed: int = 0) -> dict:
    key = jax.random.key(seed)
    ks = jax.random.split(key, 20)
    f32 = jnp.float32
    nrm = lambda k, shape, scale: jax.random.normal(k, shape, f32) * scale
    dt_init = jnp.exp(jax.random.uniform(ks[11], (N_SSD_LAYERS, M_N_HEADS), f32,
                                         np.log(1e-3), np.log(1e-1)))
    return {
        "x": nrm(ks[0], (BATCH, SEQ, D_MODEL), 1.0),
        "c": nrm(ks[1], (BATCH, D_MODEL), 1.0),
        "ada_w": nrm(ks[2], (D_MODEL, DEPTH * N_MOD * D_MODEL), 0.5 * D_MODEL ** -0.5),
        "ada_b": nrm(ks[3], (DEPTH * N_MOD * D_MODEL,), 0.02),
        "norm_g": 1.0 + nrm(ks[4], (DEPTH, 4, D_MODEL), 0.02),
        "a_w_in": nrm(ks[5], (N_CONV_LAYERS, D_MODEL, 3 * D_MODEL), D_MODEL ** -0.5),
        "a_conv_w": nrm(ks[6], (N_CONV_LAYERS, SC_WIDTH, D_MODEL), SC_WIDTH ** -0.5),
        "a_w_out": nrm(ks[7], (N_CONV_LAYERS, D_MODEL, D_MODEL), D_MODEL ** -0.5),
        "m_w_in": nrm(ks[8], (N_SSD_LAYERS, D_MODEL, M_IN_DIM), D_MODEL ** -0.5),
        "m_conv_w": nrm(ks[9], (N_SSD_LAYERS, M_CONV_WIDTH, M_CONV_DIM), M_CONV_WIDTH ** -0.5),
        "m_conv_b": nrm(ks[10], (N_SSD_LAYERS, M_CONV_DIM), 0.02),
        "m_dt_bias": dt_init + jnp.log(-jnp.expm1(-dt_init)),
        "m_a_log": jnp.log(jax.random.uniform(ks[12], (N_SSD_LAYERS, M_N_HEADS), f32, 1.0, 16.0)),
        "m_d": 1.0 + nrm(ks[13], (N_SSD_LAYERS, M_N_HEADS), 0.1),
        "m_norm_g": 1.0 + nrm(ks[14], (N_SSD_LAYERS, M_D_INNER), 0.02),
        "m_w_out": nrm(ks[15], (N_SSD_LAYERS, M_D_INNER, D_MODEL), M_D_INNER ** -0.5),
        "f_w_in": nrm(ks[16], (DEPTH, D_MODEL, 2 * D_FF), D_MODEL ** -0.5),
        "f_w_out": nrm(ks[17], (DEPTH, D_FF, D_MODEL), D_FF ** -0.5),
    }

def first_block(x, c, ada_w, ada_b, norm_g, a_w_in, a_conv_w, a_w_out, m_w_in, m_conv_w,
              m_conv_b, m_dt_bias, m_a_log, m_d, m_norm_g, m_w_out, f_w_in, f_w_out):
    bsz = x.shape[0]
    mod = (jax.nn.silu(c) @ ada_w + ada_b).reshape(bsz, DEPTH, 2, 3, D_MODEL)
    for i in range(DEPTH):
        j = i // N_MIXERS
        shift, scale, gate = (mod[:, i, 0, k][:, None, :] for k in range(3))
        h = rmsnorm(x, norm_g[i, 0]) * (1.0 + scale) + shift
        if i % N_MIXERS == 0:
            y = short_conv_mixer(h, a_w_in[j], a_conv_w[j], a_w_out[j])
        else:
            y = ssd_mixer(h, m_w_in[j], m_conv_w[j], m_conv_b[j], m_dt_bias[j], m_a_log[j],
                          m_d[j], m_norm_g[j], m_w_out[j])
        x = x + gate * rmsnorm(y, norm_g[i, 1])
        shift, scale, gate = (mod[:, i, 1, k][:, None, :] for k in range(3))
        h = rmsnorm(x, norm_g[i, 2]) * (1.0 + scale) + shift
        y = swiglu_ffn(h, f_w_in[i], f_w_out[i])
        x = x + gate * rmsnorm(y, norm_g[i, 3])
    return x


DEPTH_2 = 1

PLE_DIM = 256
GM_WIDTH = 512
GM_GROUPS = 8
GM_CHUNK = 128
HG_HEADS = 4
HG_KEY = 128
HG_VAL = 128
HG_CHUNK = 64
HG_KW = HG_HEADS * HG_KEY
HG_VW = HG_HEADS * HG_VAL
IN_SPLITS = [GM_WIDTH, GM_WIDTH, HG_KW, HG_KW, HG_VW, HG_VW, D_MODEL, D_MODEL]
IN_COLS = sum(IN_SPLITS)
N_GROUPS = 4
EXP_PER_GROUP = 8
N_EXPERTS = N_GROUPS * EXP_PER_GROUP
TOP_K = 2
D_EXPERT = 512
MOE_BLOCK = 128


def rmsnorm_2(x, g):
    xf = x.astype(jnp.float32)
    y = xf * lax.rsqrt(jnp.mean(xf * xf, axis=-1, keepdims=True) + EPS)
    return y.astype(x.dtype) * g

def layernorm(x, g, b):
    xf = x.astype(jnp.float32)
    mu = jnp.mean(xf, axis=-1, keepdims=True)
    var = jnp.mean(jnp.square(xf - mu), axis=-1, keepdims=True)
    y = (xf - mu) * lax.rsqrt(var + EPS)
    return y.astype(x.dtype) * g + b

def gmlp_branch(u, v, ln_g, ln_b, w_sp, b_sp):
    B, S, _ = u.shape
    n_c = S // GM_CHUNK
    dg = GM_WIDTH // GM_GROUPS
    v = layernorm(v, ln_g, ln_b).reshape(B, n_c, GM_CHUNK, GM_GROUPS, dg)
    mask = jnp.tril(jnp.ones((GM_CHUNK, GM_CHUNK), dtype=bool))
    w = jnp.where(mask[None], w_sp, jnp.zeros_like(w_sp))
    s = jnp.einsum('gts,bcsgd->bctgd', w, v) + b_sp.T[:, :, None]
    return u * s.reshape(B, S, GM_WIDTH)

def hgrn2_branch(q, f_raw, i_in, og, lb, norm_g):
    B, S, _ = q.shape
    C = HG_CHUNK
    n_c = S // C
    dt = q.dtype
    qf = jax.nn.silu(q.astype(jnp.float32)).reshape(B, n_c, C, HG_HEADS, HG_KEY)
    f = lb + (1.0 - lb) * jax.nn.sigmoid(f_raw.astype(jnp.float32))
    log_f = jnp.log(f).reshape(B, n_c, C, HG_HEADS, HG_KEY)
    k = (1.0 - f).reshape(B, n_c, C, HG_HEADS, HG_KEY)
    v = i_in.astype(jnp.float32).reshape(B, n_c, C, HG_HEADS, HG_VAL)
    b = jnp.cumsum(log_f, axis=2)
    b_last = b[:, :, -1:]
    q_dec = qf * jnp.exp(b)
    k_inv = k * jnp.exp(-b)
    k_end = k * jnp.exp(b_last - b)
    mask = jnp.tril(jnp.ones((C, C), dtype=bool))
    att = jnp.einsum('bcthk,bcshk->bchts', q_dec, k_inv)
    att = jnp.where(mask, att, jnp.zeros_like(att))
    o_intra = jnp.einsum('bchts,bcshv->bcthv', att, v)
    dS = jnp.einsum('bcshk,bcshv->bchkv', k_end, v)
    decay = jnp.exp(b_last[:, :, 0])

    def step(s_prev, inp):
        dec, ds = inp
        return dec[..., None] * s_prev + ds, s_prev

    s0 = jnp.zeros((B, HG_HEADS, HG_KEY, HG_VAL), jnp.float32)
    _, s_starts = lax.scan(step, s0, (jnp.moveaxis(decay, 1, 0), jnp.moveaxis(dS, 1, 0)))
    o_inter = jnp.einsum('bcthk,cbhkv->bcthv', q_dec, s_starts)
    o = (o_intra + o_inter).reshape(B, S, HG_HEADS, HG_VAL)
    o = o * lax.rsqrt(jnp.mean(o * o, axis=-1, keepdims=True) + EPS)
    o = o * norm_g.astype(jnp.float32).reshape(HG_HEADS, HG_VAL)
    return o.reshape(B, S, HG_VW).astype(dt) * jax.nn.sigmoid(og)

def hier_moe(h, w_grp, w_exp, w1, w3, w2):
    B, S, D = h.shape
    T = B * S
    xt = h.reshape(T, D)
    grp_logits = (xt @ w_grp).astype(jnp.float32)
    grp_prob = jax.nn.softmax(grp_logits, axis=-1)
    p_g, g_sel = lax.top_k(grp_prob, 1)
    exp_logits = (xt @ w_exp).astype(jnp.float32).reshape(T, N_GROUPS, EXP_PER_GROUP)
    sel_logits = jnp.take_along_axis(exp_logits, g_sel[:, :, None], axis=1)[:, 0]
    top_l, top_e = lax.top_k(sel_logits, TOP_K)
    gate = jax.nn.softmax(top_l, axis=-1) * p_g

    A = T * TOP_K
    eid = (g_sel * EXP_PER_GROUP + top_e).reshape(A)
    tok = jnp.repeat(jnp.arange(T, dtype=jnp.int32), TOP_K)
    wa = gate.reshape(A)
    order = jnp.argsort(eid)
    eid_s, tok_s, w_s = eid[order], tok[order], wa[order]
    counts = jnp.bincount(eid, length=N_EXPERTS)
    padded = ((counts + MOE_BLOCK - 1) // MOE_BLOCK) * MOE_BLOCK
    pad_end = jnp.cumsum(padded)
    pad_start = pad_end - padded
    start = jnp.cumsum(counts) - counts
    rank = jnp.arange(A, dtype=jnp.int32) - start[eid_s]
    dest = pad_start[eid_s] + rank
    n_blk = -(-A // MOE_BLOCK) + N_EXPERTS
    P = n_blk * MOE_BLOCK
    buf = jnp.zeros((P, D), xt.dtype).at[dest].set(xt[tok_s])
    blk_start = jnp.arange(n_blk, dtype=jnp.int32) * MOE_BLOCK
    blk_e = jnp.minimum(jnp.searchsorted(pad_end, blk_start, side='right'), N_EXPERTS - 1)

    def expert_block(args):
        xb, e = args
        return (jax.nn.silu(xb @ w1[e]) * (xb @ w3[e])) @ w2[e]

    ybuf = lax.map(expert_block, (buf.reshape(n_blk, MOE_BLOCK, D), blk_e)).reshape(P, D)
    contrib = ybuf[dest] * w_s[:, None].astype(xt.dtype)
    out = jax.ops.segment_sum(contrib, tok_s, num_segments=T)
    return out.reshape(B, S, D)

def second_inputs(seed: int = 0) -> dict:
    key = jax.random.key(seed)
    ks = jax.random.split(key, 24)

    def nrm(k, shape, scale):
        return jax.random.normal(k, shape, jnp.float32) * scale

    def gain(k, shape):
        return 1.0 + 0.05 * jax.random.normal(k, shape, jnp.float32)

    L = DEPTH_2
    return {
        "x": nrm(ks[0], (BATCH, SEQ, D_MODEL), 1.0),
        "p": nrm(ks[1], (DEPTH_2, BATCH, SEQ, PLE_DIM), 1.0),
        "g_mix": gain(ks[2], (L, D_MODEL)),
        "w_in": nrm(ks[3], (L, D_MODEL, IN_COLS), D_MODEL ** -0.5),
        "gm_ln_g": gain(ks[4], (L, GM_WIDTH)),
        "gm_ln_b": nrm(ks[5], (L, GM_WIDTH), 0.02),
        "gm_w_sp": nrm(ks[6], (L, GM_GROUPS, GM_CHUNK, GM_CHUNK), 0.1 * GM_CHUNK ** -0.5),
        "gm_b_sp": gain(ks[7], (L, GM_GROUPS, GM_CHUNK)),
        "w_up_a": nrm(ks[8], (L, GM_WIDTH, D_MODEL), GM_WIDTH ** -0.5),
        "hg_lb_param": gain(ks[9], (L + 1, HG_KW)),
        "hg_norm_g": gain(ks[10], (L, HG_VW)),
        "w_up_b": nrm(ks[11], (L, HG_VW, D_MODEL), HG_VW ** -0.5),
        "w_out": nrm(ks[12], (L, D_MODEL, D_MODEL), D_MODEL ** -0.5),
        "g_ffn": gain(ks[13], (L, D_MODEL)),
        "w_grp": nrm(ks[14], (L, D_MODEL, N_GROUPS), D_MODEL ** -0.5),
        "w_exp": nrm(ks[15], (L, D_MODEL, N_EXPERTS), D_MODEL ** -0.5),
        "w1": nrm(ks[16], (L, N_EXPERTS, D_MODEL, D_EXPERT), D_MODEL ** -0.5),
        "w3": nrm(ks[17], (L, N_EXPERTS, D_MODEL, D_EXPERT), D_MODEL ** -0.5),
        "w2": nrm(ks[18], (L, N_EXPERTS, D_EXPERT, D_MODEL), D_EXPERT ** -0.5),
        "g_ple": gain(ks[19], (L, D_MODEL)),
        "w_pg": nrm(ks[20], (L, D_MODEL, D_MODEL), D_MODEL ** -0.5),
        "w_ple": nrm(ks[21], (L, PLE_DIM, D_MODEL), PLE_DIM ** -0.5),
        "g_final": gain(ks[22], (D_MODEL,)),
    }

def second_block(x, p, g_mix, w_in, gm_ln_g, gm_ln_b, gm_w_sp, gm_b_sp, w_up_a,
              hg_lb_param, hg_norm_g, w_up_b, w_out, g_ffn, w_grp, w_exp,
              w1, w3, w2, g_ple, w_pg, w_ple, g_final):
    lb_all = jnp.cumsum(jax.nn.softmax(hg_lb_param.astype(jnp.float32), axis=0), axis=0)
    split_idx = [int(s) for s in np.cumsum(IN_SPLITS)[:-1]]
    for i in range(DEPTH_2):
        h = rmsnorm_2(x, g_mix[i])
        z = h @ w_in[i]
        u, v, hq, hf, hi, hog, gate_a, gate_b = jnp.split(z, split_idx, axis=-1)
        y_a = gmlp_branch(jax.nn.gelu(u), jax.nn.gelu(v), gm_ln_g[i], gm_ln_b[i], gm_w_sp[i], gm_b_sp[i])
        y_b = hgrn2_branch(hq, hf, hi, hog, lb_all[i], hg_norm_g[i])
        merged = jax.nn.sigmoid(gate_a) * (y_a @ w_up_a[i]) + jax.nn.sigmoid(gate_b) * (y_b @ w_up_b[i])
        x = x + merged @ w_out[i]
        h = rmsnorm_2(x, g_ffn[i])
        x = x + hier_moe(h, w_grp[i], w_exp[i], w1[i], w3[i], w2[i])
        h = rmsnorm_2(x, g_ple[i])
        x = x + jax.nn.sigmoid(h @ w_pg[i]) * (p[i] @ w_ple[i])
    return rmsnorm_2(x, g_final)


def setup_inputs(seed=0):
    out = dict(first_inputs(seed))
    for name, value in second_inputs(seed + 1).items():
        if name != "x":
            out[name + "_2"] = value
    return out


def reference(
    x, c, ada_w, ada_b, norm_g, a_w_in, a_conv_w, a_w_out, m_w_in, m_conv_w, m_conv_b,
    m_dt_bias, m_a_log, m_d, m_norm_g, m_w_out, f_w_in, f_w_out, p_2, g_mix_2, w_in_2,
    gm_ln_g_2, gm_ln_b_2, gm_w_sp_2, gm_b_sp_2, w_up_a_2, hg_lb_param_2, hg_norm_g_2, w_up_b_2,
    w_out_2, g_ffn_2, w_grp_2, w_exp_2, w1_2, w3_2, w2_2, g_ple_2, w_pg_2, w_ple_2, g_final_2,
):
    x = first_block(
        x, c, ada_w, ada_b, norm_g, a_w_in, a_conv_w, a_w_out, m_w_in, m_conv_w, m_conv_b,
        m_dt_bias, m_a_log, m_d, m_norm_g, m_w_out, f_w_in, f_w_out,
    )
    return second_block(
        x, p_2, g_mix_2, w_in_2, gm_ln_g_2, gm_ln_b_2, gm_w_sp_2, gm_b_sp_2, w_up_a_2,
        hg_lb_param_2, hg_norm_g_2, w_up_b_2, w_out_2, g_ffn_2, w_grp_2, w_exp_2, w1_2, w3_2,
        w2_2, g_ple_2, w_pg_2, w_ple_2, g_final_2,
    )


_drawn_inputs = setup_inputs


def setup_inputs(seed=0):
    import zlib

    import numpy as np

    out = dict(_drawn_inputs(seed))
    spreads = {}
    factors = {'m_conv_b': 3.434,
     'm_norm_g': 93.281,
     'gm_ln_g_2': 37.984,
     'gm_ln_b_2': 63.894,
     'hg_lb_param_2': 8.0,
     'hg_norm_g_2': 3.04,
     'g_ple_2': 20.112,
     'gm_b_sp_2': 3.502}
    for name, (base, spread) in spreads.items():
        noise = np.random.default_rng([zlib.crc32(name.encode()), seed]).standard_normal(out[name].shape)
        drawn = base * np.exp(spread * noise) if base else spread * noise
        out[name] = __import__('jax').numpy.asarray(drawn.astype(out[name].dtype))
    for name, factor in factors.items():
        out[name] = (out[name] * factor).astype(out[name].dtype)
    return out
```

```python
from contextlib import ExitStack

import concourse.bass as bass
from concourse import mybir

F32 = mybir.dt.float32
F32R = mybir.dt.float32r
BF16 = mybir.dt.bfloat16
I32 = mybir.dt.int32
ALU = mybir.AluOpType
ACT = mybir.ActivationFunctionType
AX = mybir.AxisListType.X

P = 128
T = 512
TT = T // P
D = 1024
DT = D // P
FF = 2816
FT = FF // P
INNER = 2048
SG = 8
SH = 32
SC = T // P
GW = 512
HC = 64
NE = 32
DE = 512
BK = 64
OVB = 15
NB = NE + OVB
EPS = 1e-6
BIG = 1e30
KB = 1024


class Stream:

    def __init__(self, eng, own):
        self.eng, self.own, self.count, self.last = eng, own, {}, None

    def send(self, ins, sem=None):
        if isinstance(sem, tuple):
            ins.then_inc(sem[0], 1)
            self.last = sem
            return
        sem = self.own if sem is None else sem
        ins.then_inc(sem, 1)
        self.count[id(sem)] = self.count.get(id(sem), 0) + 1
        self.last = (sem, self.count[id(sem)])

    def settle(self):
        if self.last:
            self.eng.wait_ge(*self.last)

    def link(self, ins, sem=None):
        self.send(ins, sem)
        self.settle()


def bc(ap, shape):
    return ap.broadcast_to(shape)



def plan():
    groups, ring = [], []

    def grp(kind, j, w, c, nk, k0=0, c2=None, **kw):
        ring.append(("grp", len(groups)))
        groups.append(dict(kind=kind, j=j, w=w, c=c, nk=nk, k0=k0, c2=c2, **kw))

    ada = iter(range(48))

    def ada_next(n=1):
        for _ in range(n):
            u = next(ada, None)
            if u is not None:
                ring.append(("ada", u))

    ada_next(8)
    for j in range(4):
        grp("conv_c", j, "a_w_in", D + 256 * j, 8)
        ada_next()
        grp("conv_v", j, "a_w_in", 2 * D + 256 * j, 8)
        ada_next()
        grp("conv_b", j, "a_w_in", 256 * j, 8)
        ada_next()
    for j in range(4):
        grp("y_only", j, "a_w_out", 256 * j, 8, src="mid")
        ada_next()

    def ffn(i):
        for half, (p0, p1) in enumerate(((0, 6), (6, 11))):
            for j in range(p0, p1):
                grp("ffn_g", j - p0, f"f_w_in{i}", 256 * j, 8)
                ada_next()
                grp("ffn_u", j - p0, f"f_w_in{i}", FF + 256 * j, 8)
                ada_next()
            for j in range(4):
                grp(("y_first", "y_last")[half], j, f"f_w_out{i}", 256 * j, 2 * (p1 - p0), 2 * p0, src="mid")
                ada_next()

    ffn(0)
    assert next(ada, None) is None
    for g in range(SG):
        grp("ssd_x", g, "m_w_in", INNER + 256 * g, 8)
        grp("ssd_bc", g, "m_w_in", 2 * INNER + P * g, 8, c2=2 * INNER + D + P * g)
        if g == 5:
            for j in range(4):
                grp("y_first", j, "m_w_out", 256 * j, 8, 0, src="mid")
        grp("ssd_z", g, "m_w_in", 256 * g, 8)
    for j in range(4):
        grp("y_last", j, "m_w_out", 256 * j, 8, 8, src="mid")
    ffn(1)
    for j in range(2):
        grp("gm_v", j, "w_in_2", GW + 256 * j, 8, tok=True)
    for j in range(2):
        grp("gm_u", j, "w_in_2", 256 * j, 8)
    for j in range(2):
        grp("hg_i", j, "w_in_2", 4 * GW + 256 * j, 8, tok=True)
    for j in range(2):
        grp("hg_f", j, "w_in_2", 3 * GW + 256 * j, 8)
        grp("hg_q", j, "w_in_2", 2 * GW + 256 * j, 8)
        if j == 0:
            for jj in range(2):
                grp("hg_og", jj, "w_in_2", 5 * GW + 256 * jj, 8)
    for j in range(4):
        grp("gate_a", j, "w_in_2", 6 * GW + 256 * j, 8)
        grp("up_a", j, "w_up_a_2", 256 * j, 4, src="ya")
        grp("gate_b", j, "w_in_2", 6 * GW + D + 256 * j, 8)
        grp("up_b", j, "w_up_b_2", 256 * j, 4, src="yb")
    for j in range(4):
        grp("w_out", j, "w_out_2", 256 * j, 8, src="merged")
    for j in range(4):
        grp("pg", j, "w_pg_2", 256 * j, 8)
        grp("ple", j, "w_ple_2", 256 * j, 2, src="pt")
    return groups, ring


def number(groups, ring):
    q = 0
    for g, G in enumerate(groups):
        G["subs"] = []
        for s in range(0, G["nk"], 4):
            G["subs"].append((q, s, min(s + 4, G["nk"])))
            q += 1
        G["end"] = q
    units, u = [], 0
    for what, n in ring:
        if what == "ada":
            units.append(("ada", n, 0, 8))
        else:
            for s in range(0, groups[n]["nk"], 8):
                units.append(("grp", n, s, min(s + 8, groups[n]["nk"])))
    return units


C_MCONV, C_ADAB, C_MCONVB = 0, 128, 224
C_NG, C_ACONV, C_MNG, C_GMIX, C_GFFN, C_COND = 256, 320, 344, 360, 368, 376
C_LB, C_HGN, C_GPLE, C_GFIN, C_END = 384, 392, 396, 404, 412


def build(nc, I, out, last_group=None, probe=None):
    groups, ring = plan()
    if last_group is not None:
        n = [g for g, G in enumerate(groups) if (G["kind"], G["j"]) == last_group]
        n = n[last_group == ("y_last", 3) and probe or 0] + 1
        ring = ring[:ring.index(("grp", n - 1)) + 1]
        groups = groups[:n]
    units = number(groups, ring)
    NG = len(groups)
    first = {}
    for g, G in enumerate(groups):
        first.setdefault(G["kind"], g)

    W = {"a_w_in": I["a_w_in"][0], "a_w_out": I["a_w_out"][0], "m_w_in": I["m_w_in"][0], "m_w_out": I["m_w_out"][0],
         "f_w_in0": I["f_w_in"][0], "f_w_in1": I["f_w_in"][1], "f_w_out0": I["f_w_out"][0], "f_w_out1": I["f_w_out"][1],
         "w_in_2": I["w_in_2"][0], "w_up_a_2": I["w_up_a_2"][0], "w_up_b_2": I["w_up_b_2"][0],
         "w_out_2": I["w_out_2"][0], "w_pg_2": I["w_pg_2"][0], "w_ple_2": I["w_ple_2"][0]}

    with ExitStack() as ctx:
        base = (nc.sbuf_base + 31) // 32 * 32
        ctx.enter_context(nc.sbuf_tensor("arena", [P, (nc.sbuf_usable_end - base) // 4 - 16], F32))

        def at(name, kb, shape, dt=F32):
            return nc.alloc_sbuf_tensor_at(name, shape, dt, offset=base + int(kb * KB))

        x = at("x", 0, [P, DT, T])
        h_hi = at("h_hi", 16, [P, DT, T], F32R)
        h_lo = at("h_lo", 32, [P, DT, T], F32R)
        y = at("y", 48, [P, DT, T])
        mid_hi = at("mid_hi", 64, [P, 12, T], F32R)
        mid_lo = at("mid_lo", 88, [P, 12, T], F32R)
        raw = at("raw", 112, [P, 3, 8, 256])
        w_hi = at("w_hi", 136, [P, 4, 4, 256], F32R)
        w_lo = at("w_lo", 152, [P, 4, 4, 256], F32R)
        xtok = at("xtok", 64, [P, TT, D])
        zrow = at("zrow", 108, [P, D])
        cgate = at("cgate", 48, [P, 2, T])
        cv = at("cv", 52, [P, 2, T + 2])
        cu = at("cu", 57, [P, 2, T])
        rstd = at("rstd", 176, [P, T])
        ssq = at("ssq", 178, [P, T])
        sqt = at("sqt", 180, [P, 2, T])
        sg = at("sg", 184, [P, 2, T])
        tmp = at("tmp", 188, [P, 2, T])
        acc = at("acc", 192, [P, 2, 256])
        xs = [at(f"xs{b}", kb, [P, 2, T]) for b, kb in ((0, 80), (1, 168))]
        bct = [at(f"bct{b}", kb, [P, 2, T]) for b, kb in ((0, 84), (1, 172))]
        pre = at("pre", 104, [P, 2, T + 3])
        btok = at("btok", 109, [P, SC, P])
        dt_t = at("dt_t", 111, [P, SC, SH])
        dA = at("dA", 111.5, [P, SC, SH])
        xdt = at("xdt", 178, [P, SC, 256])
        yy = at("yy", 178, [P, 2, T])
        xdte = at("xdte", 182, [P, 3, 256])
        dec = at("dec", 185, [P, 2, 4, P])
        S = at("S", 189, [P, 3, 256])
        sz = at("sz", 192, [P, 2, T])
        cbt = at("cbt", 196, [P, SC, P])
        ncs = at("ncs", 198, [P, SC, SH])
        dte = at("dte", 198.5, [P, SC, SH])
        ctot = at("ctot", 199, [P, SC, SH])
        sp = at("sp", 178, [P, 6, SC * SH])
        ya_hi = at("ya_hi", 64, [P, 4, T], F32R)
        ya_lo = at("ya_lo", 72, [P, 4, T], F32R)
        yb_hi = at("yb_hi", 80, [P, 4, T], F32R)
        yb_lo = at("yb_lo", 88, [P, 4, T], F32R)
        m2_hi = at("m2_hi", 48, [P, DT, T], F32R)
        m2_lo = at("m2_lo", 96, [P, DT, T], F32R)
        lng = at("lng", 80, [P, GW])
        lnb = at("lnb", 82, [P, GW])
        bsp = at("bsp", 84, [P, 4, P])
        wsp = at("wsp", 86, [P, 8, P])
        wspT = at("wspT", 90, [P, 8, P])
        vn = at("vn", 48, [P, TT, GW])
        uact = at("uact", 56, [P, 4, T])
        sog = at("sog", 48, [P, 4, T])
        vtok = at("vtok", 96, [P, TT, GW])
        HS = at("HS", 104, [P, 7, P])
        att = at("att", 108, [P, TT, P])
        ketok = at("ketok", 110, [P, TT, P])
        o_n = at("o_n", 88, [P, 4, T])
        qd = at("qd", 178, [P, 2, T])
        bcum = at("bcum", 182, [P, 2, T])
        ke = at("ke", 186, [P, 2, T])
        fk = at("fk", 190, [P, 2, T])
        kx = at("kx", 56, [P, 2, T])
        sga = at("sga", 60, [P, 2, T])
        sgb = at("sgb", 178, [P, 2, T])
        am_hi = at("am_hi", 194, [P, P])
        am_lo = at("am_lo", 194.5, [P, P])
        reset = at("reset", 195, [P, T])
        hsq = at("hsq", 197, [P, T])
        bns = at("bns", 199, [P, TT, 6])
        bna = at("bna", 199.25, [P, TT, 2])
        lbt = at("lbt", 199.5, [P, 4, 4])
        dlast = at("dlast", 199.75, [P, 2, 8])
        htok = at("htok", 16, [P, 2, D])
        xg = at("xg", 24, [BK, 2, D])
        xgT_hi = at("xgT_hi", 32, [P, 2, DT, BK], F32R)
        xgT_lo = at("xgT_lo", 36, [P, 2, DT, BK], F32R)
        eact = at("eact", 40, [BK, 2, DE])
        a_hi = at("a_hi", 44, [P, 2, 4, BK], F32R)
        a_lo = at("a_lo", 46, [P, 2, 4, BK], F32R)
        esg = at("esg", 48, [BK, 2, DE])
        ytok = at("ytok", 16, [BK, 2, D])
        ew_hi = at("ew_hi", 64, [P, 4, 4, DE], F32R)
        ew_lo = at("ew_lo", 96, [P, 4, 4, DE], F32R)
        eraw = at("eraw", 128, [P, 6, 4, DE])
        wr = at("wr", 44, [P, DT, 36])
        yg = at("yg", 64, [P, 2, 2, D])
        rt = at("rt", 178, [P, 5120])
        ptok = at("ptok", 80, [P, TT, 256])
        pT = at("pT", 84, [P, 2, T])
        pt_hi = at("pt_hi", 88, [P, 2, T], F32R)
        pt_lo = at("pt_lo", 92, [P, 2, T], F32R)
        otok = at("otok", 64, [P, 4, D])
        off = [201.0]

        def const(name, shape, dt=F32):
            n = 2 if dt == BF16 else 4
            for k in shape[1:]:
                n *= k
            t = at(name, off[0], shape, dt)
            off[0] += (n + 31) // 32 * 32 / KB
            return t

        ident = const("ident", [P, P])
        ones = const("ones", [P, P])
        tri = const("tri", [P, P])
        stri = const("stri", [P, P])
        identb = const("identb", [P, P], BF16)
        negb = const("negb", [P, P], BF16)
        cols = const("cols", [P, C_END])
        mod = const("mod", [P, 96])
        sco = const("sco", [P, 4, DT])
        gco = const("gco", [P, 4, DT])
        wdt = const("wdt", [P, DT, SH])
        dtb = const("dtb", [P, SH])
        ahead = const("ahead", [P, SH])
        dsk = const("dsk", [P, 16])
        epsc = const("epsc", [P, 1])
        zero = const("zero", [P, 1])
        sil = const("sil", [P, DT])
        spare = const("spare", [P, 1])
        assert base + off[0] * KB <= nc.sbuf_usable_end, off
        stage = at("stage", 178, [P, 4, P])

        pj = ctx.enter_context(nc.psum_tensor("pj", [P, 4, T], F32))
        M = ctx.enter_context(nc.psum_tensor("M", [P, 4, T], F32))
        Mf = M[:, :, :].rearrange("p a b -> p (a b)")

        at_rt = [0]

        def table(shape, dt=F32):
            n = 1
            for k in shape[1:]:
                n *= k
            v = rt[:, at_rt[0]:at_rt[0] + n]
            at_rt[0] += (n + 7) // 8 * 8
            v = v.bitcast(dt) if dt != F32 else v
            names = "abc"[:len(shape) - 1]
            if len(shape) > 2:
                v = v.rearrange("p (" + " ".join(names) + ") -> p " + " ".join(names),
                                **dict(zip(names, shape[1:])))
            return v

        L = table([P, TT, 36])
        io32 = table([P, NE])
        iot = table([P, NE], I32)
        tokid = table([P, TT], I32)
        gmx, gse, gpg, gix = (table([P, TT]) for _ in range(4))
        t4 = table([P, TT, 4])
        ghot = table([P, TT, 4])
        sel, sel2, t8 = (table([P, TT, 8]) for _ in range(3))
        mx = table([P, 2, TT])
        eix = table([P, 2, TT])
        wex = table([P, TT])
        gate = table([P, 2, TT])
        Ak = [table([P, TT, NE]) for _ in range(2)]
        Aall = table([P, TT, NE])
        rank = table([P, TT, NE])
        t32 = table([P, TT, NE])
        cnt, nbk, incl, obk, t1 = (table([P, NE]) for _ in range(5))
        rk, ok, qk, wk, bk, sk = (table([P, 2, TT]) for _ in range(6))
        ovc = table([P, OVB, NE])
        ovf = table([P, 16])
        ovt = table([P, 16], I32)
        slot_t = table([P, 2, TT], I32)
        slot_y = table([P, 2, TT], I32)
        idx = table([P, NB], I32)
        ic = table([P, 2], I32)
        zt = table([P, 32], I32)
        hdram = nc.dram_tensor("h_rows", (T, D), F32).ap()
        ydram = nc.dram_tensor("y_rows", (NB * BK, D), F32).ap()
        idram = nc.dram_tensor("slot_token", (BK * NB, 1), I32).ap()

        sems = {}

        def s(name):
            if name not in sems:
                sems[name] = ctx.enter_context(nc.semaphore(name))
            return sems[name]

        HSTEP = {0: 0, 1: 1, 2: 2, 3: 3, 4: 4, 6: 5}
        step_after, r = {}, 0
        for g, G in enumerate(groups):
            if (G["kind"] in ("y_only", "y_last", "w_out") and G["j"] == 3):
                r += 1
                step_after[g] = r
        mid_pairs = 0
        for g, G in enumerate(groups):
            k, src = G["kind"], G.get("src", "h")
            if k == "conv_c" and G["j"] == 0:
                G["wait"] = ("h_ready", 0)
            if k in ("y_only", "y_first", "y_last", "w_out"):
                pass
            if g and (g - 1) in step_after and k != "pg":
                G["wait"] = ("h_ready", 8 * HSTEP[step_after[g - 1]])
            if k == "pg" and G["j"] == 0:
                G["wait"] = ("h_ready", 8 * HSTEP[6])
            if k in ("conv_b", "ffn_u", "ssd_z", "up_b"):
                G["pair"] = mid_pairs
                mid_pairs += 1
        done_pairs = 0
        for g, G in enumerate(groups):
            if G["kind"] in ("y_only", "y_first", "y_last", "w_out") and G["j"] == 0:
                G["wait"] = ("mid_ready", done_pairs)
                done_pairs += (G["nk"] + 1) // 2
        for g, G in enumerate(groups):
            if G["kind"] == "up_a" and G["j"] == 0:
                G["wait"] = ("ya_ready", 0)
            if G["kind"] == "up_b" and G["j"] == 0:
                G["wait"] = ("yb_ready", 0)
            if G["kind"] == "ple" and G["j"] == 0:
                G["wait"] = ("pt_ready", 0)

        ada_at, prev = {}, []
        g_seen = -1
        for what, n in ring:
            if what == "ada":
                ada_at.setdefault(g_seen + 1, []).append(n)
            else:
                g_seen = n
        chunk_of = lambda u: 2 * (u // 12) + (u % 12 >= 8)
        chunk_after = {}
        for g, us in ada_at.items():
            for u in us:
                if u % 12 in (7, 11):
                    chunk_after.setdefault(g, []).append(chunk_of(u))
        srcs = {"merged": (m2_hi, m2_lo), "h": (h_hi, h_lo), "mid": (mid_hi, mid_lo), "ya": (ya_hi, ya_lo), "yb": (yb_hi, yb_lo),
                "pt": (pt_hi, pt_lo)}

        raw_at, raw_n, split_at = [], [0, 0, 0], []
        nsub = 0
        for n, (what, g, s0, s1) in enumerate(units):
            raw_n[n % 3] += 32 if what == "grp" and groups[g]["c2"] is not None else 16
            raw_at.append(raw_n[n % 3])
            nsub += (s1 - s0 + 3) // 4 if what == "grp" else 0
            split_at.append(nsub)
        n_pre = NG if "pg" not in first else first["pg"]
        moe = "pg" in first

        def read_out(g):
            return s(f"pj_free{g % 2}"), g // 2 + 1

        def pj2(g):
            return pj[:, 2 * (g % 2):2 * (g % 2) + 2, :]

        def pjt(g):
            return pj2(g).rearrange("p a (b n) -> p (a b) n", n=256)

        def unit_no(e, v):
            return 6 * e - 2 + v

        def raw_slot(e, v):
            return (v + 4) % 6 if e else v

        def split_slot(par, v):
            return v % 4 if par is None or par else (2 + v) % 4

        def arrivals(e, v):
            return 16 * (e + (v >= 2))

        block = ctx.enter_context(nc.Block())

        @block.sync
        def _(sp):
            st = stage
            rows = [(0, 0, I["m_conv_w"][0].rearrange("k (j p) -> (k j) p", p=P)),
                    (1, 0, I["ada_b"].rearrange("(j p) -> j p", p=P)),
                    (1, 96, I["m_conv_b"].rearrange("a (j p) -> (a j) p", p=P)),
                    (2, 0, I["norm_g"].rearrange("a b (j p) -> (a b j) p", p=P)),
                    (2, 64, I["a_conv_w"][0].rearrange("k (j p) -> (k j) p", p=P)),
                    (2, 88, I["m_norm_g"].rearrange("a (j p) -> (a j) p", p=P)),
                    (2, 104, I["g_mix_2"].rearrange("a (j p) -> (a j) p", p=P)),
                    (2, 112, I["g_ffn_2"].rearrange("a (j p) -> (a j) p", p=P)),
                    (2, 120, I["c"].rearrange("a (j p) -> (a j) p", p=P)),
                    (3, 0, I["hg_lb_param_2"].rearrange("a (j p) -> (a j) p", p=P)),
                    (3, 8, I["hg_norm_g_2"].rearrange("a (j p) -> (a j) p", p=P)),
                    (3, 12, I["g_ple_2"].rearrange("a (j p) -> (a j) p", p=P)),
                    (3, 20, I["g_final_2"].rearrange("(j p) -> j p", p=P))]
            for t, r0, src in rows:
                sp.dma_start(st[r0:r0 + src.shape[0], t, :], src).then_inc(s("params_in"), 16)
            sp.dma_start(xtok[:, :, :], I["x"][0].rearrange("(t p) d -> p t d", p=P)).then_inc(s("x_in"), 16)

            def load_unit(n):
                what, g, s0, s1 = units[n]
                if n >= 3:
                    w3, g3, _, _ = units[n - 3]
                    if w3 == "ada":
                        sp.wait_ge(s("ada_acc"), g3 + 1)
                    else:
                        sp.wait_ge(s("lo_ready"), split_at[n - 3])
                if what == "ada":
                    sp.dma_start(raw[:, n % 3, :, :], I["ada_w"][:, 256 * g:256 * g + 256].rearrange(
                        "(k p) n -> p k n", p=P)).then_inc(s(f"raw_in{n % 3}"), 16)
                    return
                G = groups[g]
                w = W[G["w"]][(G["k0"] + s0) * P:(G["k0"] + s1) * P, :].rearrange("(k p) n -> p k n", p=P)
                if G["c2"] is None:
                    sp.dma_start(raw[:, n % 3, 0:s1 - s0, :], w[:, :, G["c"]:G["c"] + 256]).then_inc(
                        s(f"raw_in{n % 3}"), 16)
                else:
                    for m, c in enumerate((G["c"], G["c2"])):
                        sp.dma_start(raw[:, n % 3, 0:s1 - s0, P * m:P * m + P], w[:, :, c:c + P]).then_inc(
                            s(f"raw_in{n % 3}"), 16)

            n_moe = next((n for n, (w_, g_, _, _) in enumerate(units) if w_ == "grp" and g_ == first.get("pg")),
                         len(units))
            for n in range(n_moe):
                load_unit(n)
                if n == 10:
                    sp.dma_start(wdt[:, :, :], W["m_w_in"][:, 2 * INNER + 2 * D:].rearrange(
                        "(k p) n -> p k n", p=P)).then_inc(s("ssd_in"), 16)
                    sp.dma_start(dtb[:, :], I["m_dt_bias"][0].partition_broadcast(P)).then_inc(s("ssd_in"), 16)
                    sp.dma_start(ahead[:, :], I["m_a_log"][0].partition_broadcast(P)).then_inc(s("ssd_in"), 16)
                    for hf in range(2):
                        sp.dma_start(dsk[64 * hf:64 * hf + 64, :], I["m_d"][0].rearrange(
                            "(i h) -> h i", h=2)[hf].partition_broadcast(64),
                                     allow_slow_non_contiguous=True).then_inc(s("ssd_in"), 16)
            if moe:
                sp.wait_ge(s("subs_done"), groups[first["pg"] - 1]["end"])
                sp.dma_start(wr[:, :, 0:4], I["w_grp_2"][0].rearrange("(k p) n -> p k n", p=P)).then_inc(s("wr_in"), 16)
                sp.dma_start(wr[:, :, 4:36], I["w_exp_2"][0].rearrange("(k p) n -> p k n", p=P)).then_inc(s("wr_in"), 16)

                def load(e, v, slot):
                    w = (I["w1_2"], I["w3_2"], I["w2_2"])[v // 2][0][bass.ds(e, 1)].rearrange("a k n -> (a k) n")
                    w = w[512 * (v % 2):512 * (v % 2) + 512, :] if v < 4 else w[:, 512 * (v % 2):512 * (v % 2) + 512]
                    sp.dma_start(eraw[:, slot, :, :], w.rearrange("(k p) n -> p k n", p=P)).then_inc(s(f"e_in{slot}"), 16)

                def load_round(e, first_wait):
                    for v in range(6):
                        if v >= first_wait:
                            sp.wait_ge(s("elo_ready"), unit_no(e, v) - 5)
                        load(e if v < 4 else e - 1, v, raw_slot(1, v))

                for v in range(4):
                    load(0, v, v)
                load_round(1, 2)
                with sp.Fori(1, NE // 2) as it:
                    for b in range(2):
                        load_round(2 * it + b, 0)
                for v in range(2):
                    sp.wait_ge(s("elo_ready"), unit_no(NE, v) - 5)
                    load(NE - 1, 4 + v, raw_slot(1, v))
                sp.wait_ge(s("table_ready"), 1)
                nov = sp.value_load(ovt[0:1, OVB:OVB + 1], min_val=0, max_val=OVB)
                with sp.Fori(0, OVB) as j:
                    with sp.If(j < nov):
                        sp.wait_ge(s("elo_ready"), 6 * NE + 6 * j)
                        e = sp.value_load(ovt[0:1, bass.ds(j, 1)], min_val=0, max_val=NE - 1)
                        for v in range(6):
                            load(e, v, v)
                sp.wait_ge(s("experts_done"), 1)
                sp.dma_start(ptok[:, :, :], I["p_2"][0, 0].rearrange("(t p) n -> p t n", p=P)).then_inc(s("p_in"), 16)
                for n in range(n_moe, len(units)):
                    load_unit(n)
            if moe:
                for t in range(TT):
                    sp.wait_ge(s("otok_odd" if t % 2 else "otok_even"), t // 2 + 1)
                    sp.dma_start(out[0, P * t:P * t + P, :], otok[:, t, :]).then_inc(s("out_done"), 16)
                sp.wait_ge(s("out_done"), 16 * TT)
            else:
                sp.wait_ge(s("test_done"), 2)
                sp.dma_start(out, x[:, :, :]).then_inc(s("out_done"), 16)
                sp.wait_ge(s("out_done"), 16)

        @block.gpsimd
        def _(pool):
            V = Stream(pool, s("pool"))
            g = nc.gpsimd
            V.send(g.memset(ident[:, :], 0.0))
            V.send(g.memset(identb[:, :], 0.0))
            V.send(g.memset(ones[:, :], 1.0))
            V.send(g.memset(tri[:, :], 1.0))
            V.send(g.memset(stri[:, :], 1.0))
            V.send(g.memset(negb[:, :], 0.0))
            V.send(g.memset(epsc[:, :], EPS))
            V.link(g.memset(zero[:, :], 0.0))
            for m_, cmp, fill, b0 in ((ident, ALU.not_equal, 1.0, 0), (identb, ALU.not_equal, 1.0, 0),
                                      (tri, ALU.is_ge, 0.0, 0), (stri, ALU.is_gt, 0.0, 0), (negb, ALU.is_ge, -BIG, 0)):
                if cmp == ALU.not_equal:
                    V.send(g.affine_select(out=m_[:, :], in_=m_[:, :], compare_op=cmp, fill=fill, base=b0,
                                           pattern=[[-1, P]], channel_multiplier=1))
                else:
                    V.send(g.affine_select(out=m_[:, :], in_=m_[:, :], compare_op=cmp, fill=fill, base=b0,
                                           pattern=[[1, P]], channel_multiplier=-1))
            V.link(g.memset(zero[:, :], 0.0), s("const_ready"))
            if moe:
                V.link(g.memset(zrow[:, :], 0.0))
                for b in range(8):
                    pool.dma_start(ydram[NE * BK + 120 * b:NE * BK + 120 * b + 120, :], zrow[0:120, :]).then_inc(
                        s("y_cleared"), 16)
            step = 0
            for gi, G in enumerate(groups):
                if G["kind"] in ("y_only", "y_last"):
                    j = G["j"]
                    if j == 3:
                        step += 1
                        continue
                    pool.wait_ge(s("ysq_ready"), 4 * step + j + 1)
                    if j == 0:
                        V.link(g.tensor_tensor(ssq[:, :], sqt[:, 0, :], sqt[:, 1, :], ALU.add), s("ssq_ready"))
                    else:
                        V.link(g.tensor_tensor(ssq[:, :], ssq[:, :], sqt[:, 0, :], ALU.add))
                        V.link(g.tensor_tensor(ssq[:, :], ssq[:, :], sqt[:, 1, :], ALU.add), s("ssq_ready"))
                if gi == first.get("gm_v"):
                    pool.wait_ge(s("xsum_ready"), 5)
                    pool.dma_start(lng[:, :], I["gm_ln_g_2"][0].partition_broadcast(P)).then_inc(s("gm_in"), 16)
                    pool.dma_start(lnb[:, :], I["gm_ln_b_2"][0].partition_broadcast(P)).then_inc(s("gm_in"), 16)
                    pool.dma_start(wsp[:, :, :], I["gm_w_sp_2"][0].rearrange("g t s -> t g s")).then_inc(s("gm_in"), 16)
                    for hf in range(2):
                        pool.dma_start(bsp[64 * hf:64 * hf + 64, :, :], I["gm_b_sp_2"][0].rearrange(
                            "(i h) t -> h i t", h=2)[hf].partition_broadcast(64)).then_inc(s("gm_in"), 16)
                    V.send(g.memset(am_hi[:, :], 0.0))
                    V.send(g.memset(reset[:, :], 1.0))
                    V.settle()
                    for c in range(T // HC):
                        V.send(g.memset(reset[:, HC * c:HC * c + 1], 0.0))
                    for b in range(2):
                        V.link(g.memset(am_hi[HC * b:HC * b + HC, HC * b:HC * b + HC], 3.0e38))
                    V.link(g.affine_select(out=am_hi[:, :], in_=am_hi[:, :], compare_op=ALU.is_ge, fill=0.0, base=0,
                                           pattern=[[1, P]], channel_multiplier=-1))
                    V.link(g.tensor_scalar(am_lo[:, :], am_hi[:, :], -1.0, None, ALU.mult), s("bounds_ready"))
            if not moe:
                return
            pool.wait_ge(s("xsum_ready"), 6)
            V.send(g.iota(iot, pattern=[[1, NE]], base=0, channel_multiplier=0))
            V.send(g.iota(tokid, pattern=[[P, TT]], base=0, channel_multiplier=1))
            V.link(g.memset(zt, 0))
            V.link(g.tensor_copy(io32, iot), s("iota_ready"))
            pool.dma_start(idram.rearrange("(a b) o -> a (b o)", b=32), zt[0:BK * NB // 32, :]).then_inc(
                s("table_clear"), 16)
            pool.wait_ge(s("table_clear"), 16)
            pool.wait_ge(s("slots_ready"), 1)
            for k in range(2):
                for t in range(TT):
                    g.indirect_dma_start(out=idram, out_offset=bass.IndirectOffsetOnAxis(ap=slot_t[:, k, t:t + 1], axis=0),
                                         in_=tokid[:, t:t + 1], in_offset=None).then_inc(s("scattered"), 16)
            pool.wait_ge(s("scattered"), 16 * 2 * TT)
            pool.dma_start(idx[0:BK, :], idram.rearrange("(s b) o -> s (b o)", b=NB)).then_inc(s("idx_in"), 16)
            pool.wait_ge(s("idx_in"), 16)
            pool.wait_ge(s("hrow_out0"), 32)
            pool.wait_ge(s("hrow_out1"), 32)

            def gather(e, b, sem):
                V.link(g.tensor_copy(ic[0:BK, b:b + 1], idx[0:BK, bass.ds(e, 1)]))
                g.indirect_dma_start(out=xg[:, b, :], out_offset=None, in_=hdram,
                                     in_offset=bass.IndirectOffsetOnAxis(ap=ic[0:BK, b:b + 1], axis=0)).then_inc(sem, 16)

            for b in range(2):
                gather(b, b, s(f"xg_in{b}"))
            with pool.Fori(1, NE // 2) as it:
                for b in range(2):
                    e = 2 * it + b
                    pool.wait_ge(s("e_turned"), e - 1)
                    g.tensor_copy(ic[0:BK, b:b + 1], idx[0:BK, bass.ds(e, 1)]).then_inc(s("ic_ready"), 1)
                    pool.wait_ge(s("ic_ready"), e - 1)
                    g.tensor_tensor(spare[:, :], zero[:, :], zero[:, :], ALU.add)
                    g.indirect_dma_start(out=xg[:, b, :], out_offset=None, in_=hdram, in_offset=bass.IndirectOffsetOnAxis(
                        ap=ic[0:BK, b:b + 1], axis=0)).then_inc(s(f"xg_in{b}"), 16)
            pool.wait_ge(s("table_ready"), 1)
            nov = pool.value_load(ovt[0:1, OVB:OVB + 1], min_val=0, max_val=OVB)
            with pool.Fori(0, OVB) as j:
                with pool.If(j < nov):
                    pool.wait_ge(s("e_turned"), NE + j)
                    g.tensor_copy(ic[0:BK, 0:1], idx[0:BK, bass.ds(NE + j, 1)]).then_inc(s("ic_ready"), 1)
                    pool.wait_ge(s("ic_ready"), NE - 1 + j)
                    g.tensor_tensor(spare[:, :], zero[:, :], zero[:, :], ALU.add)
                    g.indirect_dma_start(out=xg[:, 0, :], out_offset=None, in_=hdram, in_offset=bass.IndirectOffsetOnAxis(
                        ap=ic[0:BK, 0:1], axis=0)).then_inc(s("xg_in0"), 16)
            pool.wait_ge(s("rows_done"), 1)
            for t in range(TT):
                if t >= 2:
                    pool.wait_ge(s("combined"), t - 1)
                for k in range(2):
                    g.indirect_dma_start(out=yg[:, t % 2, k, :], out_offset=None, in_=ydram,
                                         in_offset=bass.IndirectOffsetOnAxis(ap=slot_y[:, k, t:t + 1], axis=0)
                                         ).then_inc(s(f"yg_in{t % 2}"), 16)

        @block.scalar
        def _(act):
            V = Stream(act, s("act"))
            A = nc.scalar.activation
            at_unit = [0]
            at_sub = [0]

            def advance(upto):
                upto = min(upto, len(groups) - 1) if phase[0] else min(upto, n_pre - 1)
                while at_unit[0] < len(units):
                    what, g, s0, s1 = units[at_unit[0]]
                    if what == "grp" and g > upto:
                        return
                    n = at_unit[0]
                    at_unit[0] += 1
                    if what == "ada":
                        continue
                    act.wait_ge(s(f"raw_in{n % 3}"), raw_at[n])
                    for a in range(s0, s1, 4):
                        z = min(a + 4, s1)
                        q = at_sub[0]
                        at_sub[0] += 1
                        if q >= 4:
                            act.wait_ge(s("subs_done"), q - 3)
                        V.send(A(w_hi[:, q % 4, 0:z - a, :], raw[:, n % 3, a - s0:z - s0, :], ACT.Copy), s("hi_ready"))

            def rsqrt(out_, in_, scale, sem):
                V.link(A(out_, in_, ACT.Ln, bias=epsc[:, 0:1], scale=scale))
                V.send(A(out_, out_, ACT.Exp, scale=-0.5), sem)

            phase = [0]
            act.wait_ge(s("const_ready"), 1)
            act.wait_ge(s("cols_ready"), 1)
            V.send(A(sil[:, :], cols[:, C_COND:C_COND + DT], ACT.Silu), s("sil_ready"))

            def step(r):
                if 1 <= r <= 4:
                    act.wait_ge(s("ysum_ready"), r)
                    rsqrt(rstd[:, :], M[:, 3, :], 1.0 / D, s("rstd_y_ready"))
                if r == 5:
                    act.wait_ge(*read_out(n_pre - 1))
                    act.wait_ge(*read_out(n_pre - 2))
                for i in range(DT):
                    if r != 5:
                        act.wait_ge(s("x_new"), 8 * (r - (r > 5)) + (DT if r == 6 else i + 1))
                    V.send(A(y[:, i, :], x[:, i, :], ACT.Square), s("sq_ready"))
                act.wait_ge(s("xsum_ready"), r + 1)
                rsqrt(rstd[:, :], M[:, 3, :], 1.0 / D, s("rstd_x_ready"))
                if r in HSTEP:
                    for i in range(DT):
                        act.wait_ge(s("hf_ready"), 8 * HSTEP[r] + i + 1)
                        V.send(A(h_hi[:, i, :], y[:, i, :], ACT.Copy), s("h_hi_ready"))

            step(0)
            advance(1)
            n_ysq = n_mhi = n_first = 0

            def mid_high(G, g, src, dst):
                nonlocal n_mhi
                act.wait_ge(*read_out(g))
                V.send(A(dst, src, ACT.Copy), s("mid_hi_ready"))

            def ssd_head():
                act.wait_ge(s("ssd_in"), 80)
                V.send(A(ahead[:, :], ahead[:, :], ACT.Exp), s("aexp_ready"))
                act.wait_ge(s("sp_ready"), 1)
                V.send(A(sp[:, 1, :], sp[:, 1, :], ACT.Exp, scale=-1.0), s("spe_ready"))
                act.wait_ge(s("cs_ready"), 1)
                csf = M[:, 1, 0:P]
                V.link(A(ctot[:, :, :], M[:, 1, P:2 * P].rearrange("p (c h) -> p c h", h=SH), ACT.Exp))
                V.send(A(ncs[:, :, :], csf.rearrange("p (c h) -> p c h", h=SH), ACT.Copy, scale=-1.0), s("ncs_ready"))
                act.wait_ge(s("dtex_ready"), 1)
                V.send(A(dte[:, :, :], dte[:, :, :], ACT.Exp), s("dte_ready"))

            def ssd_a(n):
                act.wait_ge(s("ssd_turned"), n + 1)
                V.send(A(btok[:, :, :], M[:, 2, :].rearrange("p (c n) -> p c n", n=P), ACT.Copy), s("bt_ready"))
                V.send(A(cbt[:, :, :], M[:, 3, :].rearrange("p (c n) -> p c n", n=P), ACT.Copy), s("bt_ready"))

            def ssd_exp(n, c):
                act.wait_ge(s("csb_ready"), 4 * n + c + 1)
                for r in range(4):
                    h = 4 * n + r
                    V.send(A(dec[:, c % 2, r, :], M[:, c % 2, P * r:P * r + P], ACT.Exp, bias=ncs[:, c, h:h + 1]),
                           s("dec_ready"))

            def ssd_silu(n, buf, c0, c1, k):
                act.wait_ge(s("conv_ready"), 2 * n + k + 1)
                for i, c in enumerate((c0, c1)):
                    V.send(A(buf[:, i, :], buf[:, i, :], ACT.Silu, bias=cols[:, C_MCONVB + c:C_MCONVB + c + 1]),
                           s("xbc_ready"))

            def ssd_ecs(n):
                act.wait_ge(s("ecs_ready"), n + 1)
                V.send(A(yy[:, :, :], M[:, 0:2, :], ACT.Exp), s("yy_ready"))

            def ssd_norm(n):
                act.wait_ge(s("yg_ready"), n + 1)
                V.send(A(sz[:, :, :], yy[:, :, :], ACT.Square), s("ygsq_ready"))
                act.wait_ge(s("yg_summed"), n + 1)
                rsqrt(rstd[:, :], M[:, 2, :], 1.0 / 256, s("yg_rstd"))

            def ssd_high(n):
                act.wait_ge(s("yn_ready"), n + 1)
                V.send(A(mid_hi[:, 2 * (n % 4):2 * (n % 4) + 2, :], yy[:, :, :], ACT.Copy), s("mid_hi_ready"))

            def hg_chain(jp):
                act.wait_ge(s("hf_f"), jp + 1)
                V.send(A(fk[:, :, :], fk[:, :, :], ACT.Ln), s("lnf_ready"))
                act.wait_ge(s("bcum_ready"), jp + 1)
                V.send(A(fk[:, :, :], bcum[:, :, :], ACT.Exp), s("eb_ready"))
                act.wait_ge(s("qd_ready"), jp + 1)
                V.send(A(fk[:, :, :], bcum[:, :, :], ACT.Exp, scale=-1.0), s("enb_ready"))
                V.send(A(dlast[:, :, :], bcum[:, :, :].rearrange("p a (c t) -> p a c t", t=HC)[:, :, :, HC - 1], ACT.Exp),
                       s("dlast_ready"))
                act.wait_ge(s("kx_ready"), jp + 1)
                V.send(A(kx[:, :, :], kx[:, :, :], ACT.Exp), s("kxe_ready"))

            def hg_k1(n):
                act.wait_ge(s("hg_scores"), n + 1)
                V.send(A(ketok[:, :, :], M[:, 1, :].rearrange("p (b k) -> p b k", k=P), ACT.Copy), s("ketok_ready"))

            def hg_k3(n):
                act.wait_ge(s("hg_out"), n + 1)
                V.send(A(hsq[:, :], M[:, 0, :], ACT.Square), s("osq_ready"))
                act.wait_ge(s("osum_ready"), n + 1)
                rsqrt(rstd[:, :], M[:, 1, :], 1.0 / P, s("orstd_ready"))
                act.wait_ge(s("on_ready"), n + 1)
                V.send(A(yb_hi[:, n, :], o_n[:, n, :], ACT.Copy), s("yb_hi_ready"))

            def expert_high(u, slot, par_slot, arrived, done):
                act.wait_ge(s(f"e_in{slot}"), arrived)
                if done is not None:
                    act.wait_ge(s("e_units"), done)
                A(ew_hi[:, par_slot, :, :], eraw[:, slot, :, :], ACT.Copy).then_inc(s("ehi_ready"), 1)

            def x_high(e, b):
                act.wait_ge(s("e_turned"), e + 1)
                A(xgT_hi[:, b, :, :], M[:, b, :].rearrange("p (k t) -> p k t", t=BK), ACT.Copy).then_inc(s("e_xhi"), 1)

            def expert_silu(e, b, done):
                act.wait_ge(s("e_units"), done)
                A(esg[:, b, :], M[0:BK, 2, :], ACT.Silu).then_inc(s("e_sg"), 1)

            def act_high(e, b):
                act.wait_ge(s("e_aturned"), e + 1)
                A(a_hi[:, b, :, :], pj[:, 0, 0:4 * BK].rearrange("p (k t) -> p k t", t=BK), ACT.Copy).then_inc(s("e_ahi"), 1)

            def expert_rows(e, b, row, done, store_sem, stored):
                act.wait_ge(s("e_units"), done)
                if stored is not None:
                    act.wait_ge(store_sem, stored)
                A(ytok[:, b, :], pj[0:BK, 2:4, :].rearrange("p a b -> p (a b)"), ACT.Copy).then_inc(s("e_ytok"), 1)
                act.wait_ge(s("e_ytok"), e + 1)
                act.dma_start(ydram[row, :], ytok[:, b, :]).then_inc(store_sem, 16)

            def rows_of(e, b, stored):
                row = slice(BK * e, BK * e + BK) if isinstance(e, int) else bass.ds(e * BK, BK)
                expert_rows(e, b, row, unit_no(e + 2, 0), s(f"y_out{b}"), stored)

            def act_round(e, par, first_round):
                for v in range(6):
                    u = unit_no(e, v)
                    expert_high(u, raw_slot(1, v), split_slot(par, v), arrivals(e, v), u - 3)
                    if v == 1:
                        x_high(e, par)
                    if v == 3 and not first_round:
                        rows_of(e - 2, par, None if isinstance(e, int) and e < 4 else (e - par - 2) * 8)
                    if v == 5:
                        expert_silu(e, par, unit_no(e, 2))
                        act_high(e - 1, 1 - par)

            def act_moe():
                for t in range(TT):
                    if t >= 2:
                        act.wait_ge(s(f"hrow_out{t % 2}"), 16)
                    act.wait_ge(s("h_turned"), t + 1)
                    V.link(A(htok[:, t % 2, :], pj[:, 2 * (t % 2):2 * (t % 2) + 2, :].rearrange("p a b -> p (a b)"),
                             ACT.Copy), s("htok_ready"))
                    act.dma_start(hdram[P * t:P * t + P, :], htok[:, t % 2, :]).then_inc(s(f"hrow_out{t % 2}"), 16)
                act.wait_ge(s("r_shift"), 1)
                V.send(A(t4, t4, ACT.Exp), s("r_exp"))
                act.wait_ge(s("r_shift"), 2)
                V.send(A(wex, wex, ACT.Exp), s("r_exp"))
                act.wait_ge(s("hrow_out0"), 32)
                act.wait_ge(s("hrow_out1"), 32)

                for v in range(4):
                    expert_high(v, v, v, 16, None)
                x_high(0, 0)
                expert_silu(0, 0, 2)
                act_round(1, 1, True)
                act_round(2, 0, False)
                act_round(3, 1, False)
                with act.Fori(2, NE // 2) as it:
                    for b in range(2):
                        act_round(2 * it + b, b, False)
                for v in range(2):
                    u = unit_no(NE, v)
                    expert_high(u, raw_slot(1, v), split_slot(0, v), arrivals(NE, v), u - 3)
                rows_of(NE - 2, 0, 16 * (NE // 2 - 1))
                act_high(NE - 1, 1)
                expert_rows(NE - 1, 1, slice(BK * (NE - 1), BK * NE), 6 * NE, s("y_out1"), 16 * (NE // 2 - 1))
                for b in range(2):
                    act.wait_ge(s(f"y_out{b}"), 8 * NE)
                act.wait_ge(s("table_ready"), 1)
                nov = act.value_load(ovt[0:1, OVB:OVB + 1], min_val=0, max_val=OVB)
                with act.Fori(0, OVB) as jj:
                    with act.If(jj < nov):
                        n, u = NE + jj, 6 * NE + 6 * jj
                        x_high(n, 0)
                        for v in range(6):
                            expert_high(u + v, v, v % 4, 16 * (NE + 1) + 16 * jj, u if v < 4 else u + v - 3)
                        expert_silu(n, 0, u + 2)
                        act_high(n, 0)
                        expert_rows(n, 0, bass.ds(n * BK, BK), u + 6, s("y_out0"), 8 * NE + 16 * jj)
                act.wait_ge(s("y_out0"), 8 * NE + 16 * nov)
                V.link(A(esg[:, 0, 0:1], zero[0:BK, 0:1], ACT.Copy), s("rows_done"))
                act.wait_ge(s("pT_ready"), 1)
                V.send(A(pt_hi[:, :, :], pT[:, :, :], ACT.Copy), s("pt_hi_ready"))

            for g, G in enumerate(groups):
                k, j = G["kind"], G["j"]
                done = (s("subs_done"), G["end"])
                banks = pj2(g)
                free = read_out(g)
                if k == "conv_c":
                    if j:
                        act.wait_ge(*read_out(g - 2))
                    act.wait_ge(*done)
                    V.send(A(cgate[:, :, :], banks, ACT.Copy), free)
                elif k == "conv_b":
                    mid_high(G, g, cu[:, :, :], mid_hi[:, 2 * j:2 * j + 2, :])
                elif k in ("y_only", "y_last"):
                    if j:
                        act.wait_ge(s("ssq_ready"), n_ysq // 4 * 3 + j)
                    act.wait_ge(*read_out(g))
                    V.send(A(sqt[:, :, :], y[:, 2 * j:2 * j + 2, :], ACT.Square), s("ysq_ready"))
                    n_ysq += 1
                elif k == "y_first":
                    act.wait_ge(*done)
                    V.send(A(y[:, 2 * j:2 * j + 2, :], banks, ACT.Copy), free)
                elif k == "ffn_g":
                    if j:
                        act.wait_ge(*read_out(g - 1))
                    act.wait_ge(*done)
                    V.send(A(sg[:, :, :], banks, ACT.Silu), free)
                elif k == "ffn_u":
                    mid_high(G, g, tmp[:, :, :], mid_hi[:, 2 * j:2 * j + 2, :])
                elif k == "ssd_x":
                    n = j - 1
                    if j == 0:
                        ssd_head()
                    if n >= 0:
                        ssd_a(n)
                        act.wait_ge(s("conv_ready"), 2 * n + 2)
                    act.wait_ge(*done)
                    V.send(A(pre[:, :, 3:], banks, ACT.Copy), free)
                elif k == "ssd_bc":
                    n = j - 1
                    if n >= 0:
                        ssd_exp(n, 0)
                        ssd_exp(n, 1)
                        ssd_exp(n, 2)
                    ssd_silu(j, xs[j % 2], 2 * j, 2 * j + 1, 0)
                    if n >= 0:
                        ssd_exp(n, 3)
                    act.wait_ge(*done)
                    V.send(A(pre[:, :, 3:], banks, ACT.Copy), free)
                elif k == "ssd_z":
                    n = j - 1
                    ssd_silu(j, bct[j % 2], 16 + j, 24 + j, 1)
                    if n >= 0:
                        ssd_ecs(n)
                        ssd_norm(n)
                    act.wait_ge(*done)
                    V.send(A(sz[:, :, :], banks, ACT.Silu), free)
                    advance(g + 2)
                    if n >= 0:
                        ssd_high(n)
                    if j == SG - 1:
                        n = j
                        ssd_a(n)
                        for c in range(SC):
                            ssd_exp(n, c)
                        ssd_ecs(n)
                        ssd_norm(n)
                        ssd_high(n)
                elif k == "gm_v":
                    act.wait_ge(*done)
                    V.send(A(vn[:, :, 256 * j:256 * j + 256], pjt(g), ACT.Gelu_apprx_tanh), free)
                elif k == "gm_u":
                    act.wait_ge(*done)
                    V.send(A(uact[:, 2 * j:2 * j + 2, :], banks, ACT.Gelu_apprx_tanh), free)
                    if j == 1:
                        act.wait_ge(s("bna_ready"), 1)
                        V.link(A(bna[:, :, 1], bna[:, :, 1], ACT.Ln, bias=epsc[:, 0:1]))
                        V.send(A(bna[:, :, 1], bna[:, :, 1], ACT.Exp, scale=-0.5), s("lnr_ready"))
                        act.wait_ge(s("lbx_ready"), 1)
                        V.send(A(lbt[:, 0:2, :], lbt[:, 0:2, :], ACT.Exp), s("lbe_ready"))
                elif k == "hg_i":
                    act.wait_ge(*done)
                    V.send(A(vtok[:, :, 256 * j:256 * j + 256], pjt(g), ACT.Copy), free)
                    if j == 1:
                        for p in range(2):
                            act.wait_ge(s("gm_y"), p + 1)
                            V.send(A(ya_hi[:, 2 * p:2 * p + 2, :], uact[:, 2 * p:2 * p + 2, :], ACT.Copy),
                                   s("ya_hi_ready"))
                elif k == "hg_f":
                    act.wait_ge(*done)
                    if j == 1:
                        hg_k1(1)
                        hg_k3(1)
                    V.send(A(fk[:, :, :], banks, ACT.Sigmoid), free)
                elif k == "hg_q":
                    act.wait_ge(*done)
                    V.send(A(qd[:, :, :], banks, ACT.Silu), free)
                    hg_chain(j)
                elif k == "hg_og":
                    act.wait_ge(*done)
                    V.send(A(sog[:, 2 * j:2 * j + 2, :], banks, ACT.Sigmoid), free)
                    if j == 0:
                        hg_k1(0)
                    else:
                        hg_k3(0)
                elif k == "gate_a":
                    if j:
                        act.wait_ge(*read_out(g - 1))
                    act.wait_ge(*done)
                    V.send(A(sga[:, :, :], banks, ACT.Sigmoid), free)
                elif k == "up_a":
                    if j == 0:
                        for n in (2, 3):
                            hg_k1(n)
                            hg_k3(n)
                elif k == "gate_b":
                    if j:
                        act.wait_ge(s("mid_ready"), groups[g - 3]["pair"] + 1)
                    act.wait_ge(*done)
                    V.send(A(sgb[:, :, :], banks, ACT.Sigmoid), free)
                elif k == "up_b":
                    mid_high(G, g, sgb[:, :, :], m2_hi[:, 2 * j:2 * j + 2, :])
                elif k == "pg":
                    if j:
                        act.wait_ge(*read_out(g - 1))
                    act.wait_ge(*done)
                    V.send(A(sg[:, :, :], banks, ACT.Sigmoid), free)
                if g in step_after:
                    step(step_after[g])
                    if step_after[g] == 5 and moe:
                        act_moe()
                        phase[0] = 1
                        advance(g + 2)
                        step(6)
                        continue
                advance(g + 2)
            if moe:
                step(7)
                for t in range(1, TT, 2):
                    act.wait_ge(s("o_turned"), t + 1)
                    V.send(A(otok[:, t, :], pj[:, 2:4, :].rearrange("p a b -> p (a b)"), ACT.Copy), s("otok_odd"))
            else:
                V.settle()
                V.send(A(stage[:, 0, 0:1], zero[:, :], ACT.Copy), s("test_done"))

        @block.vector
        def _(dve):
            V = Stream(dve, s("dve"))
            v = nc.vector
            TS, TN, STT = v.tensor_scalar, v.tensor_tensor, v.scalar_tensor_tensor
            at_unit, at_sub, phase = [0], [0], [0]

            def advance(upto):
                upto = min(upto, len(groups) - 1) if phase[0] else min(upto, n_pre - 1)
                while at_unit[0] < len(units):
                    what, g, s0, s1 = units[at_unit[0]]
                    if what == "grp" and g > upto or (what == "ada" and upto < 0 and g >= 8):
                        return
                    n = at_unit[0]
                    at_unit[0] += 1
                    if what == "ada":
                        u = g
                        dve.wait_ge(s(f"raw_in{n % 3}"), raw_at[n])
                        if u == 0:
                            dve.wait_ge(s("sil_ready"), 1)
                        if u >= 2:
                            dve.wait_ge(s("ada_summed"), u - 1)
                        a = acc[:, u % 2, :]
                        V.link(TS(a, raw[:, n % 3, 0, :], sil[:, 0:1], None, ALU.mult))
                        for k in range(1, DT):
                            V.link(STT(a, raw[:, n % 3, k, :], sil[:, k:k + 1], a, ALU.mult, ALU.add),
                                   s("ada_acc") if k == DT - 1 else None)
                        continue
                    for b in range(s0, s1, 4):
                        z = min(b + 4, s1)
                        q = at_sub[0]
                        at_sub[0] += 1
                        dve.wait_ge(s("hi_ready"), q + 1)
                        V.send(TN(w_lo[:, q % 4, 0:z - b, :], raw[:, n % 3, b - s0:z - s0, :],
                                  w_hi[:, q % 4, 0:z - b, :].bitcast(F32), ALU.subtract), s("lo_ready"))

            def coefficients(c):
                r, gate_part = c // 2, c % 2
                c0, n = 24 * r + 16 * gate_part, 8 if gate_part else 16
                dve.wait_ge(s("ada_summed"), (12 * r + 12) if gate_part else (12 * r + 8))
                V.link(TN(mod[:, c0:c0 + n], M[:, c % 3, c0:c0 + n], cols[:, C_ADAB + c0:C_ADAB + c0 + n], ALU.add),
                       s("coef_read"))
                ng = C_NG + 8 * (4 * (r // 2) + 2 * (r % 2))
                if gate_part:
                    V.link(TN(gco[:, r, :], mod[:, c0:c0 + 8], cols[:, ng + 8:ng + 16], ALU.mult))
                else:
                    V.link(STT(sco[:, r, :], mod[:, c0 + 8:c0 + 16], 1.0, cols[:, ng:ng + 8], ALU.add, ALU.mult))

            def step(r):
                if 1 <= r <= 4:
                    dve.wait_ge(s("rstd_y_ready"), r)
                    V.settle()
                    for p in range(4):
                        yp = y[:, 2 * p:2 * p + 2, :]
                        V.link(TN(yp, yp, rstd[:, :].unsqueeze(1).broadcast_to((P, 2, T)), ALU.mult))
                        for i in (2 * p, 2 * p + 1):
                            V.send(STT(x[:, i, :], y[:, i, :], gco[:, r - 1, i:i + 1], x[:, i, :], ALU.mult, ALU.add),
                                   s("x_new"))
                dve.wait_ge(s("rstd_x_ready"), r + 1)
                V.settle()
                scale = {0: sco[:, 0, :], 1: sco[:, 1, :], 2: sco[:, 2, :], 3: sco[:, 3, :],
                         4: cols[:, C_GMIX:C_GMIX + 8], 5: cols[:, C_GFFN:C_GFFN + 8], 6: cols[:, C_GPLE:C_GPLE + 8],
                         7: cols[:, C_GFIN:C_GFIN + 8]}[r]
                sem = s("hf_ready") if r in HSTEP else s("mh_ready") if r == 5 else s("fin_ready")

                def low(p):
                    for i in (2 * p, 2 * p + 1):
                        dve.wait_ge(s("h_hi_ready"), 8 * HSTEP[r] + i + 1)
                        V.send(TN(h_lo[:, i, :], y[:, i, :], h_hi[:, i, :].bitcast(F32), ALU.subtract), s("h_ready"))

                for p in range(4):
                    V.link(TN(y[:, 2 * p:2 * p + 2, :], x[:, 2 * p:2 * p + 2, :],
                              rstd[:, :].unsqueeze(1).broadcast_to((P, 2, T)), ALU.mult))
                    for i in (2 * p, 2 * p + 1):
                        shift = mod[:, 24 * r + i:24 * r + i + 1] if r < 4 else None
                        V.send(TS(y[:, i, :], y[:, i, :], scale[:, i:i + 1], shift, ALU.mult,
                                  *((ALU.add,) if r < 4 else ())), sem)
                    if p and r in HSTEP:
                        low(p - 1)
                if r in HSTEP:
                    low(3)

            n_mid = [0]

            def mid_low(src, dst, hi):
                n_mid[0] += 1
                dve.wait_ge(s("mid_hi_ready"), n_mid[0])
                V.send(TN(dst, src, hi.bitcast(F32), ALU.subtract), s("mid_ready"))

            dve.wait_ge(s("params_turned"), 1)
            V.link(v.tensor_copy(cols[:, :], M[:, 0, 0:C_END]), s("cols_ready"))
            for i in range(DT):
                dve.wait_ge(s("x_turned"), i + 1)
                V.send(v.tensor_copy(x[:, i, :], pj[:, i % 4, :]), s("x_new"))
            advance(-1)
            coefficients(0)
            step(0)
            V.settle()
            V.send(v.memset(cv[:, :, 0:2], 0.0))
            advance(1)

            def conv4(n, k, dst):
                c0 = (2 * n, 2 * n + 1) if k == 0 else (16 + n, 24 + n)
                w = lambda tap, i: cols[:, C_MCONV + 32 * tap + c0[i]:C_MCONV + 32 * tap + c0[i] + 1]
                V.settle()
                for i in range(2):
                    V.send(TS(dst[:, i, :], pre[:, i, 0:T], w(0, i), None, ALU.mult))
                V.settle()
                for tap in (1, 2, 3):
                    for i in range(2):
                        V.send(STT(dst[:, i, :], pre[:, i, tap:tap + T], w(tap, i), dst[:, i, :], ALU.mult, ALU.add),
                               s("conv_ready") if (tap, i) == (3, 1) else None)
                    V.settle()

            def ssd_head():
                dve.wait_ge(s("dt_raw"), 1)
                dve.wait_ge(s("ssd_in"), 80)
                dve.wait_ge(s("aexp_ready"), 1)
                V.settle()
                z, e, w, q, r_, t_ = (sp[:, i, :] for i in range(6))
                v3 = lambda a: a.rearrange("p (c h) -> p c h", h=SH)
                V.link(TN(v3(z), M[:, 0, 0:P].rearrange("p (c h) -> p c h", h=SH),
                          dtb[:, :].unsqueeze(1).broadcast_to((P, SC, SH)), ALU.add))
                V.link(STT(e, z, -1.0, z, ALU.mult, ALU.max), s("sp_ready"))
                dve.wait_ge(s("spe_ready"), 1)
                V.link(TS(w, e, 2.0, None, ALU.add))
                V.link(v.reciprocal(w, w))
                V.link(TN(w, w, e, ALU.mult))
                V.link(TN(q, w, w, ALU.mult))
                V.link(TS(r_, q, 1.0 / 17, 1.0 / 15, ALU.mult, ALU.add))
                for k in (13, 11, 9, 7, 5, 3, 1):
                    V.link(TN(r_, r_, q, ALU.mult))
                    V.link(TS(r_, r_, 1.0 / k, None, ALU.add))
                V.link(TN(r_, r_, w, ALU.mult))
                V.link(TS(t_, z, 0.0, None, ALU.max))
                V.link(STT(dt_t[:, :, :].rearrange("p c h -> p (c h)"), r_, 2.0, t_, ALU.mult, ALU.add))
                V.link(STT(dA[:, :, :], dt_t[:, :, :], -1.0, ahead[:, :].unsqueeze(1).broadcast_to((P, SC, SH)),
                           ALU.mult, ALU.mult), s("dA_ready"))
                dve.wait_ge(s("cs_ready"), 1)
                dve.wait_ge(s("ncs_ready"), 1)
                V.link(TN(dte[:, :, :], ncs[:, :, :], M[:, 1, P:2 * P].rearrange("p (c h) -> p c h", h=SH), ALU.add),
                       s("dtex_ready"))
                dve.wait_ge(s("dte_ready"), 1)
                V.link(v.memset(pre[:, :, 0:3], 0.0))

            def heads4(a):
                return a.rearrange("p c (r n) -> p c r n", n=64)

            def ssd_xdt(n):
                dve.wait_ge(s("ssd_turned"), n + 1)
                V.settle()
                for c in range(SC):
                    V.send(TN(xdt[:, c, :].rearrange("p (r n) -> p r n", n=64),
                              Mf[:, 256 * c:256 * c + 256].rearrange("p (r n) -> p r n", n=64),
                              dt_t[:, c, 4 * n:4 * n + 4].unsqueeze(2).broadcast_to((P, 4, 64)), ALU.mult))
                V.settle()
                for c in range(3):
                    V.send(TN(xdte[:, c, :].rearrange("p (r n) -> p r n", n=64),
                              xdt[:, c, :].rearrange("p (r n) -> p r n", n=64),
                              dte[:, c, 4 * n:4 * n + 4].unsqueeze(2).broadcast_to((P, 4, 64)), ALU.mult),
                           s("xdt_ready") if c == 2 else None)

            def ssd_scan(n):
                dve.wait_ge(s("ssd_states"), n + 1)
                V.settle()
                r4 = lambda a: a.rearrange("p (r n) -> p r n", n=64)
                V.link(v.tensor_copy(S[:, 0, :], M[:, 2, 0:256]))
                for c in (1, 2):
                    V.link(TN(r4(S[:, c, :]), r4(S[:, c - 1, :]),
                              ctot[:, c, 4 * n:4 * n + 4].unsqueeze(2).broadcast_to((P, 4, 64)), ALU.mult))
                    V.link(TN(S[:, c, :], S[:, c, :], M[:, 2, 256:512] if c == 1 else M[:, 3, 0:256], ALU.add),
                           s("S_ready") if c == 2 else None)

            def ssd_m(n, c):
                dve.wait_ge(s("dec_ready"), 16 * n + 4 * c + 4)
                V.send(TN(dec[:, c % 2, :, :], dec[:, c % 2, :, :],
                          cbt[:, c, :].unsqueeze(1).broadcast_to((P, 4, P)), ALU.mult), s("m_ready"))

            def ssd_y(n):
                dve.wait_ge(s("yy_ready"), n + 1)
                dve.wait_ge(s("ssd_yoff"), n + 1)
                V.settle()
                V.link(TN(yy[:, :, P:], yy[:, :, P:], M[:, 0:2, P:], ALU.mult))
                V.link(TN(yy[:, :, P:], yy[:, :, P:], M[:, 2:4, P:], ALU.add))
                V.link(v.tensor_copy(yy[:, :, 0:P], M[:, 2:4, 0:P]), s("y_banks_read"))
                for i in range(2):
                    V.send(STT(yy[:, i, :], xs[n % 2][:, i, :], dsk[:, 2 * n + i:2 * n + i + 1], yy[:, i, :],
                               ALU.mult, ALU.add))
                V.settle()
                V.link(TN(yy[:, :, :], yy[:, :, :], sz[:, :, :], ALU.mult), s("yg_ready"))

            def ssd_final(n):
                dve.wait_ge(s("yg_rstd"), n + 1)
                V.settle()
                V.link(TN(yy[:, :, :], yy[:, :, :], rstd[:, :].unsqueeze(1).broadcast_to((P, 2, T)), ALU.mult))
                for i in range(2):
                    V.send(TS(yy[:, i, :], yy[:, i, :], cols[:, C_MNG + 2 * n + i:C_MNG + 2 * n + i + 1], None, ALU.mult),
                           s("yn_ready") if i else None)
                p = 2 * (n % 4)
                mid_low(yy[:, :, :], mid_lo[:, p:p + 2, :], mid_hi[:, p:p + 2, :])

            def layernorm_v():
                V.settle()
                for t in range(TT):
                    V.send(v.bn_stats(bns[:, t, :], vn[:, t, :]))
                V.settle()
                for t in range(TT):
                    V.send(v.bn_aggr(bna[:, t, :], bns[:, t, :]), s("bna_ready") if t == TT - 1 else None)
                V.settle()
                c = cols[:, C_LB:C_LB + 8].rearrange("p (a j) -> p a j", j=4)
                V.link(TN(lbt[:, 2, :], c[:, 0, :], c[:, 1, :], ALU.max))
                V.link(TN(lbt[:, 0:2, :], c, lbt[:, 2, :].unsqueeze(1).broadcast_to((P, 2, 4)), ALU.subtract),
                       s("lbx_ready"))
                dve.wait_ge(s("lnr_ready"), 1)
                dve.wait_ge(s("lbe_ready"), 1)
                V.link(TN(lbt[:, 2, :], lbt[:, 0, :], lbt[:, 1, :], ALU.add))
                V.link(v.reciprocal(lbt[:, 2, :], lbt[:, 2, :]))
                V.link(TN(lbt[:, 0, :], lbt[:, 0, :], lbt[:, 2, :], ALU.mult))
                V.link(TS(lbt[:, 1, :], lbt[:, 0, :], -1.0, 1.0, ALU.mult, ALU.add))
                for t in range(TT):
                    V.send(TS(vn[:, t, :], vn[:, t, :], bna[:, t, 0:1], bna[:, t, 1:2], ALU.subtract, ALU.mult))
                dve.wait_ge(s("gm_in"), 80)
                V.settle()
                V.link(TN(vn[:, :, :], vn[:, :, :], lng[:, :].unsqueeze(1).broadcast_to((P, TT, GW)), ALU.mult))
                V.link(TN(vn[:, :, :], vn[:, :, :], lnb[:, :].unsqueeze(1).broadcast_to((P, TT, GW)), ALU.add))
                dve.wait_ge(s("wsp_turned"), 1)
                V.link(TN(wspT[:, :, :], Mf[:, 0:1024].rearrange("p (g t) -> p g t", t=P),
                          tri[:, :].unsqueeze(1).broadcast_to((P, 8, P)), ALU.mult), s("gm_ready"))

            def gmlp_out():
                dve.wait_ge(s("gm_mixed"), 1)
                V.settle()
                for i in range(4):
                    V.link(TN(hsq[:, :].rearrange("p (c t) -> p c t", t=P), M[:, i, :].rearrange("p (c t) -> p c t", t=P),
                              bsp[:, i, :].unsqueeze(1).broadcast_to((P, TT, P)), ALU.add))
                    V.link(TN(uact[:, i, :], hsq[:, :], uact[:, i, :], ALU.mult), s("gm_y") if i % 2 else None)
                for p in range(2):
                    dve.wait_ge(s("ya_hi_ready"), p + 1)
                    V.send(TN(ya_lo[:, 2 * p:2 * p + 2, :], uact[:, 2 * p:2 * p + 2, :],
                              ya_hi[:, 2 * p:2 * p + 2, :].bitcast(F32), ALU.subtract), s("ya_ready"))

            def hg_f(jp, g):
                dve.wait_ge(*read_out(g))
                V.settle()
                for i in range(2):
                    h = 2 * jp + i
                    V.send(TS(fk[:, i, :], fk[:, i, :], lbt[:, 1, h:h + 1], lbt[:, 0, h:h + 1], ALU.mult, ALU.add))
                V.settle()
                V.link(TS(ke[:, :, :], fk[:, :, :], -1.0, 1.0, ALU.mult, ALU.add), s("hf_f"))

            def hg_chain(jp, g):
                dve.wait_ge(s("lnf_ready"), jp + 1)
                dve.wait_ge(s("bounds_ready"), 1)
                V.settle()
                for i in range(2):
                    V.link(v.tensor_tensor_scan(bcum[:, i, :], reset[:, :], fk[:, i, :], 0.0, ALU.mult, ALU.add),
                           s("bcum_ready") if i else None)
                dve.wait_ge(s("eb_ready"), jp + 1)
                dve.wait_ge(*read_out(g))
                V.link(TN(qd[:, :, :], qd[:, :, :], fk[:, :, :], ALU.mult), s("qd_ready"))
                ch = lambda a: a.rearrange("p (c t) -> p c t", t=HC)
                for i in range(2):
                    last = ch(bcum[:, i, :])[:, :, HC - 1:HC].broadcast_to((P, T // HC, HC))
                    V.send(TN(ch(kx[:, i, :]), last, ch(bcum[:, i, :]), ALU.subtract), s("kx_ready") if i else None)
                dve.wait_ge(s("enb_ready"), jp + 1)
                V.settle()
                V.link(TN(fk[:, :, :], ke[:, :, :], fk[:, :, :], ALU.mult))
                dve.wait_ge(s("kxe_ready"), jp + 1)
                V.link(TN(ke[:, :, :], ke[:, :, :], kx[:, :, :], ALU.mult), s("hg_ops_ready"))

            def hg_head(n):
                dve.wait_ge(s("hg_scores"), n + 1)
                V.settle()
                sc = M[:, 0, :].rearrange("p (b t) -> p b t", t=P)
                V.link(TN(att[:, :, :], sc, am_hi[:, :].unsqueeze(1).broadcast_to((P, TT, P)), ALU.min))
                V.link(TN(att[:, :, :], att[:, :, :], am_lo[:, :].unsqueeze(1).broadcast_to((P, TT, P)), ALU.max),
                       s("att_ready"))
                dve.wait_ge(s("hg_dS"), n + 1)
                dve.wait_ge(s("dlast_ready"), n // 2 + 1)
                for c in range(7):
                    d = M[:, 2 + c % 2, P * (c // 2):P * (c // 2) + P]
                    if c == 0:
                        V.link(v.tensor_copy(HS[:, 0, :], d))
                    else:
                        V.link(STT(HS[:, c, :], HS[:, c - 1, :], dlast[:, n % 2, c:c + 1], d, ALU.mult, ALU.add),
                               s("HS_ready") if c == 6 else None)
                dve.wait_ge(s("orstd_ready"), n + 1)
                V.link(TN(o_n[:, n, :], M[:, 0, :], rstd[:, :], ALU.mult))
                dve.wait_ge(*read_out(first["hg_og"] + 1))
                V.link(STT(o_n[:, n, :], o_n[:, n, :], cols[:, C_HGN + n:C_HGN + n + 1], sog[:, n, :],
                           ALU.mult, ALU.mult), s("on_ready"))
                dve.wait_ge(s("yb_hi_ready"), n + 1)
                V.send(TN(yb_lo[:, n, :], o_n[:, n, :], yb_hi[:, n, :].bitcast(F32), ALU.subtract), s("yb_ready"))

            def expert_low(u, slot, par_slot):
                dve.wait_ge(s("ehi_ready"), u + 1)
                TN(ew_lo[:, par_slot, :, :], eraw[:, slot, :, :], ew_hi[:, par_slot, :, :].bitcast(F32),
                   ALU.subtract).then_inc(s("elo_ready"), 1)

            def x_low(e, b):
                dve.wait_ge(s("e_xhi"), e + 1)
                TN(xgT_lo[:, b, :, :], M[:, b, :].rearrange("p (k t) -> p k t", t=BK), xgT_hi[:, b, :, :].bitcast(F32),
                   ALU.subtract).then_inc(s("e_xlo"), 1)

            def expert_act(e, b, done):
                dve.wait_ge(s("e_units"), done)
                dve.wait_ge(s("e_sg"), e + 1)
                TN(eact[:, b, :], esg[:, b, :], M[0:BK, 3, :], ALU.mult).then_inc(s("e_act"), 1)

            def act_low(e, b):
                dve.wait_ge(s("e_ahi"), e + 1)
                TN(a_lo[:, b, :, :], pj[:, 0, 0:4 * BK].rearrange("p (k t) -> p k t", t=BK), a_hi[:, b, :, :].bitcast(F32),
                   ALU.subtract).then_inc(s("e_alo"), 1)

            def dve_round(e, par, w3_done):
                for v in range(6):
                    expert_low(unit_no(e, v), raw_slot(1, v), split_slot(par, v))
                    if v == 1:
                        x_low(e, par)
                        expert_act(e - 1, 1 - par, w3_done)
                act_low(e - 1, 1 - par)

            def one_hot_first(dst, src, mxv, n, ix, io):
                b3 = lambda a: a.unsqueeze(2).broadcast_to((P, TT, n))
                i3 = io[:, 0:n].unsqueeze(1).broadcast_to((P, TT, n))
                V.link(TN(dst, src, b3(mxv), ALU.is_lt))
                V.link(STT(dst, dst, BIG, i3, ALU.mult, ALU.add))
                V.link(v.tensor_reduce(ix, dst, AX, ALU.min))
                V.link(TN(dst, i3, b3(ix), ALU.is_equal))

            def dve_moe():
                b3 = lambda a, n: a.unsqueeze(2).broadcast_to((P, TT, n))
                dve.wait_ge(s("logits"), 1)
                dve.wait_ge(s("iota_ready"), 1)
                V.settle()
                V.link(v.tensor_copy(L, M[:, 0, 0:TT * 36].rearrange("p (t n) -> p t n", n=36)))
                V.link(v.tensor_reduce(gmx, L[:, :, 0:4], AX, ALU.max))
                V.link(TN(t4, L[:, :, 0:4], b3(gmx, 4), ALU.subtract), s("r_shift"))
                V.link(TN(ghot, L[:, :, 0:4], b3(gmx, 4), ALU.is_lt))
                i3 = io32[:, 0:4].unsqueeze(1).broadcast_to((P, TT, 4))
                V.link(STT(ghot, ghot, BIG, i3, ALU.mult, ALU.add))
                V.link(v.tensor_reduce(gix, ghot, AX, ALU.min))
                V.link(TN(ghot, i3, b3(gix, 4), ALU.is_equal))
                dve.wait_ge(s("r_exp"), 1)
                V.link(v.tensor_reduce(gse, t4, AX, ALU.add))
                V.link(v.reciprocal(gpg, gse))
                V.link(TN(sel, L[:, :, 4:12], b3(ghot[:, :, 0], 8), ALU.mult))
                for q in range(1, 4):
                    V.link(TN(t8, L[:, :, 4 + 8 * q:12 + 8 * q], b3(ghot[:, :, q], 8), ALU.mult))
                    V.link(TN(sel, sel, t8, ALU.add))
                V.link(v.tensor_reduce(mx[:, 0, :], sel, AX, ALU.max))
                one_hot_first(t8, sel, mx[:, 0, :], 8, eix[:, 0, :], io32)
                V.link(STT(sel2, t8, -BIG, sel, ALU.mult, ALU.add))
                V.link(v.tensor_reduce(mx[:, 1, :], sel2, AX, ALU.max))
                one_hot_first(t8, sel2, mx[:, 1, :], 8, eix[:, 1, :], io32)
                V.link(TN(wex, mx[:, 1, :], mx[:, 0, :], ALU.subtract), s("r_shift"))
                for k in range(2):
                    V.link(STT(eix[:, k, :], gix, 8.0, eix[:, k, :], ALU.mult, ALU.add))
                    V.link(TN(Ak[k], io32.unsqueeze(1).broadcast_to((P, TT, NE)), b3(eix[:, k, :], NE), ALU.is_equal))
                V.link(TN(Aall, Ak[0], Ak[1], ALU.add), s("chosen"))
                dve.wait_ge(s("r_exp"), 2)
                V.link(TS(gate[:, 0, :], wex, 1.0, None, ALU.add))
                V.link(v.reciprocal(gate[:, 0, :], gate[:, 0, :]))
                V.link(TN(gate[:, 0, :], gate[:, 0, :], gpg, ALU.mult))
                V.link(TN(gate[:, 1, :], gate[:, 0, :], wex, ALU.mult))
                dve.wait_ge(s("ranks"), 1)
                V.link(v.tensor_copy(rank, M[:, 1, 0:TT * NE].rearrange("p (t n) -> p t n", n=NE)))
                V.link(v.tensor_copy(cnt, M[:, 2, 0:NE]))
                V.link(TS(nbk, cnt, float(BK), None, ALU.is_gt))
                for q in range(2, T // BK):
                    V.link(STT(nbk, cnt, float(BK * q), nbk, ALU.is_gt, ALU.add))
                V.link(v.memset(t1, 1.0))
                V.link(v.tensor_tensor_scan(incl, t1, nbk, 0.0, ALU.mult, ALU.add))
                V.link(TN(obk, incl, nbk, ALU.subtract))
                for k in range(2):
                    V.link(TN(t32, Ak[k], rank, ALU.mult))
                    V.link(v.tensor_reduce(rk[:, k, :], t32, AX, ALU.add))
                    V.link(TN(t32, Ak[k], obk.unsqueeze(1).broadcast_to((P, TT, NE)), ALU.mult))
                    V.link(v.tensor_reduce(ok[:, k, :], t32, AX, ALU.add))
                V.link(TS(qk, rk, float(BK), None, ALU.is_ge))
                for q in range(2, T // BK):
                    V.link(STT(qk, rk, float(BK * q), qk, ALU.is_ge, ALU.add))
                V.link(STT(wk, qk, -float(BK), rk, ALU.mult, ALU.add))
                V.link(TN(bk, ok, qk, ALU.add))
                V.link(TS(bk, bk, float(NE - 1), None, ALU.add))
                V.link(TN(bk, bk, eix, ALU.subtract))
                V.link(TS(sk, qk, 0.0, None, ALU.is_gt))
                V.link(TN(bk, bk, sk, ALU.mult))
                V.link(TN(bk, bk, eix, ALU.add))
                V.link(STT(sk, wk, float(NB), bk, ALU.mult, ALU.add))
                V.link(v.tensor_copy(slot_t, sk), s("slots_ready"))
                V.link(STT(sk, bk, float(BK), wk, ALU.mult, ALU.add))
                V.link(v.tensor_copy(slot_y, sk))
                V.link(TN(ovc, incl.unsqueeze(1).broadcast_to((P, OVB, NE)),
                          io32[:, 0:OVB].unsqueeze(2).broadcast_to((P, OVB, NE)), ALU.is_le))
                V.link(v.tensor_reduce(ovf[:, 0:OVB], ovc, AX, ALU.add))
                V.link(TS(ovf[:, 0:OVB], ovf[:, 0:OVB], float(NE - 1), None, ALU.min))
                V.link(v.tensor_copy(ovf[:, OVB:OVB + 1], incl[:, NE - 1:NE]))
                V.link(v.tensor_copy(ovt, ovf), s("table_ready"))

                for w in range(4):
                    expert_low(w, w, w)
                x_low(0, 0)
                dve_round(1, 1, 4)
                with dve.Fori(1, NE // 2) as it:
                    for b in range(2):
                        dve_round(2 * it + b, b, unit_no(2 * it + b - 1, 4))
                for w in range(2):
                    expert_low(unit_no(NE, w), raw_slot(1, w), split_slot(0, w))
                expert_act(NE - 1, 1, unit_no(NE - 1, 4))
                act_low(NE - 1, 1)
                nov = dve.value_load(ovt[0:1, OVB:OVB + 1], min_val=0, max_val=OVB)
                with dve.Fori(0, OVB) as jj:
                    with dve.If(jj < nov):
                        n, u = NE + jj, 6 * NE + 6 * jj
                        x_low(n, 0)
                        for w in range(6):
                            expert_low(u + w, w, w % 4)
                        expert_act(n, 0, u + 4)
                        act_low(n, 0)
                dve.wait_ge(s("p_turned"), 1)
                V.link(v.tensor_copy(pT[:, :, :], M[:, 0:2, :]), s("pT_ready"))
                for t in range(TT):
                    dve.wait_ge(s(f"yg_in{t % 2}"), 32 * (t // 2) + 32)
                    V.link(TS(yg[:, t % 2, 0, :], yg[:, t % 2, 0, :], gate[:, 0, t:t + 1], None, ALU.mult))
                    V.link(STT(yg[:, t % 2, 0, :], yg[:, t % 2, 1, :], gate[:, 1, t:t + 1], yg[:, t % 2, 0, :],
                               ALU.mult, ALU.add), s("comb_ready"))
                    dve.wait_ge(s("combined"), t + 1)
                    for hf in range(2):
                        V.send(TN(x[:, 4 * hf:4 * hf + 4, P * t:P * t + P], x[:, 4 * hf:4 * hf + 4, P * t:P * t + P],
                                  pj[:, 2 * (t % 2) + hf, :].rearrange("p (i n) -> p i n", n=P), ALU.add), s("x_new"))
                dve.wait_ge(s("pt_hi_ready"), 1)
                V.send(TN(pt_lo[:, :, :], pT[:, :, :], pt_hi[:, :, :].bitcast(F32), ALU.subtract), s("pt_ready"))

            for g, G in enumerate(groups):
                k, j = G["kind"], G["j"]
                done = (s("subs_done"), G["end"])
                banks = pj2(g)
                free = read_out(g)
                if k == "conv_v":
                    dve.wait_ge(*read_out(g - 1))
                    dve.wait_ge(*done)
                    V.settle()
                    V.link(TN(cv[:, :, 2:], banks, cgate[:, :, :], ALU.mult), free)
                    w = lambda tap, i: cols[:, C_ACONV + 8 * tap + 2 * j + i:C_ACONV + 8 * tap + 2 * j + i + 1]
                    for i in range(2):
                        V.send(TS(cu[:, i, :], cv[:, i, 0:T], w(0, i), None, ALU.mult))
                    V.settle()
                    for tap in (1, 2):
                        for i in range(2):
                            V.send(STT(cu[:, i, :], cv[:, i, tap:tap + T], w(tap, i), cu[:, i, :], ALU.mult, ALU.add))
                        V.settle()
                elif k == "conv_b":
                    dve.wait_ge(*done)
                    V.settle()
                    V.send(TN(cu[:, :, :], banks, cu[:, :, :], ALU.mult), free)
                    mid_low(cu[:, :, :], mid_lo[:, 2 * j:2 * j + 2, :], mid_hi[:, 2 * j:2 * j + 2, :])
                elif k == "y_only":
                    if j == 0 and moe:
                        dve.wait_ge(s("y_cleared"), 128)
                    dve.wait_ge(*done)
                    V.send(v.tensor_copy(y[:, 2 * j:2 * j + 2, :], banks), free)
                elif k == "y_last":
                    dve.wait_ge(*done)
                    V.send(TN(y[:, 2 * j:2 * j + 2, :], y[:, 2 * j:2 * j + 2, :], banks, ALU.add), free)
                elif k == "ffn_u":
                    dve.wait_ge(*read_out(g - 1))
                    dve.wait_ge(*done)
                    V.send(TN(tmp[:, :, :], banks, sg[:, :, :], ALU.mult), free)
                    mid_low(tmp[:, :, :], mid_lo[:, 2 * j:2 * j + 2, :], mid_hi[:, 2 * j:2 * j + 2, :])
                elif k == "ssd_x":
                    n = j - 1
                    if j == 0:
                        ssd_head()
                    if n >= 0:
                        ssd_xdt(n)
                elif k == "ssd_bc":
                    n = j - 1
                    if n >= 0:
                        ssd_scan(n)
                        ssd_m(n, 0)
                        ssd_m(n, 1)
                    dve.wait_ge(*read_out(g - 1))
                    conv4(j, 0, xs[j % 2])
                    if n >= 0:
                        ssd_m(n, 2)
                        ssd_m(n, 3)
                elif k == "ssd_z":
                    n = j - 1
                    dve.wait_ge(*read_out(g - 5 if j == 5 else g - 1))
                    conv4(j, 1, bct[j % 2])
                    advance(g + 1)
                    if n >= 0:
                        ssd_y(n)
                    advance(g + 2)
                    if n >= 0:
                        ssd_final(n)
                    if j == SG - 1:
                        n = j
                        ssd_xdt(n)
                        ssd_scan(n)
                        for c in range(SC):
                            ssd_m(n, c)
                        ssd_y(n)
                        ssd_final(n)
                elif k == "gm_v" and j == 1:
                    dve.wait_ge(*read_out(g))
                    dve.wait_ge(*read_out(g - 1))
                elif k == "gm_u" and j == 1:
                    layernorm_v()
                elif k == "hg_i" and j == 1:
                    gmlp_out()
                elif k == "hg_f":
                    if j == 1:
                        hg_head(1)
                    hg_f(j, g)
                elif k == "hg_q":
                    hg_chain(j, g)
                elif k == "hg_og":
                    if j == 1:
                        hg_head(0)
                elif k == "up_a":
                    dve.wait_ge(*read_out(g - 1))
                    dve.wait_ge(*done)
                    V.send(TN(sga[:, :, :], banks, sga[:, :, :], ALU.mult), free)
                    if j == 0:
                        hg_head(2)
                        hg_head(3)
                elif k == "up_b":
                    dve.wait_ge(*read_out(g - 1))
                    dve.wait_ge(*done)
                    V.settle()
                    V.link(TN(sgb[:, :, :], banks, sgb[:, :, :], ALU.mult))
                    V.send(TN(sgb[:, :, :], sgb[:, :, :], sga[:, :, :], ALU.add), free)
                    mid_low(sgb[:, :, :], m2_lo[:, 2 * j:2 * j + 2, :], m2_hi[:, 2 * j:2 * j + 2, :])
                elif k == "w_out":
                    dve.wait_ge(*done)
                    V.send(TN(x[:, 2 * j:2 * j + 2, :], x[:, 2 * j:2 * j + 2, :], banks, ALU.add), free)
                elif k == "ple":
                    dve.wait_ge(*read_out(g - 1))
                    dve.wait_ge(*done)
                    V.settle()
                    V.link(TN(tmp[:, :, :], banks, sg[:, :, :], ALU.mult), free)
                    for i in range(2):
                        V.send(TN(x[:, 2 * j + i, :], x[:, 2 * j + i, :], tmp[:, i, :], ALU.add), s("x_new"))
                for c in chunk_after.get(g, ()):
                    if c:
                        V.settle()
                        coefficients(c)
                if g in step_after:
                    step(step_after[g])
                    if step_after[g] == 5 and moe:
                        dve_moe()
                        phase[0] = 1
                        advance(g + 2)
                        step(6)
                        continue
                advance(g + 2)
            if moe:
                step(7)
                for t in range(0, TT, 2):
                    dve.wait_ge(s("o_turned"), t + 1)
                    V.link(v.tensor_copy(otok[:, t, :], pj[:, 0:2, :].rearrange("p a b -> p (a b)")), s("otok_even"))
            if not moe:
                V.settle(); V.send(v.memset(acc[:, 0, 0:1], 0.0), s("test_done"))

        @block.tensor
        def _(pe):
            mm, turn = nc.tensor.matmul, nc.tensor.transpose

            def ada_sum(u):
                c = chunk_of(u)
                pe.wait_ge(s("ada_acc"), u + 1)
                if u % 12 in (0, 8) and c >= 3:
                    pe.wait_ge(s("coef_read"), c - 2)
                for m in range(2):
                    ins = mm(M[:, c % 3, 2 * u + m:2 * u + m + 1], acc[:, u % 2, P * m:P * m + P], ones[:, 0:1],
                             start=True, stop=True)
                ins.then_inc(s("ada_summed"), 1)

            def step(r):
                if 1 <= r <= 4:
                    pe.wait_ge(s("ysq_ready"), 4 * r)
                    pe.wait_ge(s("ssq_ready"), 3 * r)
                    pe.wait_ge(s("rstd_x_ready"), r)
                    if r == 3:
                        pe.wait_ge(s("y_banks_read"), SG)
                    for i, a in enumerate((ssq[:, :], sqt[:, 0, :], sqt[:, 1, :])):
                        ins = mm(M[:, 3, :], ones[:, :], a, start=i == 0, stop=i == 2)
                    ins.then_inc(s("ysum_ready"), 1)
                    pe.wait_ge(s("rstd_y_ready"), r)
                elif r:
                    pe.wait_ge(s("rstd_x_ready"), r)
                if r == 5:
                    pe.wait_ge(s("HS_ready"), 4)
                for i in range(DT):
                    pe.wait_ge(s("sq_ready"), 8 * r + i + 1)
                    ins = mm(M[:, 3, :], ones[:, :], y[:, i, :], start=i == 0, stop=i == DT - 1)
                ins.then_inc(s("xsum_ready"), 1)

            def products(g, G, k, q, k0, part, last):
                hi, lo = srcs[G.get("src", "h")]
                for m in range(2):
                    cols_ = slice(P * m, P * m + P)
                    o = pj[:, 2 * (g % 2) + m, :]
                    wh, wl = w_hi[:, q % 4, k - k0, cols_], w_lo[:, q % 4, k - k0, cols_]
                    mm(o, wh, hi[:, k, :], start=k == 0, stop=False)
                    mm(o, wh, lo[:, k, :], start=False, stop=False)
                    ins = mm(o, wl, hi[:, k, :], start=False, stop=k == G["nk"] - 1)
                if last:
                    ins.then_inc(s("subs_done"), 1)

            def token_products(g, G):
                for q, _, _ in G["subs"]:
                    pe.wait_ge(s("hi_ready"), q + 1)
                    pe.wait_ge(s("lo_ready"), q + 1)
                for t in range(TT):
                    o = pj[:, 2 * (g % 2) + t // 2, 256 * (t % 2):256 * (t % 2) + 256]
                    for q, k0, k1 in G["subs"]:
                        for k in range(k0, k1):
                            wh, wl = w_hi[:, q % 4, k - k0, :], w_lo[:, q % 4, k - k0, :]
                            hh, hl = h_hi[:, k, P * t:P * t + P], h_lo[:, k, P * t:P * t + P]
                            mm(o, hh, wh, start=k == 0, stop=False)
                            mm(o, hl, wh, start=False, stop=False)
                            ins = mm(o, hh, wl, start=False, stop=k == DT - 1)
                        if t == TT - 1:
                            ins.then_inc(s("subs_done"), 1)

            def ssd_head():
                pe.wait_ge(s("ssd_in"), 80)
                pe.wait_ge(s("coef_read"), 8)
                for t in range(TT):
                    for i, hh in enumerate((h_hi, h_lo)):
                        for k in range(DT):
                            if t == 0 and i == 0:
                                pe.wait_ge(s("h_ready"), 8 * HSTEP[2] + k + 1)
                            ins = mm(M[:, 0, SH * t:SH * t + SH], hh[:, k, P * t:P * t + P].bitcast(F32), wdt[:, k, :],
                                     start=i == 0 and k == 0, stop=i == 1 and k == DT - 1)
                ins.then_inc(s("dt_raw"), 1)
                pe.wait_ge(s("dA_ready"), 1)
                dAf = dA[:, :, :].rearrange("p c h -> p (c h)")
                mm(M[:, 1, 0:P], tri[:, :], dAf, start=True, stop=True)
                mm(M[:, 1, P:2 * P], ones[:, :], dAf, start=True, stop=True).then_inc(s("cs_ready"), 1)

            def ssd_a(n):
                pe.wait_ge(s("xbc_ready"), 4 * n + 4)
                if n == 0:
                    pe.wait_ge(s("dte_ready"), 1)
                else:
                    pe.wait_ge(s("y_banks_read"), n)
                    pe.wait_ge(s("yg_rstd"), n)
                for c in range(SC):
                    for i in range(2):
                        turn(Mf[:, 256 * c + P * i:256 * c + P * i + P], xs[n % 2][:, i, P * c:P * c + P], ident[:, :])
                for c in range(SC):
                    turn(M[:, 2, P * c:P * c + P], bct[n % 2][:, 0, P * c:P * c + P], ident[:, :])
                for c in range(SC):
                    ins = mm(M[:, 3, P * c:P * c + P], bct[n % 2][:, 0, P * c:P * c + P],
                             bct[n % 2][:, 1, P * c:P * c + P], start=True, stop=True)
                ins.then_inc(s("ssd_turned"), 1)

            def ssd_csb(n, c):
                if c < 2:
                    pe.wait_ge(s("xdt_ready"), n + 1)
                else:
                    pe.wait_ge(s("dec_ready"), 16 * n + 4 * (c - 2) + 4)
                for r in range(4):
                    o = M[:, c % 2, P * r:P * r + P]
                    h = 4 * n + r
                    mm(o, bc(dA[:, c, h:h + 1], (P, P)), tri[:, :], start=True, stop=False)
                    ins = mm(o, identb[:, :], negb[:, :], start=False, stop=True)
                ins.then_inc(s("csb_ready"), 1)

            def ssd_states(n):
                pe.wait_ge(s("bt_ready"), 2 * n + 2)
                pe.wait_ge(s("xdt_ready"), n + 1)
                for c in range(3):
                    o = M[:, 2, 256 * c:256 * c + 256] if c < 2 else M[:, 3, 0:256]
                    ins = mm(o, btok[:, c, :], xdte[:, c, :], start=True, stop=True)
                ins.then_inc(s("ssd_states"), 1)

            def ssd_ydiag(n, c):
                pe.wait_ge(s("m_ready"), 4 * n + c + 1)
                pe.wait_ge(s("S_ready"), n + 1)
                for i in range(2):
                    for hf in range(2):
                        ins = mm(M[64 * hf:64 * hf + 64, 2 + i, P * c:P * c + P],
                                 xdt[:, c, P * i + 64 * hf:P * i + 64 * hf + 64], dec[:, c % 2, 2 * i + hf, :],
                                 start=True, stop=True)

            def ssd_ecs(n):
                pe.wait_ge(s("dec_ready"), 16 * n + 16)
                for i in range(2):
                    for c in range(SC):
                        for hf in range(2):
                            h = 4 * n + 2 * i + hf
                            ins = mm(M[64 * hf:64 * hf + 64, i, P * c:P * c + P], bc(dA[:, c, h:h + 1], (P, 64)),
                                     tri[:, :], start=True, stop=True)
                ins.then_inc(s("ecs_ready"), 1)

            def ssd_yoff(n):
                pe.wait_ge(s("yy_ready"), n + 1)
                for i in range(2):
                    for c in range(1, SC):
                        ins = mm(M[:, i, P * c:P * c + P], S[:, c - 1, P * i:P * i + P],
                                 bct[n % 2][:, 1, P * c:P * c + P], start=True, stop=True)
                ins.then_inc(s("ssd_yoff"), 1)

            def ssd_ynorm(n):
                pe.wait_ge(s("ygsq_ready"), n + 1)
                mm(M[:, 2, :], ones[:, :], sz[:, 0, :], start=True, stop=False)
                mm(M[:, 2, :], ones[:, :], sz[:, 1, :], start=False, stop=True).then_inc(s("yg_summed"), 1)

            def turn_wsp():
                pe.wait_ge(s("gm_in"), 80)
                for i in range(GW // 64):
                    ins = turn(Mf[:, P * i:P * i + P], wsp[:, i, :], ident[:, :])
                ins.then_inc(s("wsp_turned"), 1)

            def gm_mix():
                pe.wait_ge(s("gm_ready"), 1)
                for i in range(4):
                    for c in range(TT):
                        for hf in range(2):
                            w = 2 * i + hf
                            ins = mm(M[64 * hf:64 * hf + 64, i, P * c:P * c + P], vn[:, c, 64 * w:64 * w + 64],
                                     wspT[:, w, :], start=True, stop=True)
                ins.then_inc(s("gm_mixed"), 1)

            def hg_scores(n):
                i = n % 2
                pe.wait_ge(s("hg_ops_ready"), n // 2 + 1)
                if n:
                    pe.wait_ge(s("on_ready"), n)
                else:
                    pe.wait_ge(s("gm_y"), 2)
                for b in range(TT):
                    mm(M[:, 0, P * b:P * b + P], fk[:, i, P * b:P * b + P], qd[:, i, P * b:P * b + P],
                       start=True, stop=True)
                for b in range(TT):
                    ins = turn(M[:, 1, P * b:P * b + P], ke[:, i, P * b:P * b + P], ident[:, :])
                ins.then_inc(s("hg_scores"), 1)

            def hg_dstate(n):
                pe.wait_ge(s("ketok_ready"), n + 1)
                if n:
                    pe.wait_ge(s("HS_ready"), n)
                for c in range(7):
                    p0 = 64 * (c % 2)
                    ins = mm(M[:, 2 + c % 2, P * (c // 2):P * (c // 2) + P], ketok[p0:p0 + 64, c // 2, :],
                             vtok[p0:p0 + 64, c // 2, P * n:P * n + P], start=True, stop=True)
                ins.then_inc(s("hg_dS"), 1)

            def hg_out(n):
                pe.wait_ge(s("att_ready"), n + 1)
                pe.wait_ge(s("HS_ready"), n + 1)
                for b in range(TT):
                    mm(M[:, 0, P * b:P * b + P], vtok[:, b, P * n:P * n + P], att[:, b, :], start=True, stop=False)
                    for c in (2 * b, 2 * b + 1):
                        if c:
                            ins = mm(M[:, 0, HC * c:HC * c + HC], HS[:, c - 1, :], qd[:, n % 2, HC * c:HC * c + HC],
                                     start=False, stop=c % 2 == 1)
                ins.then_inc(s("hg_out"), 1)

            def hg_norm(n):
                pe.wait_ge(s("osq_ready"), n + 1)
                mm(M[:, 1, :], ones[:, :], hsq[:, :], start=True, stop=True).then_inc(s("osum_ready"), 1)

            def carry_wait(o):
                mm(o, ones[:, :], ones[:, 0:1], start=True, stop=True)

            def turn_xg(b):
                carry_wait(M[:, b, 0:1])
                for k in range(DT):
                    ins = turn(M[:, b, BK * k:BK * k + BK], xg[:, b, P * k:P * k + P], ident[0:BK, 0:BK])
                ins.then_inc(s("e_turned"), 1)

            def unit(u, slot, v, b):
                pe.wait_ge(s("elo_ready"), u + 1)
                hi, lo = (xgT_hi, xgT_lo) if v < 4 else (a_hi, a_lo)
                o = M[0:BK, 2 + v // 2, :] if v < 4 else pj[0:BK, v - 2, :]
                k0 = 4 * (v % 2) if v < 4 else 0
                for k in range(4):
                    first_, last = k == 0 and (v >= 4 or v % 2 == 0), k == 3 and (v >= 4 or v % 2 == 1)
                    mm(o, hi[:, b, k0 + k, :], ew_hi[:, slot, k, :], start=first_, stop=False)
                    mm(o, hi[:, b, k0 + k, :], ew_lo[:, slot, k, :], start=False, stop=False)
                    ins = mm(o, lo[:, b, k0 + k, :], ew_hi[:, slot, k, :], start=False, stop=last)
                ins.then_inc(s("e_units"), 1)

            def turn_act(b):
                carry_wait(pj[:, 0, 0:1])
                for k in range(4):
                    ins = turn(pj[:, 0, BK * k:BK * k + BK], eact[:, b, P * k:P * k + P], ident[0:BK, 0:BK])
                ins.then_inc(s("e_aturned"), 1)

            def pe_round(e, par, gathers):
                for v in range(6):
                    if v == 0:
                        pe.wait_ge(s("e_xlo"), e + 1)
                        pe.wait_ge(s("e_sg"), e)
                    elif v == 2:
                        pe.wait_ge(s("e_act"), e)
                        if not isinstance(e, int) or e >= 2:
                            pe.wait_ge(s("e_alo"), e - 1)
                        turn_act(1 - par)
                    elif v == 4:
                        if gathers is not None:
                            pe.wait_ge(s(f"xg_in{1 - par}"), 16 * gathers)
                            pe.wait_ge(s("e_xlo"), e)
                            turn_xg(1 - par)
                        pe.wait_ge(s("e_alo"), e)
                        if not isinstance(e, int) or e >= 2:
                            pe.wait_ge(s("e_ytok"), e - 1)
                    unit(unit_no(e, v), split_slot(par, v), v, par if v < 4 else 1 - par)

            def moe_program():
                pe.wait_ge(s("mh_ready"), 8)
                pe.wait_ge(s("wr_in"), 32)
                for t in range(TT):
                    for k in range(DT):
                        ins = mm(M[:, 0, 36 * t:36 * t + 36], y[:, k, P * t:P * t + P], wr[:, k, :],
                                 start=k == 0, stop=k == DT - 1)
                ins.then_inc(s("logits"), 1)
                pe.wait_ge(*read_out(n_pre - 1))
                pe.wait_ge(*read_out(n_pre - 2))
                for t in range(TT):
                    if t >= 2:
                        pe.wait_ge(s("htok_ready"), t - 1)
                    rows = pj[:, 2 * (t % 2):2 * (t % 2) + 2, :].rearrange("p a b -> p (a b)")
                    for i in range(DT):
                        ins = turn(rows[:, P * i:P * i + P], y[:, i, P * t:P * t + P], ident[:, :])
                    ins.then_inc(s("h_turned"), 1)
                pe.wait_ge(s("chosen"), 1)
                for t in range(TT):
                    o = M[:, 1, NE * t:NE * t + NE]
                    mm(o, stri[:, :], Aall[:, t, :], start=True, stop=t == 0)
                    for u in range(t):
                        mm(o, ones[:, :], Aall[:, u, :], start=False, stop=u == t - 1)
                for t in range(TT):
                    ins = mm(M[:, 2, 0:NE], ones[:, :], Aall[:, t, :], start=t == 0, stop=t == TT - 1)
                ins.then_inc(s("ranks"), 1)
                pe.wait_ge(s("slots_ready"), 1)
                pe.wait_ge(s("htok_ready"), TT)
                for b in range(2):
                    pe.wait_ge(s(f"xg_in{b}"), 16)
                    turn_xg(b)
                pe.wait_ge(s("e_xlo"), 1)
                for v in range(4):
                    unit(v, v, v, 0)
                pe_round(1, 1, 2)
                with pe.Fori(1, NE // 2 - 1) as it:
                    pe_round(2 * it, 0, it + 1)
                    pe_round(2 * it + 1, 1, it + 2)
                pe_round(NE - 2, 0, NE // 2)
                pe_round(NE - 1, 1, None)
                pe.wait_ge(s("e_act"), NE)
                pe.wait_ge(s("e_alo"), NE - 1)
                turn_act(1)
                pe.wait_ge(s("e_alo"), NE)
                pe.wait_ge(s("e_ytok"), NE - 1)
                for v in range(2):
                    unit(unit_no(NE, v), split_slot(0, v), 4 + v, 1)
                pe.wait_ge(s("table_ready"), 1)
                nov = pe.value_load(ovt[0:1, OVB:OVB + 1], min_val=0, max_val=OVB)
                with pe.Fori(0, OVB) as j:
                    with pe.If(j < nov):
                        n, u = NE + j, 6 * NE + 6 * j
                        pe.wait_ge(s("xg_in0"), 8 * NE + 16 + 16 * j)
                        pe.wait_ge(s("e_xlo"), n)
                        turn_xg(0)
                        pe.wait_ge(s("e_xlo"), n + 1)
                        pe.wait_ge(s("e_sg"), n)
                        pe.wait_ge(s("e_act"), n)
                        for v in range(4):
                            unit(u + v, v, v, 0)
                        pe.wait_ge(s("e_act"), n + 1)
                        pe.wait_ge(s("e_alo"), n)
                        turn_act(0)
                        pe.wait_ge(s("e_alo"), n + 1)
                        pe.wait_ge(s("e_ytok"), n)
                        for v in (4, 5):
                            unit(u + v, v % 4, v, 0)
                pe.wait_ge(s("rows_done"), 1)
                mm(M[:, 3, 0:1], ones[:, :], ones[:, 0:1], start=True, stop=True).then_inc(s("experts_done"), 1)
                pe.wait_ge(s("p_in"), 16)
                for i in range(2):
                    for t in range(TT):
                        ins = turn(M[:, i, P * t:P * t + P], ptok[:, t, P * i:P * i + P], ident[:, :])
                ins.then_inc(s("p_turned"), 1)
                for t in range(TT):
                    pe.wait_ge(s("comb_ready"), t + 1)
                    if t >= 2:
                        pe.wait_ge(s("x_new"), 40 + 2 * (t - 1))
                    o = pj[:, 2 * (t % 2):2 * (t % 2) + 2, :].rearrange("p a b -> p (a b)")
                    for i in range(DT):
                        ins = turn(o[:, P * i:P * i + P], yg[:, t % 2, 0, P * i:P * i + P], ident[:, :])
                    ins.then_inc(s("combined"), 1)

            def hook(k, j, n_sub):
                n = j - 1
                if k == "ssd_x" and n_sub == 0 and n >= 0:
                    if n >= 1:
                        ssd_ynorm(n - 1)
                    ssd_a(n)
                elif k == "ssd_x" and n >= 0:
                    ssd_csb(n, 0)
                    ssd_csb(n, 1)
                    ssd_states(n)
                elif k == "ssd_bc" and n >= 0:
                    ssd_ydiag(n, n_sub)
                    ssd_csb(n, 2 + n_sub)
                elif k == "ssd_z":
                    if n >= 0 and n_sub == 0:
                        ssd_ydiag(n, 2)
                        ssd_ydiag(n, 3)
                        ssd_ecs(n)
                    elif n >= 0:
                        ssd_yoff(n)
                    if j == SG - 1 and n_sub == 1:
                        ssd_ynorm(j - 1)
                        n = j
                        ssd_a(n)
                        ssd_csb(n, 0)
                        ssd_csb(n, 1)
                        ssd_states(n)
                        for c in range(2):
                            ssd_ydiag(n, c)
                            ssd_csb(n, 2 + c)
                        ssd_ydiag(n, 2)
                        ssd_ydiag(n, 3)
                        ssd_ecs(n)
                        ssd_yoff(n)
                        ssd_ynorm(n)
                elif (k, j) == ("hg_og", 0) and n_sub == 1:
                    hg_scores(0)
                elif (k, j) == ("hg_og", 1):
                    hg_dstate(0) if n_sub == 0 else hg_out(0)
                elif (k, j) == ("hg_f", 1):
                    hg_norm(0) if n_sub == 0 else hg_scores(1)
                elif (k, j) == ("hg_q", 1):
                    if n_sub == 0:
                        hg_dstate(1)
                    else:
                        hg_out(1)
                        hg_norm(1)
                elif (k, j) == ("up_a", 0):
                    hg_scores(2)
                elif (k, j) == ("gate_b", 0):
                    if n_sub == 0:
                        hg_dstate(2)
                    else:
                        hg_out(2)
                        hg_norm(2)
                        hg_scores(3)
                        hg_dstate(3)
                        hg_out(3)
                        hg_norm(3)

            pe.wait_ge(s("const_ready"), 1)
            pe.wait_ge(s("params_in"), 16 * 13)
            for t in range(4):
                n = P if t < 3 else C_END - 3 * P
                ins = turn(M[:, 0, P * t:P * t + n], stage[0:n, t, :], ident[0:n, 0:n])
            ins.then_inc(s("params_turned"), 1)
            pe.wait_ge(s("x_in"), 16)
            for i in range(DT):
                if i >= 4:
                    pe.wait_ge(s("x_new"), i - 3)
                for t in range(TT):
                    ins = turn(pj[:, i % 4, P * t:P * t + P], xtok[:, t, P * i:P * i + P], ident[:, :])
                ins.then_inc(s("x_turned"), 1)
            pe.wait_ge(s("x_new"), 8)
            pe.wait_ge(s("cols_ready"), 1)
            for u in ada_at[0]:
                ada_sum(u)
            step(0)
            for g, G in enumerate(groups):
                if g >= 2:
                    pe.wait_ge(*read_out(g - 2))
                if g:
                    for u in ada_at.get(g, ()):
                        ada_sum(u)
                if G["kind"] == "ssd_x" and G["j"] == 0:
                    ssd_head()
                sem, base = G.get("wait", (None, 0))
                if G.get("tok"):
                    if sem:
                        pe.wait_ge(s(sem), base + DT)
                    token_products(g, G)
                else:
                    for n_sub, (q, k0, k1) in enumerate(G["subs"]):
                        pe.wait_ge(s("hi_ready"), q + 1)
                        pe.wait_ge(s("lo_ready"), q + 1)
                        for k in range(k0, k1):
                            if sem in ("mid_ready", "ya_ready"):
                                pe.wait_ge(s(sem), base + k // 2 + 1)
                            elif sem:
                                pe.wait_ge(s(sem), base + (0 if sem == "pt_ready" else k) + 1)
                            products(g, G, k, q, k0, n_sub, k == k1 - 1)
                        hook(G["kind"], G["j"], n_sub)
                if (G["kind"], G["j"]) == ("gm_u", 0):
                    turn_wsp()
                elif (G["kind"], G["j"]) == ("hg_i", 1):
                    gm_mix()
                if g in step_after:
                    step(step_after[g])
                    if step_after[g] == 5 and moe:
                        moe_program()
                        step(6)
            for g, us in ada_at.items():
                if g >= NG:
                    for u in us:
                        ada_sum(u)
            if moe:
                step(7)
                pe.wait_ge(s("fin_ready"), 8)
                for t in range(TT):
                    if t >= 2:
                        pe.wait_ge(s("otok_odd" if t % 2 else "otok_even"), 1)
                    o = pj[:, 2 * (t % 2):2 * (t % 2) + 2, :].rearrange("p a b -> p (a b)")
                    for i in range(DT):
                        ins = turn(o[:, P * i:P * i + P], y[:, i, P * t:P * t + P], ident[:, :])
                    ins.then_inc(s("o_turned"), 1)


_INS = ("x", "c", "ada_w", "ada_b", "norm_g", "a_w_in", "a_conv_w", "a_w_out", "m_w_in", "m_conv_w", "m_conv_b",
        "m_dt_bias", "m_a_log", "m_d", "m_norm_g", "m_w_out", "f_w_in", "f_w_out", "p_2", "g_mix_2", "w_in_2",
        "gm_ln_g_2", "gm_ln_b_2", "gm_w_sp_2", "gm_b_sp_2", "w_up_a_2", "hg_lb_param_2", "hg_norm_g_2", "w_up_b_2",
        "w_out_2", "g_ffn_2", "w_grp_2", "w_exp_2", "w1_2", "w3_2", "w2_2", "g_ple_2", "w_pg_2", "w_ple_2", "g_final_2")


def kernel(**inputs):
    import numpy as _np
    import concourse.bacc as _bacc
    from concourse import mybir as _mybir
    from concourse.bass_utils import run_bass_kernel_spmd as _run

    nc = _bacc.Bacc("TRN2", target_bir_lowering=False, num_devices=1)
    arrays, args = {}, {}
    for name in _INS:
        a = _np.ascontiguousarray(inputs[name])
        arrays[f"in_{name}_dram"] = a
        args[name] = nc.dram_tensor(f"in_{name}_dram", a.shape, _mybir.dt.from_np(a.dtype), kind="ExternalInput").ap()
    out = nc.dram_tensor("out_0_dram", (1, T, D), F32, kind="ExternalOutput").ap()
    build(nc, args, out)
    r = _run(nc, [arrays], core_ids=[0])
    return r.results[0]["out_0_dram"]
```

```python
from contextlib import ExitStack

import concourse.bass as bass
from concourse import mybir

F32 = mybir.dt.float32
F32R = mybir.dt.float32r
BF16 = mybir.dt.bfloat16
I32 = mybir.dt.int32
ALU = mybir.AluOpType
ACT = mybir.ActivationFunctionType
AX = mybir.AxisListType.X

P = 128
T = 512
TT = T // P
D = 1024
DT = D // P
FF = 2816
FT = FF // P
INNER = 2048
SG = 8
SH = 32
SC = T // P
GW = 512
HC = 64
NE = 32
DE = 512
BK = 64
OVB = 15
NB = NE + OVB
EPS = 1e-6
BIG = 1e30
KB = 1024


class Stream:

    def __init__(self, eng, own):
        self.eng, self.own, self.count, self.last = eng, own, {}, None

    def send(self, ins, sem=None):
        if isinstance(sem, tuple):
            ins.then_inc(sem[0], 1)
            self.last = sem
            return
        sem = self.own if sem is None else sem
        ins.then_inc(sem, 1)
        self.count[id(sem)] = self.count.get(id(sem), 0) + 1
        self.last = (sem, self.count[id(sem)])

    def settle(self):
        if self.last:
            self.eng.wait_ge(*self.last)

    def link(self, ins, sem=None):
        self.send(ins, sem)
        self.settle()


def further_blocks(eng, count, body):
    with eng.If(count > 0):
        body(0)
        with eng.If(count > 1):
            with eng.Fori(1, OVB) as j:
                with eng.If(j < count):
                    body(j)


def bc(ap, shape):
    return ap.broadcast_to(shape)



def plan():
    groups, ring = [], []

    def grp(kind, j, w, c, nk, k0=0, c2=None, **kw):
        ring.append(("grp", len(groups)))
        groups.append(dict(kind=kind, j=j, w=w, c=c, nk=nk, k0=k0, c2=c2, **kw))

    ada = iter(range(48))

    def ada_next(n=1):
        for _ in range(n):
            u = next(ada, None)
            if u is not None:
                ring.append(("ada", u))

    ada_next(8)
    for j in range(4):
        grp("conv_c", j, "a_w_in", D + 256 * j, 8)
        ada_next()
        grp("conv_v", j, "a_w_in", 2 * D + 256 * j, 8)
        ada_next()
        grp("conv_b", j, "a_w_in", 256 * j, 8)
        ada_next()
    for j in range(4):
        grp("y_only", j, "a_w_out", 256 * j, 8, src="mid")
        ada_next()

    def ffn(i):
        for half, (p0, p1) in enumerate(((0, 6), (6, 11))):
            for j in range(p0, p1):
                grp("ffn_g", j - p0, f"f_w_in{i}", 256 * j, 8)
                ada_next()
                grp("ffn_u", j - p0, f"f_w_in{i}", FF + 256 * j, 8)
                ada_next()
            for j in range(4):
                grp(("y_first", "y_last")[half], j, f"f_w_out{i}", 256 * j, 2 * (p1 - p0), 2 * p0, src="mid")
                ada_next()

    ffn(0)
    assert next(ada, None) is None
    for g in range(SG):
        grp("ssd_x", g, "m_w_in", INNER + 256 * g, 8)
        grp("ssd_bc", g, "m_w_in", 2 * INNER + P * g, 8, c2=2 * INNER + D + P * g)
        if g == 5:
            for j in range(4):
                grp("y_first", j, "m_w_out", 256 * j, 8, 0, src="mid")
        grp("ssd_z", g, "m_w_in", 256 * g, 8)
    for j in range(4):
        grp("y_last", j, "m_w_out", 256 * j, 8, 8, src="mid")
    ffn(1)
    grp("gm_u", 0, "w_in_2", 0, 8)
    for j in range(2):
        grp("gm_v", j, "w_in_2", GW + 256 * j, 8, tok=True)
    grp("gm_u", 1, "w_in_2", 256, 8)
    for j in range(2):
        grp("hg_i", j, "w_in_2", 4 * GW + 256 * j, 8, tok=True)
    for j in range(2):
        grp("hg_f", j, "w_in_2", 3 * GW + 256 * j, 8)
        grp("hg_q", j, "w_in_2", 2 * GW + 256 * j, 8)
        if j == 0:
            for jj in range(2):
                grp("hg_og", jj, "w_in_2", 5 * GW + 256 * jj, 8)
    for js in ((0, 1), (2,), (3,)):
        for j in js:
            grp("gate_a", j, "w_in_2", 6 * GW + 256 * j, 8)
            grp("up_a", j, "w_up_a_2", 256 * j, 4, src="ya")
        for j in js:
            grp("gate_b", j, "w_in_2", 6 * GW + D + 256 * j, 8)
            grp("up_b", j, "w_up_b_2", 256 * j, 4, src="yb")
    for j in range(4):
        grp("w_out", j, "w_out_2", 256 * j, 8, src="merged")
    for j in range(4):
        grp("pg", j, "w_pg_2", 256 * j, 8)
        grp("ple", j, "w_ple_2", 256 * j, 2, src="pt")
    return groups, ring


def number(groups, ring):
    q = 0
    for g, G in enumerate(groups):
        G["subs"] = []
        for s in range(0, G["nk"], 4):
            G["subs"].append((q, s, min(s + 4, G["nk"])))
            q += 1
        G["end"] = q
    units, u = [], 0
    for what, n in ring:
        if what == "ada":
            units.append(("ada", n, 0, 8))
        else:
            for s in range(0, groups[n]["nk"], 8):
                units.append(("grp", n, s, min(s + 8, groups[n]["nk"])))
    return units


C_MCONV, C_ADAB, C_MCONVB = 0, 128, 224
C_NG, C_ACONV, C_MNG, C_GMIX, C_GFFN, C_COND = 256, 320, 344, 360, 368, 376
C_LB, C_HGN, C_GPLE, C_GFIN, C_END = 384, 392, 396, 404, 412


def build(nc, I, out):
    groups, ring = plan()
    units = number(groups, ring)
    first = {}
    for g, G in enumerate(groups):
        first.setdefault(G["kind"], g)

    W = {"a_w_in": I["a_w_in"][0], "a_w_out": I["a_w_out"][0], "m_w_in": I["m_w_in"][0], "m_w_out": I["m_w_out"][0],
         "f_w_in0": I["f_w_in"][0], "f_w_in1": I["f_w_in"][1], "f_w_out0": I["f_w_out"][0], "f_w_out1": I["f_w_out"][1],
         "w_in_2": I["w_in_2"][0], "w_up_a_2": I["w_up_a_2"][0], "w_up_b_2": I["w_up_b_2"][0],
         "w_out_2": I["w_out_2"][0], "w_pg_2": I["w_pg_2"][0], "w_ple_2": I["w_ple_2"][0]}

    with ExitStack() as ctx:
        base = (nc.sbuf_base + 31) // 32 * 32
        ctx.enter_context(nc.sbuf_tensor("arena", [P, (nc.sbuf_usable_end - base) // 4 - 16], F32))

        def at(name, kb, shape, dt=F32):
            return nc.alloc_sbuf_tensor_at(name, shape, dt, offset=base + int(kb * KB))

        x = at("x", 0, [P, DT, T])
        h_hi = at("h_hi", 16, [P, DT, T], F32R)
        h_lo = at("h_lo", 32, [P, DT, T], F32R)
        y = at("y", 48, [P, DT, T])
        mid_hi = at("mid_hi", 64, [P, 12, T], F32R)
        mid_lo = at("mid_lo", 88, [P, 12, T], F32R)
        raw = at("raw", 112, [P, 3, 8, 256])
        w_hi = at("w_hi", 136, [P, 4, 4, 256], F32R)
        w_lo = at("w_lo", 152, [P, 4, 4, 256], F32R)
        xtok = at("xtok", 64, [P, TT, D])
        zrow = at("zrow", 108, [P, D])
        cgate = at("cgate", 48, [P, 2, T])
        cv = at("cv", 52, [P, 2, T + 2])
        cu = at("cu", 57, [P, 2, T])
        rstd = at("rstd", 176, [P, T])
        ssq = at("ssq", 178, [P, T])
        sqt = at("sqt", 180, [P, 2, T])
        sg = at("sg", 184, [P, 2, T])
        tmp = at("tmp", 188, [P, 2, T])
        acc = at("acc", 192, [P, 2, 256])
        xs = [at(f"xs{b}", kb, [P, 2, T]) for b, kb in ((0, 80), (1, 168))]
        bct = [at(f"bct{b}", kb, [P, 2, T]) for b, kb in ((0, 84), (1, 172))]
        pre = at("pre", 104, [P, 2, T + 3])
        btok = at("btok", 109.0625, [P, SC, P])
        dt_t = at("dt_t", 111.0625, [P, SC, SH])
        dA = at("dA", 200.5, [P, SC, SH])
        xdt = at("xdt", 178, [P, SC, 256])
        yy = [at(f"yy{k}", 88 + 4 * k, [P, 2, T]) for k in range(4)]
        yq = [at(f"yq{k}", 64 + 4 * k, [P, 2, T]) for k in range(4)]
        xdte = at("xdte", 182, [P, 3, 256])
        wdt_hi = at("wdt_hi", 185, [P, DT, SH], F32R)
        wdt_lo = at("wdt_lo", 186, [P, DT, SH], F32R)
        dtr = at("dtr", 182, [SH, T])
        dec = at("dec", 185, [P, 2, 4, P])
        S = at("S", 189, [P, 3, 256])
        sz = at("sz", 192, [P, 2, T])
        cbt = at("cbt", 196, [P, SC, P])
        ncs = at("ncs", 198, [P, SC, SH])
        dte = at("dte", 198.5, [P, SC, SH])
        ctot = at("ctot", 199, [P, SC, SH])
        negb = at("negb", 199.5, [P, SC, P], BF16)
        csr = at("csr", 108.0625, [P // 4 * 3, T], BF16)
        csx = at("csx", 184, [P // 4 * 3, T])
        sp = at("sp", 178, [P, 6, SC * SH])
        ya_hi = at("ya_hi", 64, [P, 4, T], F32R)
        ya_lo = at("ya_lo", 72, [P, 4, T], F32R)
        yb_hi = at("yb_hi", 80, [P, 4, T], F32R)
        yb_lo = at("yb_lo", 88, [P, 4, T], F32R)
        m2_hi = at("m2_hi", 48, [P, DT, T], F32R)
        m2_lo = at("m2_lo", 96, [P, DT, T], F32R)
        lng = at("lng", 80, [P, GW])
        lnb = at("lnb", 82, [P, GW])
        bsp = at("bsp", 84, [P, 4, P])
        wsp = at("wsp", 86, [P, 8, P])
        wspT = at("wspT", 90, [P, 8, P])
        vn = at("vn", 48, [P, TT, GW])
        uact = at("uact", 56, [P, 4, T])
        sog = at("sog", 48, [P, 4, T])
        vtok = at("vtok", 96, [P, TT, GW])
        HS = at("HS", 104, [P, 7, P])
        att = at("att", 108, [P, TT, P])
        ketok = at("ketok", 110, [P, TT, P])
        o_n = at("o_n", 88, [P, 4, T])
        qd = at("qd", 178, [P, 2, T])
        bcum = at("bcum", 182, [P, 2, T])
        ke = at("ke", 186, [P, 2, T])
        fk = at("fk", 190, [P, 2, T])
        kx = at("kx", 56, [P, 2, T])
        sga = [at(f"sga{b}", 60 - 4 * b, [P, 2, T]) for b in range(2)]
        sgb = at("sgb", 182, [P, 2, T])
        am_hi = at("am_hi", 194, [P, P])
        am_lo = at("am_lo", 194.5, [P, P])
        reset = at("reset", 195, [P, T])
        hsq = at("hsq", 197, [P, T])
        bns = at("bns", 199, [P, TT, 6])
        bna = at("bna", 199.25, [P, TT, 2])
        lbt = at("lbt", 199.5, [P, 4, 4])
        dlast = at("dlast", 199.75, [P, 2, 8])
        htok = at("htok", 16, [P, 2, D])
        xg = at("xg", 24, [BK, 2, D])
        xgT_hi = at("xgT_hi", 32, [P, 2, DT, BK], F32R)
        xgT_lo = at("xgT_lo", 36, [P, 2, DT, BK], F32R)
        eact = at("eact", 40, [BK, 2, DE])
        a_hi = at("a_hi", 44, [P, 2, 4, BK], F32R)
        a_lo = at("a_lo", 46, [P, 2, 4, BK], F32R)
        esg = at("esg", 48, [BK, 2, DE])
        ytok = at("ytok", 16, [BK, 2, D])
        ew_hi = at("ew_hi", 64, [P, 4, 4, DE], F32R)
        ew_lo = at("ew_lo", 96, [P, 4, 4, DE], F32R)
        eraw = at("eraw", 128, [P, 6, 4, DE])
        lgs = at("lgs", 45.25, [36, T])
        wr = at("wr", 44, [P, DT, 36])
        yg = at("yg", 64, [P, TT, 2, D])
        rt = at("rt", 178, [P, 5120])
        ptok = at("ptok", 52, [P, TT, 256])
        pT = at("pT", 56, [P, 2, T])
        pt_hi = at("pt_hi", 96, [P, 2, T], F32R)
        pt_lo = at("pt_lo", 100, [P, 2, T], F32R)
        otok = at("otok", 64, [P, 4, D])
        off = [201.0]

        def const(name, shape, dt=F32):
            n = 2 if dt == BF16 else 4
            for k in shape[1:]:
                n *= k
            t = at(name, off[0], shape, dt)
            off[0] += (n + 31) // 32 * 32 / KB
            return t

        ident = const("ident", [P, P])
        ones = const("ones", [P, P])
        tri = const("tri", [P, P])
        stri = const("stri", [P, P])
        identb = const("identb", [P, P], BF16)
        sel3 = const("sel3", [P, SH], BF16)
        cols = const("cols", [P, C_END])
        mod = const("mod", [P, 96])
        sco = const("sco", [P, 4, DT])
        gco = const("gco", [P, 4, DT])
        wdt = const("wdt", [P, DT, SH])
        dtb = const("dtb", [P, SH])
        ahead = const("ahead", [P, SH])
        dsk = const("dsk", [P, 16])
        epsc = const("epsc", [P, 1])
        zero = const("zero", [P, 1])
        sil = const("sil", [P, DT])
        spare = const("spare", [P, 1])
        spare_a = const("spare_a", [P, 1])
        assert base + off[0] * KB <= nc.sbuf_usable_end, off
        stage = at("stage", 178, [P, 4, P])

        pj = ctx.enter_context(nc.psum_tensor("pj", [P, 4, T], F32))
        M = ctx.enter_context(nc.psum_tensor("M", [P, 4, T], F32))
        Mf = M[:, :, :].rearrange("p a b -> p (a b)")

        at_rt = [0]

        def table(shape, dt=F32):
            n = 1
            for k in shape[1:]:
                n *= k
            v = rt[:, at_rt[0]:at_rt[0] + n]
            at_rt[0] += (n + 7) // 8 * 8
            v = v.bitcast(dt) if dt != F32 else v
            names = "abc"[:len(shape) - 1]
            if len(shape) > 2:
                v = v.rearrange("p (" + " ".join(names) + ") -> p " + " ".join(names),
                                **dict(zip(names, shape[1:])))
            return v

        L = table([P, TT, 36])
        io64 = table([P, BK])
        io32 = io64[:, 0:NE]
        iot = table([P, BK], I32)
        tokid = table([P, TT], I32)
        tokf = table([P, TT])
        thr = table([P, 8])
        cq = table([P, NE, 7])
        rq = table([P, 2 * TT, 7])
        hot_w = table([P, 2 * TT, BK])
        hot_b = table([P, 2 * TT, NB])
        gmx, gse, gpg, gix = (table([P, TT]) for _ in range(4))
        t4 = table([P, TT, 4])
        ghot = table([P, TT, 4])
        sel, sel2, t8 = (table([P, TT, 8]) for _ in range(3))
        mx = table([P, 2, TT])
        eix = table([P, 2, TT])
        wex = table([P, TT])
        gate = table([P, 2, TT])
        Ak = [table([P, TT, NE]) for _ in range(2)]
        Aall = table([P, TT, NE])
        rank = table([P, TT, NE])
        t32 = table([P, TT, NE])
        cnt, nbk, incl, obk, t1 = (table([P, NE]) for _ in range(5))
        rk8, ok8, qk8, wk8, bk8, sk8 = (table([P, 2 * TT]) for _ in range(6))
        rk, ok, qk, wk, bk, sk = (a.rearrange("p (k t) -> p k t", t=TT) for a in (rk8, ok8, qk8, wk8, bk8, sk8))
        ovc = table([P, OVB, NE])
        ovf = table([P, 16])
        ovt = table([P, 16], I32)
        slot_y = table([P, 2, TT], I32)
        idx = table([P, NB], I32)
        ic = table([P, 2], I32)
        hdram = nc.dram_tensor("h_rows", (T, D), F32).ap()
        ydram = nc.dram_tensor("y_rows", (NB * BK, D), F32).ap()
        assert at_rt[0] <= 5120, at_rt

        sems = {}

        def s(name):
            if name not in sems:
                sems[name] = ctx.enter_context(nc.semaphore(name))
            return sems[name]

        HSTEP = {0: 0, 1: 1, 2: 2, 3: 3, 4: 4, 6: 5}
        step_after, r = {}, 0
        for g, G in enumerate(groups):
            if (G["kind"] in ("y_only", "y_last", "w_out") and G["j"] == 3):
                r += 1
                step_after[g] = r
        mid_pairs = 0
        for g, G in enumerate(groups):
            k, src = G["kind"], G.get("src", "h")
            if k == "conv_c" and G["j"] == 0:
                G["wait"] = ("h_ready", 0)
            if g and (g - 1) in step_after and k != "pg":
                G["wait"] = ("h_ready", 8 * HSTEP[step_after[g - 1]])
            if k == "pg" and G["j"] == 0:
                G["wait"] = ("h_ready", 8 * HSTEP[6])
            if k in ("conv_b", "ffn_u", "ssd_z", "up_b"):
                G["pair"] = mid_pairs
                mid_pairs += 1
        done_pairs = 0
        for g, G in enumerate(groups):
            if G["kind"] in ("y_only", "y_first", "y_last", "w_out") and G["j"] == 0:
                G["wait"] = ("mid_ready", done_pairs)
                done_pairs += (G["nk"] + 1) // 2
        for g, G in enumerate(groups):
            if G["kind"] == "up_a" and G["j"] == 0:
                G["wait"] = ("ya_ready", 0)
            if G["kind"] == "up_b" and G["j"] == 0:
                G["wait"] = ("yb_ready", 0)
            if G["kind"] == "ple" and G["j"] == 0:
                G["wait"] = ("pt_ready", 0)

        ada_at, prev = {}, []
        g_seen = -1
        for what, n in ring:
            if what == "ada":
                ada_at.setdefault(g_seen + 1, []).append(n)
            else:
                g_seen = n
        chunk_of = lambda u: 2 * (u // 12) + (u % 12 >= 8)
        chunk_after = {}
        for g, us in ada_at.items():
            for u in us:
                if u % 12 in (7, 11):
                    chunk_after.setdefault(g, []).append(chunk_of(u))
        srcs = {"merged": (m2_hi, m2_lo), "h": (h_hi, h_lo), "mid": (mid_hi, mid_lo), "ya": (ya_hi, ya_lo), "yb": (yb_hi, yb_lo),
                "pt": (pt_hi, pt_lo)}

        raw_at, raw_n, split_at = [], [0, 0, 0], []
        nsub = 0
        for n, (what, g, s0, s1) in enumerate(units):
            raw_n[n % 3] += 32 if what == "grp" and groups[g]["c2"] is not None else 16
            raw_at.append(raw_n[n % 3])
            nsub += (s1 - s0 + 3) // 4 if what == "grp" else 0
            split_at.append(nsub)
        n_pre = first["pg"]

        def read_out(g):
            return s(f"pj_free{g % 2}"), g // 2 + 1

        def pj2(g):
            return pj[:, 2 * (g % 2):2 * (g % 2) + 2, :]

        def pjt(g):
            return pj2(g).rearrange("p a (b n) -> p (a b) n", n=256)

        def unit_no(e, v):
            return 6 * e - 2 + v

        def raw_slot(e, v):
            return (v + 4) % 6 if e else v

        def split_slot(par, v):
            return v % 4 if par is None or par else (2 + v) % 4

        def arrivals(e, v):
            return 16 * (e + (v >= 2))

        gate_of = lambda j: sga[1 if j == 1 else 0][:, :, :]
        group_no = {(G["kind"], G["j"]): g for g, G in enumerate(groups)}

        block = ctx.enter_context(nc.Block())

        @block.sync
        def _(sp):
            st = stage
            rows = [(0, 0, I["m_conv_w"][0].rearrange("k (j p) -> (k j) p", p=P)),
                    (1, 0, I["ada_b"].rearrange("(j p) -> j p", p=P)),
                    (1, 96, I["m_conv_b"].rearrange("a (j p) -> (a j) p", p=P)),
                    (2, 0, I["norm_g"].rearrange("a b (j p) -> (a b j) p", p=P)),
                    (2, 64, I["a_conv_w"][0].rearrange("k (j p) -> (k j) p", p=P)),
                    (2, 88, I["m_norm_g"].rearrange("a (j p) -> (a j) p", p=P)),
                    (2, 104, I["g_mix_2"].rearrange("a (j p) -> (a j) p", p=P)),
                    (2, 112, I["g_ffn_2"].rearrange("a (j p) -> (a j) p", p=P)),
                    (2, 120, I["c"].rearrange("a (j p) -> (a j) p", p=P)),
                    (3, 0, I["hg_lb_param_2"].rearrange("a (j p) -> (a j) p", p=P)),
                    (3, 8, I["hg_norm_g_2"].rearrange("a (j p) -> (a j) p", p=P)),
                    (3, 12, I["g_ple_2"].rearrange("a (j p) -> (a j) p", p=P)),
                    (3, 20, I["g_final_2"].rearrange("(j p) -> j p", p=P))]
            for t, r0, src in rows:
                sp.dma_start(st[r0:r0 + src.shape[0], t, :], src).then_inc(s("params_in"), 16)
            sp.dma_start(xtok[:, :, :], I["x"][0].rearrange("(t p) d -> p t d", p=P)).then_inc(s("x_in"), 16)

            def load_unit(n):
                what, g, s0, s1 = units[n]
                if n >= 3:
                    w3, g3, _, _ = units[n - 3]
                    if w3 == "ada":
                        sp.wait_ge(s("ada_acc"), g3 + 1)
                    else:
                        sp.wait_ge(s("lo_ready"), split_at[n - 3])
                if what == "ada":
                    sp.dma_start(raw[:, n % 3, :, :], I["ada_w"][:, 256 * g:256 * g + 256].rearrange(
                        "(k p) n -> p k n", p=P)).then_inc(s(f"raw_in{n % 3}"), 16)
                    return
                G = groups[g]
                w = W[G["w"]][(G["k0"] + s0) * P:(G["k0"] + s1) * P, :].rearrange("(k p) n -> p k n", p=P)
                if G["c2"] is None:
                    sp.dma_start(raw[:, n % 3, 0:s1 - s0, :], w[:, :, G["c"]:G["c"] + 256]).then_inc(
                        s(f"raw_in{n % 3}"), 16)
                else:
                    for m, c in enumerate((G["c"], G["c2"])):
                        sp.dma_start(raw[:, n % 3, 0:s1 - s0, P * m:P * m + P], w[:, :, c:c + P]).then_inc(
                            s(f"raw_in{n % 3}"), 16)

            n_moe = next((n for n, (w_, g_, _, _) in enumerate(units) if w_ == "grp" and g_ == first["pg"]),
                         len(units))
            for n in range(n_moe):
                load_unit(n)
                if n == 10:
                    sp.dma_start(wdt[:, :, :], W["m_w_in"][:, 2 * INNER + 2 * D:].rearrange(
                        "(k p) n -> p k n", p=P)).then_inc(s("ssd_in"), 16)
                    sp.dma_start(dtb[:, :], I["m_dt_bias"][0].partition_broadcast(P)).then_inc(s("ssd_in"), 16)
                    sp.dma_start(ahead[:, :], I["m_a_log"][0].partition_broadcast(P)).then_inc(s("ssd_in"), 16)
                    for hf in range(2):
                        sp.dma_start(dsk[64 * hf:64 * hf + 64, :], I["m_d"][0].rearrange(
                            "(i h) -> h i", h=2)[hf].partition_broadcast(64),
                                     allow_slow_non_contiguous=True).then_inc(s("ssd_in"), 16)
            sp.wait_ge(s("subs_done"), groups[first["pg"] - 1]["end"])
            sp.dma_start(wr[:, :, 0:4], I["w_grp_2"][0].rearrange("(k p) n -> p k n", p=P)).then_inc(s("wr_in"), 16)
            sp.dma_start(wr[:, :, 4:36], I["w_exp_2"][0].rearrange("(k p) n -> p k n", p=P)).then_inc(s("wr_in"), 16)

            def load(e, v, slot):
                w = (I["w1_2"], I["w3_2"], I["w2_2"])[v // 2][0][bass.ds(e, 1)].rearrange("a k n -> (a k) n")
                w = w[512 * (v % 2):512 * (v % 2) + 512, :] if v < 4 else w[:, 512 * (v % 2):512 * (v % 2) + 512]
                sp.dma_start(eraw[:, slot, :, :], w.rearrange("(k p) n -> p k n", p=P)).then_inc(s(f"e_in{slot}"), 16)

            def load_round(e, first_wait):
                for v in range(6):
                    if v >= first_wait:
                        sp.wait_ge(s("elo_ready"), unit_no(e, v) - 5)
                    load(e if v < 4 else e - 1, v, raw_slot(1, v))

            for v in range(4):
                load(0, v, v)
            load_round(1, 2)
            with sp.Fori(1, NE // 2) as it:
                for b in range(2):
                    load_round(2 * it + b, 0)
            for v in range(2):
                sp.wait_ge(s("elo_ready"), unit_no(NE, v) - 5)
                load(NE - 1, 4 + v, raw_slot(1, v))
            sp.wait_ge(s("table_ready"), 1)
            nov = sp.value_load(ovt[0:1, OVB:OVB + 1], min_val=0, max_val=OVB)

            def block_in(j):
                e = sp.value_load(ovt[0:1, bass.ds(j, 1)], min_val=0, max_val=NE - 1)
                for v in range(6):
                    sp.wait_ge(s("elo_ready"), 6 * NE - 5 + 6 * j + v)
                    load(e, v, v)
            further_blocks(sp, nov, block_in)
            sp.wait_ge(s("experts_done"), 1)
            for n in range(n_moe, len(units)):
                load_unit(n)
            for t in range(TT):
                sp.wait_ge(s("otok_odd" if t % 2 else "otok_even"), t // 2 + 1)
                sp.dma_start(out[0, P * t:P * t + P, :], otok[:, t, :]).then_inc(s("out_done"), 16)
            sp.wait_ge(s("out_done"), 16 * TT)

        @block.gpsimd
        def _(pool):
            V = Stream(pool, s("pool"))
            g = nc.gpsimd
            V.send(g.memset(ident[:, :], 0.0))
            V.send(g.memset(identb[:, :], 0.0))
            V.send(g.memset(ones[:, :], 1.0))
            V.send(g.memset(tri[:, :], 1.0))
            V.send(g.memset(stri[:, :], 1.0))
            V.send(g.memset(negb[:, :, :], 0.0))
            V.send(g.memset(sel3[:, :], 0.0))
            V.send(g.memset(epsc[:, :], EPS))
            V.link(g.memset(zero[:, :], 0.0))
            for m_, cmp, fill, b0 in ((ident, ALU.not_equal, 1.0, 0), (identb, ALU.not_equal, 1.0, 0),
                                      (tri, ALU.is_ge, 0.0, 0), (stri, ALU.is_gt, 0.0, 0)):
                if cmp == ALU.not_equal:
                    V.send(g.affine_select(out=m_[:, :], in_=m_[:, :], compare_op=cmp, fill=fill, base=b0,
                                           pattern=[[-1, P]], channel_multiplier=1))
                else:
                    V.send(g.affine_select(out=m_[:, :], in_=m_[:, :], compare_op=cmp, fill=fill, base=b0,
                                           pattern=[[1, P]], channel_multiplier=-1))
            V.send(g.affine_select(out=negb[:, :, :], in_=negb[:, :, :], compare_op=ALU.is_ge, fill=-BIG, base=0,
                                   pattern=[[0, SC], [1, P]], channel_multiplier=-1))
            for k in range(3):
                V.settle()
                V.send(g.affine_select(out=sel3[:, :], in_=sel3[:, :], compare_op=ALU.not_equal, fill=1.0, base=-SH * k,
                                       pattern=[[-1, SH]], channel_multiplier=1))
            V.link(g.memset(zero[:, :], 0.0), s("const_ready"))
            V.link(g.memset(zrow[:, :], 0.0))
            for b in range(8):
                pool.dma_start(ydram[NE * BK + 120 * b:NE * BK + 120 * b + 120, :], zrow[0:120, :]).then_inc(
                    s("y_cleared"), 16)
            step = 0
            for gi, G in enumerate(groups):
                if G["kind"] in ("y_only", "y_last"):
                    j = G["j"]
                    if j == 3:
                        step += 1
                        continue
                    pool.wait_ge(s("ysq_ready"), 4 * step + j + 1)
                    if j == 0:
                        V.link(g.tensor_tensor(ssq[:, :], sqt[:, 0, :], sqt[:, 1, :], ALU.add), s("ssq_ready"))
                    else:
                        V.link(g.tensor_tensor(ssq[:, :], ssq[:, :], sqt[:, 0, :], ALU.add))
                        V.link(g.tensor_tensor(ssq[:, :], ssq[:, :], sqt[:, 1, :], ALU.add), s("ssq_ready"))
                if gi == first["gm_v"]:
                    pool.wait_ge(s("xsum_ready"), 5)
                    pool.dma_start(lng[:, :], I["gm_ln_g_2"][0].partition_broadcast(P)).then_inc(s("gm_in"), 16)
                    pool.dma_start(lnb[:, :], I["gm_ln_b_2"][0].partition_broadcast(P)).then_inc(s("gm_in"), 16)
                    pool.dma_start(wsp[:, :, :], I["gm_w_sp_2"][0].rearrange("g t s -> t g s")).then_inc(s("gm_in"), 16)
                    for hf in range(2):
                        pool.dma_start(bsp[64 * hf:64 * hf + 64, :, :], I["gm_b_sp_2"][0].rearrange(
                            "(i h) t -> h i t", h=2)[hf].partition_broadcast(64)).then_inc(s("gm_in"), 16)
                    V.send(g.memset(am_hi[:, :], 0.0))
                    V.send(g.memset(reset[:, :], 1.0))
                    V.settle()
                    for c in range(T // HC):
                        V.send(g.memset(reset[:, HC * c:HC * c + 1], 0.0))
                    for b in range(2):
                        V.link(g.memset(am_hi[HC * b:HC * b + HC, HC * b:HC * b + HC], 3.0e38))
                    V.link(g.affine_select(out=am_hi[:, :], in_=am_hi[:, :], compare_op=ALU.is_ge, fill=0.0, base=0,
                                           pattern=[[1, P]], channel_multiplier=-1))
                    V.link(g.tensor_scalar(am_lo[:, :], am_hi[:, :], -1.0, None, ALU.mult), s("bounds_ready"))
            pool.wait_ge(s("xsum_ready"), 6)
            V.send(g.iota(iot, pattern=[[1, BK]], base=0, channel_multiplier=0))
            V.send(g.iota(tokid, pattern=[[P, TT]], base=0, channel_multiplier=1))
            V.settle()
            V.send(g.tensor_copy(io64, iot))
            V.send(g.tensor_copy(tokf, tokid))
            V.settle()
            V.link(g.tensor_scalar(thr, io64[:, 0:8], float(BK), None, ALU.mult), s("iota_ready"))
            pool.wait_ge(s("idx_ready"), 1)
            pool.wait_ge(s("hrow_out0"), 32)
            pool.wait_ge(s("hrow_out1"), 32)

            def gather(e, b, sem):
                V.link(g.tensor_copy(ic[0:BK, b:b + 1], idx[0:BK, bass.ds(e, 1)]))
                g.indirect_dma_start(out=xg[:, b, :], out_offset=None, in_=hdram,
                                     in_offset=bass.IndirectOffsetOnAxis(ap=ic[0:BK, b:b + 1], axis=0)).then_inc(sem, 16)

            for b in range(2):
                gather(b, b, s(f"xg_in{b}"))
            with pool.Fori(1, NE // 2) as it:
                for b in range(2):
                    e = 2 * it + b
                    pool.wait_ge(s("e_turned"), e - 1)
                    g.tensor_copy(ic[0:BK, b:b + 1], idx[0:BK, bass.ds(e, 1)]).then_inc(s("ic_ready"), 1)
                    pool.wait_ge(s("ic_ready"), e - 1)
                    g.tensor_tensor(spare[:, :], zero[:, :], zero[:, :], ALU.add)
                    g.indirect_dma_start(out=xg[:, b, :], out_offset=None, in_=hdram, in_offset=bass.IndirectOffsetOnAxis(
                        ap=ic[0:BK, b:b + 1], axis=0)).then_inc(s(f"xg_in{b}"), 16)
            pool.wait_ge(s("table_ready"), 1)
            nov = pool.value_load(ovt[0:1, OVB:OVB + 1], min_val=0, max_val=OVB)

            def block_tokens(j):
                pool.wait_ge(s("e_turned"), NE + j)
                g.tensor_copy(ic[0:BK, 0:1], idx[0:BK, bass.ds(NE + j, 1)]).then_inc(s("ic_ready"), 1)
                pool.wait_ge(s("ic_ready"), NE - 1 + j)
                g.tensor_tensor(spare[:, :], zero[:, :], zero[:, :], ALU.add)
                g.indirect_dma_start(out=xg[:, 0, :], out_offset=None, in_=hdram, in_offset=bass.IndirectOffsetOnAxis(
                    ap=ic[0:BK, 0:1], axis=0)).then_inc(s("xg_in0"), 16)
            further_blocks(pool, nov, block_tokens)
            pool.wait_ge(s("rows_done"), 1)
            for t in range(TT):
                for k in range(2):
                    g.indirect_dma_start(out=yg[:, t, k, :], out_offset=None, in_=ydram,
                                         in_offset=bass.IndirectOffsetOnAxis(ap=slot_y[:, k, t:t + 1], axis=0)
                                         ).then_inc(s(f"yg_in{t}"), 16)

        @block.scalar
        def _(act):
            V = Stream(act, s("act"))
            A = nc.scalar.activation
            at_unit = [0]
            at_sub = [0]

            def advance(upto):
                upto = min(upto, len(groups) - 1) if phase[0] else min(upto, n_pre - 1)
                while at_unit[0] < len(units):
                    what, g, s0, s1 = units[at_unit[0]]
                    if what == "grp" and g > upto:
                        return
                    n = at_unit[0]
                    at_unit[0] += 1
                    if what == "ada":
                        continue
                    act.wait_ge(s(f"raw_in{n % 3}"), raw_at[n])
                    for a in range(s0, s1, 4):
                        z = min(a + 4, s1)
                        q = at_sub[0]
                        at_sub[0] += 1
                        if q >= 4:
                            act.wait_ge(s("subs_done"), q - 3)
                        V.send(A(w_hi[:, q % 4, 0:z - a, :], raw[:, n % 3, a - s0:z - s0, :], ACT.Copy), s("hi_ready"))

            def ln_table():
                V.settle()
                V.send(A(spare_a[:, :], epsc[:, :], ACT.Ln))

            def rsqrt(out_, in_, scale, sem):
                V.link(A(out_, in_, ACT.Ln, bias=epsc[:, 0:1], scale=scale))
                V.send(A(out_, out_, ACT.Exp, scale=-0.5), sem)

            phase = [0]
            act.wait_ge(s("const_ready"), 1)
            act.wait_ge(s("cols_ready"), 1)
            V.send(A(sil[:, :], cols[:, C_COND:C_COND + DT], ACT.Silu), s("sil_ready"))

            def step(r):
                if 1 <= r <= 4:
                    ln_table()
                    act.wait_ge(s("ysum_ready"), r)
                    rsqrt(rstd[:, :], M[:, 3, :], 1.0 / D, s("rstd_y_ready"))
                ln_table()
                if r == 2:
                    act.wait_ge(s("ssd_in"), 80)
                    V.send(A(wdt_hi[:, :, :], wdt[:, :, :], ACT.Copy), s("wdt_hi_ready"))
                if r == 5:
                    act.wait_ge(*read_out(n_pre - 1))
                    act.wait_ge(*read_out(n_pre - 2))
                if r == 6:
                    act.wait_ge(s("pt_ready"), 1)
                for i in range(DT):
                    if r != 5:
                        act.wait_ge(s("x_new"), 8 * (r - (r > 5)) + (DT if r == 6 else i + 1))
                    V.send(A(y[:, i, :], x[:, i, :], ACT.Square), s("sq_ready"))
                act.wait_ge(s("xsum_ready"), r + 1)
                rsqrt(rstd[:, :], M[:, 3, :], 1.0 / D, s("rstd_x_ready"))
                if r in HSTEP:
                    for i in range(DT):
                        act.wait_ge(s("hf_ready"), 8 * HSTEP[r] + i + 1)
                        if r < 4:
                            V.send(A(h_hi[:, i, :], y[:, i, :], ACT.Identity, bias=mod[:, 24 * r + i:24 * r + i + 1]),
                                   s("h_hi_ready"))
                        else:
                            V.send(A(h_hi[:, i, :], y[:, i, :], ACT.Copy), s("h_hi_ready"))

            advance(0)
            step(0)
            advance(1)
            n_ysq = n_mhi = n_first = 0

            def mid_high(G, g, src, dst):
                nonlocal n_mhi
                act.wait_ge(*read_out(g))
                V.send(A(dst, src, ACT.Copy), s("mid_hi_ready"))

            def ssd_head():
                V.send(A(ahead[:, :], ahead[:, :], ACT.Exp), s("aexp_ready"))
                act.wait_ge(s("sp_ready"), 1)
                V.send(A(sp[:, 1, :], sp[:, 1, :], ACT.Exp, scale=-1.0), s("aexp_ready"))

            def ssd_head_decays():
                act.wait_ge(s("cs_ready"), 1)
                csf = M[:, 1, 0:P]
                V.link(A(ctot[:, :, :], M[:, 1, P:2 * P].rearrange("p (c h) -> p c h", h=SH), ACT.Exp))
                V.send(A(ncs[:, :, :], csf.rearrange("p (c h) -> p c h", h=SH), ACT.Copy, scale=-1.0), s("ncs_ready"))
                act.wait_ge(s("dtex_ready"), 1)
                V.send(A(dte[:, :, :], dte[:, :, :], ACT.Exp), s("ncs_ready"))

            def ssd_a(n):
                act.wait_ge(s("ssd_turned2"), n + 1)
                V.send(A(btok[:, :, :], M[:, 2, :].rearrange("p (c n) -> p c n", n=P), ACT.Copy), s("bt_ready"))
                V.send(A(cbt[:, :, :], M[:, 3, :].rearrange("p (c n) -> p c n", n=P), ACT.Copy), s("bt_ready"))

            def ssd_exp(n, r):
                act.wait_ge(s("csb_ready"), 4 * n + r + 1)
                h = 4 * n + r
                for c in range(SC):
                    V.send(A(dec[:, r % 2, c, :], M[:, r % 2, P * c:P * c + P], ACT.Exp, bias=ncs[:, c, h:h + 1]),
                           s("dec_ready"))

            def ssd_silu(n, buf, c0, c1, k):
                act.wait_ge(s("conv_ready"), 2 * n + k + 1)
                for i, c in enumerate((c0, c1)):
                    V.send(A(buf[:, i, :], buf[:, i, :], ACT.Silu, bias=cols[:, C_MCONVB + c:C_MCONVB + c + 1]),
                           s("xbc_ready"))

            def ssd_ecs(n):
                act.wait_ge(s("ecs_ready"), n + 1)
                V.send(A(yy[n % 4][:, :, :], M[:, 0:2, :], ACT.Exp), s("yy_ready"))

            def ssd_square(n):
                act.wait_ge(s("yg_ready"), n + 1)
                V.send(A(yq[n % 4][:, :, :], yy[n % 4][:, :, :], ACT.Square), s("ygsq_ready"))

            def ssd_norm(n):
                ln_table()
                act.wait_ge(s("yg_summed"), n + 1)
                rsqrt(rstd[:, :], M[:, 2, :], 1.0 / 256, s("yg_rstd"))

            def ssd_high(n):
                act.wait_ge(s("yn_ready"), n + 1)
                V.send(A(mid_hi[:, 2 * (n % 4):2 * (n % 4) + 2, :], yy[n % 4][:, :, :], ACT.Copy), s("mid_hi_ready"))

            def hg_chain(jp):
                act.wait_ge(s("hf_f"), jp + 1)
                V.send(A(fk[:, :, :], fk[:, :, :], ACT.Ln), s("lnf_ready"))
                act.wait_ge(s("bcum_ready"), jp + 1)
                V.send(A(fk[:, :, :], bcum[:, :, :], ACT.Exp), s("eb_ready"))
                act.wait_ge(s("qd_ready"), jp + 1)
                V.send(A(fk[:, :, :], bcum[:, :, :], ACT.Exp, scale=-1.0), s("enb_ready"))
                V.send(A(dlast[:, :, :], bcum[:, :, :].rearrange("p a (c t) -> p a c t", t=HC)[:, :, :, HC - 1], ACT.Exp),
                       s("dlast_ready"))
                act.wait_ge(s("kx_ready"), jp + 1)
                V.send(A(kx[:, :, :], kx[:, :, :], ACT.Exp), s("kxe_ready"))

            def hg_k1(n):
                act.wait_ge(s("hg_scores"), n + 1)
                V.send(A(ketok[:, :, :], M[:, 1, :].rearrange("p (b k) -> p b k", k=P), ACT.Copy), s("ketok_ready"))

            def hg_k3(n):
                act.wait_ge(s("hg_out"), n + 1)
                V.send(A(hsq[:, :], M[:, 0, :], ACT.Square), s("osq_ready"))
                act.wait_ge(s("osum_ready"), n + 1)
                rsqrt(rstd[:, :], M[:, 1, :], 1.0 / P, s("orstd_ready"))
                act.wait_ge(s("on_ready"), n + 1)
                V.send(A(yb_hi[:, n, :], o_n[:, n, :], ACT.Copy), s("yb_hi_ready"))

            def expert_high(u, slot, par_slot, arrived, done):
                act.wait_ge(s(f"e_in{slot}"), arrived)
                if done is not None:
                    act.wait_ge(s("e_units"), done)
                A(ew_hi[:, par_slot, :, :], eraw[:, slot, :, :], ACT.Copy).then_inc(s("ehi_ready"), 1)

            def x_high(e, b):
                act.wait_ge(s("e_turned"), e + 1)
                A(xgT_hi[:, b, :, :], M[:, b, :].rearrange("p (k t) -> p k t", t=BK), ACT.Copy).then_inc(s("e_xhi"), 1)

            def expert_silu(e, b, done):
                act.wait_ge(s("e_units"), done)
                A(esg[:, b, :], M[0:BK, 2, :], ACT.Silu).then_inc(s("e_sg"), 1)

            def act_high(e, b):
                act.wait_ge(s("e_aturned"), e + 1)
                A(a_hi[:, b, :, :], pj[:, 0, 0:4 * BK].rearrange("p (k t) -> p k t", t=BK), ACT.Copy).then_inc(s("e_ahi"), 1)

            def expert_rows(e, b, row, done, store_sem, stored):
                act.wait_ge(s("e_units"), done)
                if stored is not None:
                    act.wait_ge(store_sem, stored)
                A(ytok[:, b, :], pj[0:BK, 2:4, :].rearrange("p a b -> p (a b)"), ACT.Copy).then_inc(s("e_ytok"), 1)
                act.wait_ge(s("e_ytok"), e + 1)
                act.dma_start(ydram[row, :], ytok[:, b, :]).then_inc(store_sem, 16)

            def rows_of(e, b, stored):
                row = slice(BK * e, BK * e + BK) if isinstance(e, int) else bass.ds(e * BK, BK)
                expert_rows(e, b, row, unit_no(e + 2, 0), s(f"y_out{b}"), stored)

            def act_round(e, par, first_round):
                for v in range(6):
                    u = unit_no(e, v)
                    expert_high(u, raw_slot(1, v), split_slot(par, v), arrivals(e, v), u - 3)
                    if v == 1:
                        x_high(e, par)
                    if v == 3 and not first_round:
                        rows_of(e - 2, par, None if isinstance(e, int) and e < 4 else (e - par - 2) * 8)
                    if v == 5:
                        expert_silu(e, par, unit_no(e, 2))
                        act_high(e - 1, 1 - par)

            def act_moe():
                act.wait_ge(s("r_shift"), 1)
                V.send(A(t4, t4, ACT.Exp), s("r_exp"))
                for t in range(TT):
                    if t >= 2:
                        act.wait_ge(s(f"hrow_out{t % 2}"), 16)
                    act.wait_ge(s("h_turned"), t + 1)
                    V.link(A(htok[:, t % 2, :], pj[:, 2 * (t % 2):2 * (t % 2) + 2, :].rearrange("p a b -> p (a b)"),
                             ACT.Copy), s("htok_ready"))
                    act.dma_start(hdram[P * t:P * t + P, :], htok[:, t % 2, :]).then_inc(s(f"hrow_out{t % 2}"), 16)
                act.dma_start(ptok[:, :, :], I["p_2"][0, 0].rearrange("(t p) n -> p t n", p=P)).then_inc(s("p_in"), 16)
                act.wait_ge(s("r_shift"), 2)
                V.send(A(wex, wex, ACT.Exp), s("r_exp"))
                act.wait_ge(s("hrow_out0"), 32)
                act.wait_ge(s("hrow_out1"), 32)

                for v in range(4):
                    expert_high(v, v, v, 16, None)
                x_high(0, 0)
                expert_silu(0, 0, 2)
                act_round(1, 1, True)
                act_round(2, 0, False)
                act_round(3, 1, False)
                with act.Fori(2, NE // 2) as it:
                    for b in range(2):
                        act_round(2 * it + b, b, False)
                for v in range(2):
                    u = unit_no(NE, v)
                    expert_high(u, raw_slot(1, v), split_slot(0, v), arrivals(NE, v), u - 3)
                rows_of(NE - 2, 0, 16 * (NE // 2 - 1))
                act_high(NE - 1, 1)
                expert_rows(NE - 1, 1, slice(BK * (NE - 1), BK * NE), 6 * NE, s("y_out1"), 16 * (NE // 2 - 1))
                for b in range(2):
                    act.wait_ge(s(f"y_out{b}"), 8 * NE)
                act.wait_ge(s("table_ready"), 1)
                nov = act.value_load(ovt[0:1, OVB:OVB + 1], min_val=0, max_val=OVB)

                def block(jj):
                    n, u = NE + jj, 6 * NE + 6 * jj
                    x_high(n, 0)
                    for v in range(6):
                        expert_high(u + v, v, v % 4, 16 * (NE + 1) + 16 * jj, u if v < 4 else u + v - 3)
                    expert_silu(n, 0, u + 2)
                    act_high(n, 0)
                    expert_rows(n, 0, bass.ds(n * BK, BK), u + 6, s("y_out0"), 8 * NE + 16 * jj)
                further_blocks(act, nov, block)
                act.wait_ge(s("y_out0"), 8 * NE + 16 * nov)
                V.link(A(esg[:, 0, 0:1], zero[0:BK, 0:1], ACT.Copy), s("rows_done"))
                act.wait_ge(s("pT_ready"), 1)
                V.send(A(pt_hi[:, :, :], pT[:, :, :], ACT.Copy), s("pt_hi_ready"))

            for g, G in enumerate(groups):
                k, j = G["kind"], G["j"]
                done = (s("subs_done"), G["end"])
                banks = pj2(g)
                free = read_out(g)
                if k == "conv_c":
                    if j:
                        act.wait_ge(*read_out(g - 2))
                    act.wait_ge(*done)
                    V.send(A(cgate[:, :, :], banks, ACT.Copy), free)
                elif k == "conv_b":
                    mid_high(G, g, cu[:, :, :], mid_hi[:, 2 * j:2 * j + 2, :])
                elif k in ("y_only", "y_last"):
                    if j:
                        act.wait_ge(s("ssq_ready"), n_ysq // 4 * 3 + j)
                    act.wait_ge(*read_out(g))
                    V.send(A(sqt[:, :, :], y[:, 2 * j:2 * j + 2, :], ACT.Square), s("ysq_ready"))
                    n_ysq += 1
                elif k == "y_first":
                    act.wait_ge(*done)
                    V.send(A(y[:, 2 * j:2 * j + 2, :], banks, ACT.Copy), free)
                elif k == "ffn_g":
                    if j:
                        act.wait_ge(*read_out(g - 1))
                    act.wait_ge(*done)
                    V.send(A(sg[:, :, :], banks, ACT.Silu), free)
                elif k == "ffn_u":
                    mid_high(G, g, tmp[:, :, :], mid_hi[:, 2 * j:2 * j + 2, :])
                elif k == "ssd_x":
                    n = j - 1
                    if j == 0:
                        ssd_head()
                    if n >= 0:
                        if n:
                            ssd_norm(n - 1)
                        ssd_exp(n, 0)
                        ssd_exp(n, 1)
                        ssd_a(n)
                        if n:
                            ssd_high(n - 1)
                        act.wait_ge(s("conv_ready"), 2 * n + 2)
                    act.wait_ge(*done)
                    V.send(A(pre[:, :, 3:], banks, ACT.Copy), free)
                elif k == "ssd_bc":
                    n = j - 1
                    if n >= 0:
                        ssd_exp(n, 2)
                        ssd_exp(n, 3)
                    ssd_silu(j, xs[j % 2], 2 * j, 2 * j + 1, 0)
                    act.wait_ge(*done)
                    V.send(A(pre[:, :, 3:], banks, ACT.Copy), free)
                    if j == 0:
                        advance(g + 2)
                        ssd_head_decays()
                elif k == "ssd_z":
                    n = j - 1
                    if n >= 0:
                        ssd_ecs(n)
                        ssd_square(n)
                    act.wait_ge(*done)
                    V.send(A(sz[:, :, :], banks, ACT.Silu), free)
                    advance(g + 2)
                    ssd_silu(j, bct[j % 2], 16 + j, 24 + j, 1)
                    if j == SG - 1:
                        ssd_norm(n)
                        ssd_exp(j, 0)
                        ssd_exp(j, 1)
                        ssd_a(j)
                        ssd_high(n)
                        ssd_exp(j, 2)
                        ssd_exp(j, 3)
                        ssd_ecs(j)
                        ssd_square(j)
                        ssd_norm(j)
                        ssd_high(j)
                elif k == "gm_v":
                    act.wait_ge(*done)
                    V.send(A(vn[:, :, 256 * j:256 * j + 256], pjt(g), ACT.Gelu_apprx_tanh), free)
                elif k == "gm_u":
                    act.wait_ge(*done)
                    V.send(A(uact[:, 2 * j:2 * j + 2, :], banks, ACT.Gelu_apprx_tanh), free)
                    if j == 1:
                        advance(g + 2)
                        act.wait_ge(s("bna_ready"), 1)
                        V.link(A(bna[:, :, 1], bna[:, :, 1], ACT.Ln, bias=epsc[:, 0:1]))
                        V.send(A(bna[:, :, 1], bna[:, :, 1], ACT.Exp, scale=-0.5), s("lnr_ready"))
                        act.wait_ge(s("bna_ready"), 2)
                        V.send(A(lbt[:, 0:2, :], lbt[:, 0:2, :], ACT.Exp), s("lnr_ready"))
                elif k == "hg_i":
                    act.wait_ge(*done)
                    V.send(A(vtok[:, :, 256 * j:256 * j + 256], pjt(g), ACT.Copy), free)
                    if j == 1:
                        advance(g + 2)
                        for p in range(2):
                            act.wait_ge(s("gm_y"), p + 1)
                            V.send(A(ya_hi[:, 2 * p:2 * p + 2, :], uact[:, 2 * p:2 * p + 2, :], ACT.Copy),
                                   s("ya_hi_ready"))
                elif k == "hg_f":
                    act.wait_ge(*done)
                    if j == 1:
                        hg_k1(1)
                    V.send(A(fk[:, :, :], banks, ACT.Sigmoid), free)
                    if j == 1:
                        advance(g + 2)
                        hg_k3(1)
                elif k == "hg_q":
                    act.wait_ge(*done)
                    V.send(A(qd[:, :, :], banks, ACT.Silu), free)
                    advance(g + 2)
                    hg_chain(j)
                elif k == "hg_og":
                    act.wait_ge(*done)
                    V.send(A(sog[:, 2 * j:2 * j + 2, :], banks, ACT.Sigmoid), free)
                    if j == 0:
                        hg_k1(0)
                    else:
                        advance(g + 2)
                        hg_k3(0)
                elif k == "gate_a":
                    if j >= 2:
                        act.wait_ge(*read_out(group_no["up_b", 2 if j == 3 else 0]))
                    act.wait_ge(*done)
                    V.send(A(gate_of(j), banks, ACT.Sigmoid), free)
                    if j == 1:
                        advance(g + 2)
                        hg_k3(2)
                elif k == "up_a":
                    if j < 2:
                        advance(g + 2)
                        hg_k1(2 + j)
                elif k == "gate_b":
                    if j:
                        act.wait_ge(s("mid_ready"), groups[group_no["up_b", j - 1]]["pair"] + 1)
                    act.wait_ge(*done)
                    V.send(A(sgb[:, :, :], banks, ACT.Sigmoid), free)
                    if j == 0:
                        advance(g + 2)
                        hg_k3(3)
                elif k == "up_b":
                    mid_high(G, g, sgb[:, :, :], m2_hi[:, 2 * j:2 * j + 2, :])
                elif k == "pg":
                    if j:
                        act.wait_ge(*read_out(g - 1))
                    act.wait_ge(*done)
                    V.send(A(sg[:, :, :], banks, ACT.Sigmoid), free)
                if g in step_after:
                    step(step_after[g])
                    if step_after[g] == 5:
                        act_moe()
                        phase[0] = 1
                        advance(g + 2)
                        step(6)
                        continue
                advance(g + 2)
            step(7)
            for t in range(1, TT, 2):
                act.wait_ge(s("o_turned"), t + 1)
                V.send(A(otok[:, t, :], pj[:, 2:4, :].rearrange("p a b -> p (a b)"), ACT.Copy), s("otok_odd"))

        @block.vector
        def _(dve):
            V = Stream(dve, s("dve"))
            v = nc.vector
            TS, TN, STT = v.tensor_scalar, v.tensor_tensor, v.scalar_tensor_tensor
            at_unit, at_sub, phase = [0], [0], [0]

            def advance(upto):
                upto = min(upto, len(groups) - 1) if phase[0] else min(upto, n_pre - 1)
                while at_unit[0] < len(units):
                    what, g, s0, s1 = units[at_unit[0]]
                    if what == "grp" and g > upto:
                        return
                    n = at_unit[0]
                    at_unit[0] += 1
                    if what == "ada":
                        u = g
                        dve.wait_ge(s(f"raw_in{n % 3}"), raw_at[n])
                        if u == 0:
                            dve.wait_ge(s("sil_ready"), 1)
                        if u >= 2:
                            dve.wait_ge(s("ada_summed"), u - 1)
                        a = acc[:, u % 2, :]
                        V.link(TS(a, raw[:, n % 3, 0, :], sil[:, 0:1], None, ALU.mult))
                        for k in range(1, DT):
                            V.link(STT(a, raw[:, n % 3, k, :], sil[:, k:k + 1], a, ALU.mult, ALU.add),
                                   s("ada_acc") if k == DT - 1 else None)
                        continue
                    for b in range(s0, s1, 4):
                        z = min(b + 4, s1)
                        q = at_sub[0]
                        at_sub[0] += 1
                        dve.wait_ge(s("hi_ready"), q + 1)
                        V.send(TN(w_lo[:, q % 4, 0:z - b, :], raw[:, n % 3, b - s0:z - s0, :],
                                  w_hi[:, q % 4, 0:z - b, :].bitcast(F32), ALU.subtract), s("lo_ready"))

            def coefficients(c):
                r, gate_part = c // 2, c % 2
                c0, n = 24 * r + 16 * gate_part, 8 if gate_part else 16
                dve.wait_ge(s("ada_summed"), (12 * r + 12) if gate_part else (12 * r + 8))
                V.link(TN(mod[:, c0:c0 + n], M[:, c % 3, c0:c0 + n], cols[:, C_ADAB + c0:C_ADAB + c0 + n], ALU.add),
                       s("coef_read"))
                ng = C_NG + 8 * (4 * (r // 2) + 2 * (r % 2))
                if gate_part:
                    V.link(TN(gco[:, r, :], mod[:, c0:c0 + 8], cols[:, ng + 8:ng + 16], ALU.mult))
                else:
                    V.link(STT(sco[:, r, :], mod[:, c0 + 8:c0 + 16], 1.0, cols[:, ng:ng + 8], ALU.add, ALU.mult))

            def step(r):
                if 1 <= r <= 4:
                    dve.wait_ge(s("rstd_y_ready"), r)
                    V.settle()
                    scaled = []
                    for i in range(DT + 1):
                        if i < DT:
                            V.send(TN(y[:, i, :], y[:, i, :], rstd[:, :], ALU.mult))
                            scaled.append(V.last)
                        if i:
                            dve.wait_ge(*scaled[i - 1])
                            V.send(STT(x[:, i - 1, :], y[:, i - 1, :], gco[:, r - 1, i - 1:i], x[:, i - 1, :],
                                       ALU.mult, ALU.add), s("x_new"))
                if r == 2:
                    dve.wait_ge(s("wdt_hi_ready"), 1)
                    V.send(TN(wdt_lo[:, :, :], wdt[:, :, :], wdt_hi[:, :, :].bitcast(F32), ALU.subtract), s("dt_low"))
                dve.wait_ge(s("rstd_x_ready"), r + 1)
                V.settle()
                scale = {0: sco[:, 0, :], 1: sco[:, 1, :], 2: sco[:, 2, :], 3: sco[:, 3, :],
                         4: cols[:, C_GMIX:C_GMIX + 8], 5: cols[:, C_GFFN:C_GFFN + 8], 6: cols[:, C_GPLE:C_GPLE + 8],
                         7: cols[:, C_GFIN:C_GFIN + 8]}[r]
                sem = s("hf_ready") if r in HSTEP else s("mh_ready") if r == 5 else s("fin_ready")

                def low(i):
                    dve.wait_ge(s("h_hi_ready"), 8 * HSTEP[r] + i + 1)
                    hi = h_hi[:, i, :].bitcast(F32)
                    V.send(STT(h_lo[:, i, :], y[:, i, :], mod[:, 24 * r + i:24 * r + i + 1], hi, ALU.add, ALU.subtract)
                           if r < 4 else TN(h_lo[:, i, :], y[:, i, :], hi, ALU.subtract), s("h_ready"))

                for i in range(DT):
                    V.send(STT(y[:, i, :], x[:, i, :], scale[:, i:i + 1], rstd[:, :], ALU.mult, ALU.mult), sem)
                    if i and r in HSTEP:
                        low(i - 1)
                if r in HSTEP:
                    low(DT - 1)

            n_mid = [0]

            def mid_low(src, dst, hi):
                n_mid[0] += 1
                dve.wait_ge(s("mid_hi_ready"), n_mid[0])
                V.send(TN(dst, src, hi.bitcast(F32), ALU.subtract), s("mid_ready"))

            dve.wait_ge(s("params_turned"), 1)
            V.link(v.tensor_copy(cols[:, :], M[:, 0, 0:C_END]), s("cols_ready"))
            for i in range(DT):
                dve.wait_ge(s("x_turned"), i + 1)
                V.send(v.tensor_copy(x[:, i, :], pj[:, i % 4, :]), s("x_new"))
            advance(0)
            coefficients(0)
            step(0)
            V.settle()
            V.send(v.memset(cv[:, :, 0:2], 0.0))
            advance(1)

            def conv4(n, k, dst):
                c0 = (2 * n, 2 * n + 1) if k == 0 else (16 + n, 24 + n)
                w = lambda tap, i: cols[:, C_MCONV + 32 * tap + c0[i]:C_MCONV + 32 * tap + c0[i] + 1]
                V.settle()
                for i in range(2):
                    V.send(TS(dst[:, i, :], pre[:, i, 0:T], w(0, i), None, ALU.mult))
                V.settle()
                for tap in (1, 2, 3):
                    for i in range(2):
                        V.send(STT(dst[:, i, :], pre[:, i, tap:tap + T], w(tap, i), dst[:, i, :], ALU.mult, ALU.add),
                               s("conv_ready") if (tap, i) == (3, 1) else None)
                    V.settle()

            def ssd_head():
                dve.wait_ge(s("dt_raw"), 1)
                V.settle()
                V.link(v.tensor_copy(dtr[:, :], M[0:SH, 0, :]), s("dt_low"))
                V.link(v.memset(pre[:, :, 0:3], 0.0))
                dve.wait_ge(s("dt_raw"), 2)
                z, e, w, q, r_, t_ = (sp[:, i, :] for i in range(6))
                v3 = lambda a: a.rearrange("p (c h) -> p c h", h=SH)
                V.link(TN(v3(z), M[:, 1, 0:P].rearrange("p (c h) -> p c h", h=SH),
                          dtb[:, :].unsqueeze(1).broadcast_to((P, SC, SH)), ALU.add))
                V.link(STT(e, z, -1.0, z, ALU.mult, ALU.max), s("sp_ready"))
                dve.wait_ge(s("aexp_ready"), 2)
                V.link(TS(w, e, 2.0, None, ALU.add))
                V.link(v.reciprocal(w, w))
                V.link(TN(w, w, e, ALU.mult))
                V.link(TN(q, w, w, ALU.mult))
                V.link(TS(r_, q, 1.0 / 17, 1.0 / 15, ALU.mult, ALU.add))
                for k in (13, 11, 9, 7, 5, 3, 1):
                    V.link(TN(r_, r_, q, ALU.mult))
                    V.link(TS(r_, r_, 1.0 / k, None, ALU.add))
                V.link(TN(r_, r_, w, ALU.mult))
                V.link(TS(t_, z, 0.0, None, ALU.max))
                V.link(STT(dt_t[:, :, :].rearrange("p c h -> p (c h)"), r_, 2.0, t_, ALU.mult, ALU.add))
                V.link(STT(dA[:, :, :], dt_t[:, :, :], -1.0, ahead[:, :].unsqueeze(1).broadcast_to((P, SC, SH)),
                           ALU.mult, ALU.mult), s("sp_ready"))

            def ssd_head_decays():
                dve.wait_ge(s("cs_ready"), 1)
                dve.wait_ge(s("ncs_ready"), 1)
                V.link(TN(dte[:, :, :], ncs[:, :, :], M[:, 1, P:2 * P].rearrange("p (c h) -> p c h", h=SH), ALU.add),
                       s("dtex_ready"))
                m2 = M[:, 2, :]
                V.link(v.tensor_copy(csr[:, :], m2[0:3 * SH, :]))
                V.link(TN(csx[:, :], m2[0:3 * SH, :], csr[:, :], ALU.subtract))
                for k in (1, 2):
                    V.send(v.tensor_copy(csr[SH * k:SH * k + SH, :], csx[SH * k:SH * k + SH, :]))
                V.settle()
                r2 = slice(2 * SH, 3 * SH)
                V.link(TN(csx[r2, :], csx[r2, :], csr[r2, :], ALU.subtract))
                V.link(v.tensor_copy(csr[r2, :], csx[r2, :]), s("dtex_ready"))

            def heads4(a):
                return a.rearrange("p c (r n) -> p c r n", n=64)

            def ssd_xdt(n):
                dve.wait_ge(s("ssd_turned"), n + 1)
                if n == 0:
                    dve.wait_ge(s("ncs_ready"), 2)
                V.settle()
                for c in range(SC):
                    V.send(TN(xdt[:, c, :].rearrange("p (r n) -> p r n", n=64),
                              Mf[:, 256 * c:256 * c + 256].rearrange("p (r n) -> p r n", n=64),
                              dt_t[:, c, 4 * n:4 * n + 4].unsqueeze(2).broadcast_to((P, 4, 64)), ALU.mult))
                V.settle()
                for c in range(3):
                    V.send(TN(xdte[:, c, :].rearrange("p (r n) -> p r n", n=64),
                              xdt[:, c, :].rearrange("p (r n) -> p r n", n=64),
                              dte[:, c, 4 * n:4 * n + 4].unsqueeze(2).broadcast_to((P, 4, 64)), ALU.mult),
                           s("xdt_ready") if c == 2 else None)

            def ssd_scan(n):
                dve.wait_ge(s("ssd_states"), n + 1)
                V.settle()
                r4 = lambda a: a.rearrange("p (r n) -> p r n", n=64)
                V.link(v.tensor_copy(S[:, 0, :], M[:, 2, 0:256]))
                for c in (1, 2):
                    V.link(TN(r4(S[:, c, :]), r4(S[:, c - 1, :]),
                              ctot[:, c, 4 * n:4 * n + 4].unsqueeze(2).broadcast_to((P, 4, 64)), ALU.mult))
                    V.link(TN(S[:, c, :], S[:, c, :], M[:, 2, 256:512] if c == 1 else M[:, 3, 0:256], ALU.add),
                           s("S_ready") if c == 2 else None)

            def ssd_m(n, r):
                dve.wait_ge(s("dec_ready"), 16 * n + 4 * r + 4)
                V.send(TN(dec[:, r % 2, :, :], dec[:, r % 2, :, :], cbt[:, :, :], ALU.mult), s("m_ready"))

            def ssd_y(n):
                yk = yy[n % 4]
                dve.wait_ge(s("yy_ready"), n + 1)
                dve.wait_ge(s("ssd_yoff"), n + 1)
                V.settle()
                V.link(TN(yk[:, :, P:], yk[:, :, P:], M[:, 0:2, P:], ALU.mult))
                V.link(TN(yk[:, :, P:], yk[:, :, P:], M[:, 2:4, P:], ALU.add))
                V.link(v.tensor_copy(yk[:, :, 0:P], M[:, 2:4, 0:P]), s("y_banks_read"))
                for i in range(2):
                    V.send(STT(yk[:, i, :], xs[n % 2][:, i, :], dsk[:, 2 * n + i:2 * n + i + 1], yk[:, i, :],
                               ALU.mult, ALU.add))
                V.settle()
                V.link(TN(yk[:, :, :], yk[:, :, :], sz[:, :, :], ALU.mult), s("yg_ready"))

            def ssd_final(n):
                yk = yy[n % 4]
                dve.wait_ge(s("yg_rstd"), n + 1)
                V.settle()
                V.link(TN(yk[:, :, :], yk[:, :, :], rstd[:, :].unsqueeze(1).broadcast_to((P, 2, T)), ALU.mult))
                for i in range(2):
                    V.send(TS(yk[:, i, :], yk[:, i, :], cols[:, C_MNG + 2 * n + i:C_MNG + 2 * n + i + 1], None, ALU.mult),
                           s("yn_ready") if i else None)

            def ssd_low(n):
                p = 2 * (n % 4)
                mid_low(yy[n % 4][:, :, :], mid_lo[:, p:p + 2, :], mid_hi[:, p:p + 2, :])

            def layernorm_v():
                V.settle()
                for t in range(TT):
                    V.send(v.bn_stats(bns[:, t, :], vn[:, t, :]))
                V.settle()
                for t in range(TT):
                    V.send(v.bn_aggr(bna[:, t, :], bns[:, t, :]), s("bna_ready") if t == TT - 1 else None)
                V.settle()
                c = cols[:, C_LB:C_LB + 8].rearrange("p (a j) -> p a j", j=4)
                V.link(TN(lbt[:, 2, :], c[:, 0, :], c[:, 1, :], ALU.max))
                V.link(TN(lbt[:, 0:2, :], c, lbt[:, 2, :].unsqueeze(1).broadcast_to((P, 2, 4)), ALU.subtract),
                       s("bna_ready"))
                dve.wait_ge(s("lnr_ready"), 2)
                V.link(TN(lbt[:, 2, :], lbt[:, 0, :], lbt[:, 1, :], ALU.add))
                V.link(v.reciprocal(lbt[:, 2, :], lbt[:, 2, :]))
                V.link(TN(lbt[:, 0, :], lbt[:, 0, :], lbt[:, 2, :], ALU.mult))
                V.link(TS(lbt[:, 1, :], lbt[:, 0, :], -1.0, 1.0, ALU.mult, ALU.add))
                for t in range(TT):
                    V.send(TS(vn[:, t, :], vn[:, t, :], bna[:, t, 0:1], bna[:, t, 1:2], ALU.subtract, ALU.mult))
                dve.wait_ge(s("gm_in"), 80)
                V.settle()
                V.link(TN(vn[:, :, :], vn[:, :, :], lng[:, :].unsqueeze(1).broadcast_to((P, TT, GW)), ALU.mult))
                V.link(TN(vn[:, :, :], vn[:, :, :], lnb[:, :].unsqueeze(1).broadcast_to((P, TT, GW)), ALU.add))
                dve.wait_ge(s("wsp_turned"), 1)
                V.link(TN(wspT[:, :, :], Mf[:, 0:1024].rearrange("p (g t) -> p g t", t=P),
                          tri[:, :].unsqueeze(1).broadcast_to((P, 8, P)), ALU.mult), s("gm_ready"))

            def gmlp_out():
                dve.wait_ge(s("gm_mixed"), 1)
                V.settle()
                for i in range(4):
                    V.link(TN(hsq[:, :].rearrange("p (c t) -> p c t", t=P), M[:, i, :].rearrange("p (c t) -> p c t", t=P),
                              bsp[:, i, :].unsqueeze(1).broadcast_to((P, TT, P)), ALU.add))
                    V.link(TN(uact[:, i, :], hsq[:, :], uact[:, i, :], ALU.mult), s("gm_y") if i % 2 else None)
                for p in range(2):
                    dve.wait_ge(s("ya_hi_ready"), p + 1)
                    V.send(TN(ya_lo[:, 2 * p:2 * p + 2, :], uact[:, 2 * p:2 * p + 2, :],
                              ya_hi[:, 2 * p:2 * p + 2, :].bitcast(F32), ALU.subtract), s("ya_ready"))

            def hg_f(jp, g):
                dve.wait_ge(*read_out(g))
                V.settle()
                for i in range(2):
                    h = 2 * jp + i
                    V.send(TS(fk[:, i, :], fk[:, i, :], lbt[:, 1, h:h + 1], lbt[:, 0, h:h + 1], ALU.mult, ALU.add))
                V.settle()
                V.link(TS(ke[:, :, :], fk[:, :, :], -1.0, 1.0, ALU.mult, ALU.add), s("hf_f"))

            def hg_chain(jp, g):
                dve.wait_ge(s("lnf_ready"), jp + 1)
                dve.wait_ge(s("bounds_ready"), 1)
                V.settle()
                for i in range(2):
                    V.link(v.tensor_tensor_scan(bcum[:, i, :], reset[:, :], fk[:, i, :], 0.0, ALU.mult, ALU.add),
                           s("bcum_ready") if i else None)
                dve.wait_ge(s("eb_ready"), jp + 1)
                dve.wait_ge(*read_out(g))
                V.link(TN(qd[:, :, :], qd[:, :, :], fk[:, :, :], ALU.mult), s("qd_ready"))
                ch = lambda a: a.rearrange("p (c t) -> p c t", t=HC)
                for i in range(2):
                    last = ch(bcum[:, i, :])[:, :, HC - 1:HC].broadcast_to((P, T // HC, HC))
                    V.send(TN(ch(kx[:, i, :]), last, ch(bcum[:, i, :]), ALU.subtract), s("kx_ready") if i else None)
                dve.wait_ge(s("enb_ready"), jp + 1)
                V.settle()
                V.link(TN(fk[:, :, :], ke[:, :, :], fk[:, :, :], ALU.mult))
                dve.wait_ge(s("kxe_ready"), jp + 1)
                V.link(TN(ke[:, :, :], ke[:, :, :], kx[:, :, :], ALU.mult), s("hg_ops_ready"))

            def hg_head(n):
                dve.wait_ge(s("hg_scores"), n + 1)
                V.settle()
                sc = M[:, 0, :].rearrange("p (b t) -> p b t", t=P)
                V.link(TN(att[:, :, :], sc, am_hi[:, :].unsqueeze(1).broadcast_to((P, TT, P)), ALU.min))
                V.link(TN(att[:, :, :], att[:, :, :], am_lo[:, :].unsqueeze(1).broadcast_to((P, TT, P)), ALU.max),
                       s("att_ready"))
                dve.wait_ge(s("hg_dS"), n + 1)
                dve.wait_ge(s("dlast_ready"), n // 2 + 1)
                for c in range(7):
                    d = M[:, 2 + c % 2, P * (c // 2):P * (c // 2) + P]
                    if c == 0:
                        V.link(v.tensor_copy(HS[:, 0, :], d))
                    else:
                        V.link(STT(HS[:, c, :], HS[:, c - 1, :], dlast[:, n % 2, c:c + 1], d, ALU.mult, ALU.add),
                               s("HS_ready") if c == 6 else None)

            def hg_head_out(n):
                dve.wait_ge(s("orstd_ready"), n + 1)
                V.settle()
                V.link(TN(o_n[:, n, :], M[:, 0, :], rstd[:, :], ALU.mult))
                dve.wait_ge(*read_out(first["hg_og"] + 1))
                V.link(STT(o_n[:, n, :], o_n[:, n, :], cols[:, C_HGN + n:C_HGN + n + 1], sog[:, n, :],
                           ALU.mult, ALU.mult), s("on_ready"))
                dve.wait_ge(s("yb_hi_ready"), n + 1)
                V.send(TN(yb_lo[:, n, :], o_n[:, n, :], yb_hi[:, n, :].bitcast(F32), ALU.subtract), s("yb_ready"))

            def expert_low(u, slot, par_slot):
                dve.wait_ge(s("ehi_ready"), u + 1)
                TN(ew_lo[:, par_slot, :, :], eraw[:, slot, :, :], ew_hi[:, par_slot, :, :].bitcast(F32),
                   ALU.subtract).then_inc(s("elo_ready"), 1)

            def x_low(e, b):
                dve.wait_ge(s("e_xhi"), e + 1)
                TN(xgT_lo[:, b, :, :], M[:, b, :].rearrange("p (k t) -> p k t", t=BK), xgT_hi[:, b, :, :].bitcast(F32),
                   ALU.subtract).then_inc(s("e_xlo"), 1)

            def expert_act(e, b, done):
                dve.wait_ge(s("e_units"), done)
                dve.wait_ge(s("e_sg"), e + 1)
                TN(eact[:, b, :], esg[:, b, :], M[0:BK, 3, :], ALU.mult).then_inc(s("e_act"), 1)

            def act_low(e, b):
                dve.wait_ge(s("e_ahi"), e + 1)
                TN(a_lo[:, b, :, :], pj[:, 0, 0:4 * BK].rearrange("p (k t) -> p k t", t=BK), a_hi[:, b, :, :].bitcast(F32),
                   ALU.subtract).then_inc(s("e_alo"), 1)

            def dve_round(e, par, w3_done):
                for v in range(6):
                    expert_low(unit_no(e, v), raw_slot(1, v), split_slot(par, v))
                    if v == 1:
                        x_low(e, par)
                        expert_act(e - 1, 1 - par, w3_done)
                act_low(e - 1, 1 - par)

            def one_hot_first(dst, src, mxv, n, ix, io):
                b3 = lambda a: a.unsqueeze(2).broadcast_to((P, TT, n))
                i3 = io[:, 0:n].unsqueeze(1).broadcast_to((P, TT, n))
                V.link(TN(dst, src, b3(mxv), ALU.is_lt))
                V.link(STT(dst, dst, BIG, i3, ALU.mult, ALU.add))
                V.link(v.tensor_reduce(ix, dst, AX, ALU.min))
                V.link(TN(dst, i3, b3(ix), ALU.is_equal))

            def dve_moe():
                b3 = lambda a, n: a.unsqueeze(2).broadcast_to((P, TT, n))
                dve.wait_ge(s("logit_rows"), 1)
                V.settle()
                V.link(v.tensor_copy(lgs[:, :], M[0:36, 1, :]), s("lgs_ready"))
                dve.wait_ge(s("logits"), 1)
                dve.wait_ge(s("iota_ready"), 1)
                V.settle()
                V.link(v.tensor_copy(L, M[:, 0, 0:TT * 36].rearrange("p (t n) -> p t n", n=36)))
                V.link(v.tensor_reduce(gmx, L[:, :, 0:4], AX, ALU.max))
                V.link(TN(t4, L[:, :, 0:4], b3(gmx, 4), ALU.subtract), s("r_shift"))
                V.link(TN(ghot, L[:, :, 0:4], b3(gmx, 4), ALU.is_lt))
                i3 = io32[:, 0:4].unsqueeze(1).broadcast_to((P, TT, 4))
                V.link(STT(ghot, ghot, BIG, i3, ALU.mult, ALU.add))
                V.link(v.tensor_reduce(gix, ghot, AX, ALU.min))
                V.link(TN(ghot, i3, b3(gix, 4), ALU.is_equal))
                dve.wait_ge(s("r_exp"), 1)
                V.link(v.tensor_reduce(gse, t4, AX, ALU.add))
                V.link(v.reciprocal(gpg, gse))
                V.link(TN(sel, L[:, :, 4:12], b3(ghot[:, :, 0], 8), ALU.mult))
                for q in range(1, 4):
                    V.link(TN(t8, L[:, :, 4 + 8 * q:12 + 8 * q], b3(ghot[:, :, q], 8), ALU.mult))
                    V.link(TN(sel, sel, t8, ALU.add))
                V.link(v.tensor_reduce(mx[:, 0, :], sel, AX, ALU.max))
                one_hot_first(t8, sel, mx[:, 0, :], 8, eix[:, 0, :], io32)
                V.link(STT(sel2, t8, -BIG, sel, ALU.mult, ALU.add))
                V.link(v.tensor_reduce(mx[:, 1, :], sel2, AX, ALU.max))
                one_hot_first(t8, sel2, mx[:, 1, :], 8, eix[:, 1, :], io32)
                V.link(TN(wex, mx[:, 1, :], mx[:, 0, :], ALU.subtract), s("r_shift"))
                for k in range(2):
                    V.link(STT(eix[:, k, :], gix, 8.0, eix[:, k, :], ALU.mult, ALU.add))
                    V.link(TN(Ak[k], io32.unsqueeze(1).broadcast_to((P, TT, NE)), b3(eix[:, k, :], NE), ALU.is_equal))
                V.link(TN(Aall, Ak[0], Ak[1], ALU.add), s("chosen"))
                dve.wait_ge(s("ranks"), 1)
                V.link(v.tensor_copy(rank, M[:, 1, 0:TT * NE].rearrange("p (t n) -> p t n", n=NE)))
                V.link(v.tensor_copy(cnt, M[:, 2, 0:NE]))
                nq = T // BK - 1
                V.link(TN(cq, cnt.unsqueeze(2).broadcast_to((P, NE, nq)),
                          thr[:, 1:nq + 1].unsqueeze(1).broadcast_to((P, NE, nq)), ALU.is_gt))
                V.link(v.tensor_reduce(nbk, cq, AX, ALU.add))
                V.link(v.memset(t1, 1.0))
                V.link(v.tensor_tensor_scan(incl, t1, nbk, 0.0, ALU.mult, ALU.add))
                V.link(TN(obk, incl, nbk, ALU.subtract))
                for k in range(2):
                    V.link(TN(t32, Ak[k], rank, ALU.mult))
                    V.link(v.tensor_reduce(rk[:, k, :], t32, AX, ALU.add))
                    V.link(TN(t32, Ak[k], obk.unsqueeze(1).broadcast_to((P, TT, NE)), ALU.mult))
                    V.link(v.tensor_reduce(ok[:, k, :], t32, AX, ALU.add))
                V.link(TN(rq, rk8.unsqueeze(2).broadcast_to((P, 2 * TT, nq)),
                          thr[:, 1:nq + 1].unsqueeze(1).broadcast_to((P, 2 * TT, nq)), ALU.is_ge))
                V.link(v.tensor_reduce(qk8, rq, AX, ALU.add))
                V.link(STT(wk, qk, -float(BK), rk, ALU.mult, ALU.add))
                V.link(TN(bk, ok, qk, ALU.add))
                V.link(TS(bk, bk, float(NE - 1), None, ALU.add))
                V.link(TN(bk, bk, eix, ALU.subtract))
                V.link(TS(sk, qk, 0.0, None, ALU.is_gt))
                V.link(TN(bk, bk, sk, ALU.mult))
                V.link(TN(bk, bk, eix, ALU.add))
                V.link(TN(hot_w, wk8.unsqueeze(2).broadcast_to((P, 2 * TT, BK)),
                          io64.unsqueeze(1).broadcast_to((P, 2 * TT, BK)), ALU.is_equal))
                for k in range(2):
                    V.send(TN(hot_w[:, TT * k:TT * k + TT, :], hot_w[:, TT * k:TT * k + TT, :],
                              tokf.unsqueeze(2).broadcast_to((P, TT, BK)), ALU.mult))
                V.send(TN(hot_b, bk8.unsqueeze(2).broadcast_to((P, 2 * TT, NB)),
                          io64[:, 0:NB].unsqueeze(1).broadcast_to((P, 2 * TT, NB)), ALU.is_equal), s("slots_ready"))
                V.settle()
                V.link(STT(sk, bk, float(BK), wk, ALU.mult, ALU.add))
                V.link(v.tensor_copy(slot_y, sk))
                dve.wait_ge(s("idx_summed"), 1)
                V.link(v.tensor_copy(idx[0:BK, :], M[0:BK, 3, 0:NB]), s("idx_ready"))
                V.link(TN(ovc, incl.unsqueeze(1).broadcast_to((P, OVB, NE)),
                          io32[:, 0:OVB].unsqueeze(2).broadcast_to((P, OVB, NE)), ALU.is_le))
                V.link(v.tensor_reduce(ovf[:, 0:OVB], ovc, AX, ALU.add))
                V.link(TS(ovf[:, 0:OVB], ovf[:, 0:OVB], float(NE - 1), None, ALU.min))
                V.link(v.tensor_copy(ovf[:, OVB:OVB + 1], incl[:, NE - 1:NE]))
                V.link(v.tensor_copy(ovt, ovf), s("table_ready"))
                dve.wait_ge(s("r_exp"), 2)
                V.link(TS(gate[:, 0, :], wex, 1.0, None, ALU.add))
                V.link(v.reciprocal(gate[:, 0, :], gate[:, 0, :]))
                V.link(TN(gate[:, 0, :], gate[:, 0, :], gpg, ALU.mult))
                V.link(TN(gate[:, 1, :], gate[:, 0, :], wex, ALU.mult))

                for w in range(4):
                    expert_low(w, w, w)
                x_low(0, 0)
                dve_round(1, 1, 4)
                with dve.Fori(1, NE // 2) as it:
                    for b in range(2):
                        dve_round(2 * it + b, b, unit_no(2 * it + b - 1, 4))
                for w in range(2):
                    expert_low(unit_no(NE, w), raw_slot(1, w), split_slot(0, w))
                expert_act(NE - 1, 1, unit_no(NE - 1, 4))
                act_low(NE - 1, 1)
                dve.wait_ge(s("p_turned"), 1)
                V.link(v.tensor_copy(pT[:, :, :], M[:, 0:2, :]), s("pT_ready"))
                nov = dve.value_load(ovt[0:1, OVB:OVB + 1], min_val=0, max_val=OVB)

                def block(jj):
                    n, u = NE + jj, 6 * NE + 6 * jj
                    x_low(n, 0)
                    for w in range(6):
                        expert_low(u + w, w, w % 4)
                    expert_act(n, 0, u + 4)
                    act_low(n, 0)
                further_blocks(dve, nov, block)
                dve.wait_ge(s("pt_hi_ready"), 1)
                V.send(TN(pt_lo[:, :, :], pT[:, :, :], pt_hi[:, :, :].bitcast(F32), ALU.subtract), s("pt_ready"))
                for t in range(TT + 1):
                    if t < TT:
                        dve.wait_ge(s(f"yg_in{t}"), 32)
                        V.link(TS(yg[:, t, 0, :], yg[:, t, 0, :], gate[:, 0, t:t + 1], None, ALU.mult))
                        V.send(STT(yg[:, t, 0, :], yg[:, t, 1, :], gate[:, 1, t:t + 1], yg[:, t, 0, :],
                                   ALU.mult, ALU.add), s("comb_ready"))
                    if t:
                        dve.wait_ge(s("combined"), t)
                        xt = x[:, :, P * (t - 1):P * t]
                        for hf in range(2):
                            V.send(TN(xt[:, 4 * hf:4 * hf + 4, :], xt[:, 4 * hf:4 * hf + 4, :],
                                      pj[:, 2 * ((t - 1) % 2) + hf, :].rearrange("p (i n) -> p i n", n=P), ALU.add),
                                   s("x_new"))

            for g, G in enumerate(groups):
                k, j = G["kind"], G["j"]
                done = (s("subs_done"), G["end"])
                banks = pj2(g)
                free = read_out(g)
                if k == "conv_v":
                    dve.wait_ge(*read_out(g - 1))
                    dve.wait_ge(*done)
                    V.settle()
                    V.link(TN(cv[:, :, 2:], banks, cgate[:, :, :], ALU.mult), free)
                    w = lambda tap, i: cols[:, C_ACONV + 8 * tap + 2 * j + i:C_ACONV + 8 * tap + 2 * j + i + 1]
                    for i in range(2):
                        V.send(TS(cu[:, i, :], cv[:, i, 0:T], w(0, i), None, ALU.mult))
                    V.settle()
                    for tap in (1, 2):
                        for i in range(2):
                            V.send(STT(cu[:, i, :], cv[:, i, tap:tap + T], w(tap, i), cu[:, i, :], ALU.mult, ALU.add))
                        V.settle()
                elif k == "conv_b":
                    dve.wait_ge(*done)
                    V.settle()
                    V.send(TN(cu[:, :, :], banks, cu[:, :, :], ALU.mult), free)
                    mid_low(cu[:, :, :], mid_lo[:, 2 * j:2 * j + 2, :], mid_hi[:, 2 * j:2 * j + 2, :])
                elif k == "y_only":
                    if j == 0:
                        dve.wait_ge(s("y_cleared"), 128)
                    dve.wait_ge(*done)
                    V.send(v.tensor_copy(y[:, 2 * j:2 * j + 2, :], banks), free)
                elif k == "y_last":
                    dve.wait_ge(*done)
                    V.send(TN(y[:, 2 * j:2 * j + 2, :], y[:, 2 * j:2 * j + 2, :], banks, ALU.add), free)
                elif k == "ffn_u":
                    dve.wait_ge(*read_out(g - 1))
                    dve.wait_ge(*done)
                    V.send(TN(tmp[:, :, :], banks, sg[:, :, :], ALU.mult), free)
                    mid_low(tmp[:, :, :], mid_lo[:, 2 * j:2 * j + 2, :], mid_hi[:, 2 * j:2 * j + 2, :])
                elif k == "ssd_x":
                    n = j - 1
                    if j == 0:
                        ssd_head()
                    if n >= 0:
                        ssd_xdt(n)
                        if n:
                            ssd_final(n - 1)
                elif k == "ssd_bc":
                    n = j - 1
                    if n >= 0:
                        ssd_scan(n)
                        ssd_m(n, 0)
                        ssd_m(n, 1)
                        if n:
                            ssd_low(n - 1)
                    dve.wait_ge(*read_out(g - 1))
                    conv4(j, 0, xs[j % 2])
                    if j == 0:
                        ssd_head_decays()
                    if n >= 0:
                        ssd_m(n, 2)
                        ssd_m(n, 3)
                elif k == "ssd_z":
                    n = j - 1
                    advance(g + 1)
                    if n >= 0:
                        ssd_y(n)
                    dve.wait_ge(*read_out(g - 5 if j == 5 else g - 1))
                    conv4(j, 1, bct[j % 2])
                    advance(g + 2)
                    if j == SG - 1:
                        ssd_xdt(j)
                        ssd_final(n)
                        ssd_low(n)
                        ssd_scan(j)
                        for r in range(4):
                            ssd_m(j, r)
                        ssd_y(j)
                        ssd_final(j)
                        ssd_low(j)
                elif k == "gm_v" and j == 1:
                    dve.wait_ge(*read_out(g))
                    dve.wait_ge(*read_out(g - 1))
                elif k == "gm_u" and j == 1:
                    advance(g + 2)
                    layernorm_v()
                elif k == "hg_i" and j == 1:
                    advance(g + 2)
                    gmlp_out()
                elif k == "hg_f":
                    if j == 1:
                        hg_head_out(0)
                        hg_head(1)
                    hg_f(j, g)
                elif k == "hg_q":
                    if j == 1:
                        hg_head_out(1)
                    advance(g + 2)
                    hg_chain(j, g)
                elif k == "hg_og":
                    if j == 1:
                        hg_head(0)
                elif k == "gate_a" and j == 1:
                    advance(g + 2)
                    hg_head_out(2)
                elif k == "gate_b" and j == 0:
                    advance(g + 2)
                    hg_head_out(3)
                elif k == "up_a":
                    dve.wait_ge(*read_out(g - 1))
                    dve.wait_ge(*done)
                    V.send(TN(gate_of(j), banks, gate_of(j), ALU.mult), free)
                    if j < 2:
                        advance(g + 2)
                        hg_head(2 + j)
                elif k == "up_b":
                    dve.wait_ge(*read_out(g - 1))
                    dve.wait_ge(*done)
                    V.settle()
                    V.link(TN(sgb[:, :, :], banks, sgb[:, :, :], ALU.mult))
                    V.send(TN(sgb[:, :, :], sgb[:, :, :], gate_of(j), ALU.add), free)
                    mid_low(sgb[:, :, :], m2_lo[:, 2 * j:2 * j + 2, :], m2_hi[:, 2 * j:2 * j + 2, :])
                elif k == "w_out":
                    dve.wait_ge(*done)
                    V.send(TN(x[:, 2 * j:2 * j + 2, :], x[:, 2 * j:2 * j + 2, :], banks, ALU.add), free)
                elif k == "ple":
                    dve.wait_ge(*read_out(g - 1))
                    dve.wait_ge(*done)
                    V.settle()
                    V.link(TN(tmp[:, :, :], banks, sg[:, :, :], ALU.mult), free)
                    for i in range(2):
                        V.send(TN(x[:, 2 * j + i, :], x[:, 2 * j + i, :], tmp[:, i, :], ALU.add), s("x_new"))
                for c in chunk_after.get(g, ()):
                    if c:
                        V.settle()
                        coefficients(c)
                if g in step_after:
                    step(step_after[g])
                    if step_after[g] == 5:
                        dve_moe()
                        phase[0] = 1
                        advance(g + 2)
                        step(6)
                        continue
                advance(g + 2)
            step(7)
            for t in range(0, TT, 2):
                dve.wait_ge(s("o_turned"), t + 1)
                V.link(v.tensor_copy(otok[:, t, :], pj[:, 0:2, :].rearrange("p a b -> p (a b)")), s("otok_even"))

        @block.tensor
        def _(pe):
            mm, turn = nc.tensor.matmul, nc.tensor.transpose

            def ada_sum(u):
                c = chunk_of(u)
                pe.wait_ge(s("ada_acc"), u + 1)
                if u % 12 in (0, 8) and c >= 3:
                    pe.wait_ge(s("coef_read"), c - 2)
                for m in range(2):
                    ins = mm(M[:, c % 3, 2 * u + m:2 * u + m + 1], acc[:, u % 2, P * m:P * m + P], ones[:, 0:1],
                             start=True, stop=True)
                ins.then_inc(s("ada_summed"), 1)

            def step(r):
                if 1 <= r <= 4:
                    pe.wait_ge(s("ssq_ready"), 3 * r)
                    pe.wait_ge(s("rstd_x_ready"), r)
                    if r == 3:
                        pe.wait_ge(s("y_banks_read"), SG)
                    mm(M[:, 3, :], ones[:, :], ssq[:, :], start=True, stop=False)
                    pe.wait_ge(s("ysq_ready"), 4 * r)
                    mm(M[:, 3, :], ones[:, :], sqt[:, 0, :], start=False, stop=False)
                    mm(M[:, 3, :], ones[:, :], sqt[:, 1, :], start=False, stop=True).then_inc(s("ysum_ready"), 1)
                    pe.wait_ge(s("rstd_y_ready"), r)
                elif r:
                    pe.wait_ge(s("rstd_x_ready"), r)
                if r == 5:
                    pe.wait_ge(s("HS_ready"), 4)
                for i in range(DT):
                    pe.wait_ge(s("sq_ready"), 8 * r + i + 1)
                    ins = mm(M[:, 3, :], ones[:, :], y[:, i, :], start=i == 0, stop=i == DT - 1)
                ins.then_inc(s("xsum_ready"), 1)

            def products(g, G, k, q, k0, part, last):
                hi, lo = srcs[G.get("src", "h")]
                for m in range(2):
                    cols_ = slice(P * m, P * m + P)
                    o = pj[:, 2 * (g % 2) + m, :]
                    wh, wl = w_hi[:, q % 4, k - k0, cols_], w_lo[:, q % 4, k - k0, cols_]
                    mm(o, wh, hi[:, k, :], start=k == 0, stop=False)
                    mm(o, wh, lo[:, k, :], start=False, stop=False)
                    ins = mm(o, wl, hi[:, k, :], start=False, stop=k == G["nk"] - 1)
                if last:
                    ins.then_inc(s("subs_done"), 1)

            def token_products(g, G):
                for q, _, _ in G["subs"]:
                    pe.wait_ge(s("hi_ready"), q + 1)
                    pe.wait_ge(s("lo_ready"), q + 1)
                for t in range(TT):
                    o = pj[:, 2 * (g % 2) + t // 2, 256 * (t % 2):256 * (t % 2) + 256]
                    for q, k0, k1 in G["subs"]:
                        for k in range(k0, k1):
                            wh, wl = w_hi[:, q % 4, k - k0, :], w_lo[:, q % 4, k - k0, :]
                            hh, hl = h_hi[:, k, P * t:P * t + P], h_lo[:, k, P * t:P * t + P]
                            mm(o, hh, wh, start=k == 0, stop=False)
                            mm(o, hl, wh, start=False, stop=False)
                            ins = mm(o, hh, wl, start=False, stop=k == DT - 1)
                        if t == TT - 1:
                            ins.then_inc(s("subs_done"), 1)

            def ssd_head():
                pe.wait_ge(s("coef_read"), 8)
                pe.wait_ge(s("dt_low"), 1)
                for k in range(DT):
                    pe.wait_ge(s("h_ready"), 8 * HSTEP[2] + k + 1)
                    mm(M[0:SH, 0, :], wdt_hi[:, k, :], h_hi[:, k, :], start=k == 0, stop=False)
                    mm(M[0:SH, 0, :], wdt_hi[:, k, :], h_lo[:, k, :], start=False, stop=False)
                    ins = mm(M[0:SH, 0, :], wdt_lo[:, k, :], h_hi[:, k, :], start=False, stop=k == DT - 1)
                ins.then_inc(s("dt_raw"), 1)

            def ssd_head_turn():
                pe.wait_ge(s("dt_low"), 2)
                for t in range(TT):
                    ins = turn(M[:, 1, SH * t:SH * t + SH], dtr[:, P * t:P * t + P], ident[0:SH, 0:SH])
                ins.then_inc(s("dt_raw"), 1)

            def ssd_head_sums():
                pe.wait_ge(s("sp_ready"), 2)
                dAf = dA[:, :, :].rearrange("p c h -> p (c h)")
                mm(M[:, 1, 0:P], tri[:, :], dAf, start=True, stop=True)
                for k in range(3):
                    for c in range(SC):
                        mm(M[SH * k:SH * k + SH, 2, P * c:P * c + P], dA[:, c, :], tri[:, :], start=True, stop=True)
                mm(M[:, 1, P:2 * P], ones[:, :], dAf, start=True, stop=True).then_inc(s("cs_ready"), 1)

            def ssd_a1(n):
                pe.wait_ge(s("xbc_ready"), 4 * n + 2)
                if n == 0:
                    pe.wait_ge(s("ncs_ready"), 2)
                    pe.wait_ge(s("dtex_ready"), 2)
                else:
                    pe.wait_ge(s("y_banks_read"), n)
                for c in range(SC):
                    for i in range(2):
                        ins = turn(Mf[:, 256 * c + P * i:256 * c + P * i + P], xs[n % 2][:, i, P * c:P * c + P],
                                   ident[:, :])
                ins.then_inc(s("ssd_turned"), 1)

            def ssd_a2(n):
                pe.wait_ge(s("xbc_ready"), 4 * n + 4)
                if n:
                    pe.wait_ge(s("yg_rstd"), n)
                for c in range(SC):
                    turn(M[:, 2, P * c:P * c + P], bct[n % 2][:, 0, P * c:P * c + P], ident[:, :])
                for c in range(SC):
                    ins = mm(M[:, 3, P * c:P * c + P], bct[n % 2][:, 0, P * c:P * c + P],
                             bct[n % 2][:, 1, P * c:P * c + P], start=True, stop=True)
                ins.then_inc(s("ssd_turned2"), 1)

            def ssd_csb(n, r):
                if r < 2:
                    pe.wait_ge(s("xdt_ready"), n + 1)
                else:
                    pe.wait_ge(s("dec_ready"), 16 * n + 4 * (r - 2) + 4)
                h = 4 * n + r
                mm(M[:, r % 2, :], bc(sel3[0:3 * SH, h:h + 1], (3 * SH, P)), csr[:, :], start=True, stop=False)
                mm(M[:, r % 2, :], identb[:, :], negb[:, :, :].rearrange("p c n -> p (c n)"), start=False,
                   stop=True).then_inc(s("csb_ready"), 1)

            def ssd_states(n):
                pe.wait_ge(s("bt_ready"), 2 * n + 2)
                pe.wait_ge(s("xdt_ready"), n + 1)
                for c in range(3):
                    o = M[:, 2, 256 * c:256 * c + 256] if c < 2 else M[:, 3, 0:256]
                    ins = mm(o, btok[:, c, :], xdte[:, c, :], start=True, stop=True)
                ins.then_inc(s("ssd_states"), 1)

            def ssd_ydiag(n, r):
                pe.wait_ge(s("m_ready"), 4 * n + r + 1)
                pe.wait_ge(s("S_ready"), n + 1)
                i, hf = r // 2, r % 2
                for c in range(SC):
                    mm(M[64 * hf:64 * hf + 64, 2 + i, P * c:P * c + P], xdt[:, c, 64 * r:64 * r + 64],
                       dec[:, r % 2, c, :], start=True, stop=True)

            def ssd_ecs(n):
                pe.wait_ge(s("dec_ready"), 16 * n + 16)
                for r in range(4):
                    h, hf = 4 * n + r, r % 2
                    ins = mm(M[64 * hf:64 * hf + 64, r // 2, :], bc(sel3[0:3 * SH, h:h + 1], (3 * SH, 64)), csr[:, :],
                             start=True, stop=True)
                ins.then_inc(s("ecs_ready"), 1)

            def ssd_yoff(n):
                pe.wait_ge(s("yy_ready"), n + 1)
                for i in range(2):
                    for c in range(1, SC):
                        ins = mm(M[:, i, P * c:P * c + P], S[:, c - 1, P * i:P * i + P],
                                 bct[n % 2][:, 1, P * c:P * c + P], start=True, stop=True)
                ins.then_inc(s("ssd_yoff"), 1)

            def ssd_ynorm(n):
                pe.wait_ge(s("ygsq_ready"), n + 1)
                mm(M[:, 2, :], ones[:, :], yq[n % 4][:, 0, :], start=True, stop=False)
                mm(M[:, 2, :], ones[:, :], yq[n % 4][:, 1, :], start=False, stop=True).then_inc(s("yg_summed"), 1)

            def turn_wsp():
                pe.wait_ge(s("gm_in"), 80)
                for i in range(GW // 64):
                    ins = turn(Mf[:, P * i:P * i + P], wsp[:, i, :], ident[:, :])
                ins.then_inc(s("wsp_turned"), 1)

            def gm_mix():
                pe.wait_ge(s("gm_ready"), 1)
                for i in range(4):
                    for c in range(TT):
                        for hf in range(2):
                            w = 2 * i + hf
                            ins = mm(M[64 * hf:64 * hf + 64, i, P * c:P * c + P], vn[:, c, 64 * w:64 * w + 64],
                                     wspT[:, w, :], start=True, stop=True)
                ins.then_inc(s("gm_mixed"), 1)

            def hg_scores(n):
                i = n % 2
                pe.wait_ge(s("hg_ops_ready"), n // 2 + 1)
                if n:
                    pe.wait_ge(s("on_ready"), n)
                else:
                    pe.wait_ge(s("gm_y"), 2)
                for b in range(TT):
                    mm(M[:, 0, P * b:P * b + P], fk[:, i, P * b:P * b + P], qd[:, i, P * b:P * b + P],
                       start=True, stop=True)
                for b in range(TT):
                    ins = turn(M[:, 1, P * b:P * b + P], ke[:, i, P * b:P * b + P], ident[:, :])
                ins.then_inc(s("hg_scores"), 1)

            def hg_dstate(n):
                pe.wait_ge(s("ketok_ready"), n + 1)
                if n:
                    pe.wait_ge(s("HS_ready"), n)
                for c in range(7):
                    p0 = 64 * (c % 2)
                    ins = mm(M[:, 2 + c % 2, P * (c // 2):P * (c // 2) + P], ketok[p0:p0 + 64, c // 2, :],
                             vtok[p0:p0 + 64, c // 2, P * n:P * n + P], start=True, stop=True)
                ins.then_inc(s("hg_dS"), 1)

            def hg_out(n):
                pe.wait_ge(s("att_ready"), n + 1)
                pe.wait_ge(s("HS_ready"), n + 1)
                for b in range(TT):
                    mm(M[:, 0, P * b:P * b + P], vtok[:, b, P * n:P * n + P], att[:, b, :], start=True, stop=False)
                    for c in (2 * b, 2 * b + 1):
                        if c:
                            ins = mm(M[:, 0, HC * c:HC * c + HC], HS[:, c - 1, :], qd[:, n % 2, HC * c:HC * c + HC],
                                     start=False, stop=c % 2 == 1)
                ins.then_inc(s("hg_out"), 1)

            def hg_norm(n):
                pe.wait_ge(s("osq_ready"), n + 1)
                mm(M[:, 1, :], ones[:, :], hsq[:, :], start=True, stop=True).then_inc(s("osum_ready"), 1)

            def carry_wait(o):
                mm(o, ones[:, :], ones[:, 0:1], start=True, stop=True)

            def turn_xg(b):
                carry_wait(M[:, b, 0:1])
                for k in range(DT):
                    ins = turn(M[:, b, BK * k:BK * k + BK], xg[:, b, P * k:P * k + P], ident[0:BK, 0:BK])
                ins.then_inc(s("e_turned"), 1)

            def unit(u, slot, v, b):
                pe.wait_ge(s("elo_ready"), u + 1)
                hi, lo = (xgT_hi, xgT_lo) if v < 4 else (a_hi, a_lo)
                o = M[0:BK, 2 + v // 2, :] if v < 4 else pj[0:BK, v - 2, :]
                k0 = 4 * (v % 2) if v < 4 else 0
                for k in range(4):
                    first_, last = k == 0 and (v >= 4 or v % 2 == 0), k == 3 and (v >= 4 or v % 2 == 1)
                    mm(o, hi[:, b, k0 + k, :], ew_hi[:, slot, k, :], start=first_, stop=False)
                    mm(o, hi[:, b, k0 + k, :], ew_lo[:, slot, k, :], start=False, stop=False)
                    ins = mm(o, lo[:, b, k0 + k, :], ew_hi[:, slot, k, :], start=False, stop=last)
                ins.then_inc(s("e_units"), 1)

            def turn_act(b):
                carry_wait(pj[:, 0, 0:1])
                for k in range(4):
                    ins = turn(pj[:, 0, BK * k:BK * k + BK], eact[:, b, P * k:P * k + P], ident[0:BK, 0:BK])
                ins.then_inc(s("e_aturned"), 1)

            def pe_round(e, par, gathers):
                for v in range(6):
                    if v == 0:
                        pe.wait_ge(s("e_xlo"), e + 1)
                        pe.wait_ge(s("e_sg"), e)
                    elif v == 2:
                        pe.wait_ge(s("e_act"), e)
                        if not isinstance(e, int) or e >= 2:
                            pe.wait_ge(s("e_alo"), e - 1)
                        turn_act(1 - par)
                    elif v == 4:
                        if gathers is not None:
                            pe.wait_ge(s(f"xg_in{1 - par}"), 16 * gathers)
                            pe.wait_ge(s("e_xlo"), e)
                            turn_xg(1 - par)
                        pe.wait_ge(s("e_alo"), e)
                        if not isinstance(e, int) or e >= 2:
                            pe.wait_ge(s("e_ytok"), e - 1)
                    unit(unit_no(e, v), split_slot(par, v), v, par if v < 4 else 1 - par)

            def moe_program():
                pe.wait_ge(s("wr_in"), 32)
                for k in range(DT):
                    pe.wait_ge(s("mh_ready"), k + 1)
                    ins = mm(M[0:36, 1, :], wr[:, k, :], y[:, k, :], start=k == 0, stop=k == DT - 1)
                ins.then_inc(s("logit_rows"), 1)
                pe.wait_ge(s("lgs_ready"), 1)
                for t in range(TT):
                    ins = turn(M[:, 0, 36 * t:36 * t + 36], lgs[:, P * t:P * t + P], ident[0:36, 0:36])
                ins.then_inc(s("logits"), 1)
                pe.wait_ge(*read_out(n_pre - 1))
                pe.wait_ge(*read_out(n_pre - 2))

                def turn_rows_of_h(t):
                    if t >= 2:
                        pe.wait_ge(s("htok_ready"), t - 1)
                    rows = pj[:, 2 * (t % 2):2 * (t % 2) + 2, :].rearrange("p a b -> p (a b)")
                    for i in range(DT):
                        ins = turn(rows[:, P * i:P * i + P], y[:, i, P * t:P * t + P], ident[:, :])
                    ins.then_inc(s("h_turned"), 1)

                turn_rows_of_h(0)
                turn_rows_of_h(1)
                pe.wait_ge(s("chosen"), 1)
                for t in range(TT):
                    o = M[:, 1, NE * t:NE * t + NE]
                    mm(o, stri[:, :], Aall[:, t, :], start=True, stop=t == 0)
                    for u in range(t):
                        mm(o, ones[:, :], Aall[:, u, :], start=False, stop=u == t - 1)
                for t in range(TT):
                    ins = mm(M[:, 2, 0:NE], ones[:, :], Aall[:, t, :], start=t == 0, stop=t == TT - 1)
                ins.then_inc(s("ranks"), 1)
                turn_rows_of_h(2)
                turn_rows_of_h(3)
                pe.wait_ge(s("slots_ready"), 1)
                for u in range(2 * TT):
                    ins = mm(M[0:BK, 3, 0:NB], hot_w[:, u, :], hot_b[:, u, :], start=u == 0, stop=u == 2 * TT - 1)
                ins.then_inc(s("idx_summed"), 1)
                pe.wait_ge(s("htok_ready"), TT)
                for b in range(2):
                    pe.wait_ge(s(f"xg_in{b}"), 16)
                    turn_xg(b)
                pe.wait_ge(s("e_xlo"), 1)
                for v in range(4):
                    unit(v, v, v, 0)
                pe_round(1, 1, 2)
                with pe.Fori(1, NE // 2 - 1) as it:
                    pe_round(2 * it, 0, it + 1)
                    pe_round(2 * it + 1, 1, it + 2)
                pe_round(NE - 2, 0, NE // 2)
                pe_round(NE - 1, 1, None)
                pe.wait_ge(s("e_act"), NE)
                pe.wait_ge(s("e_alo"), NE - 1)
                turn_act(1)
                pe.wait_ge(s("e_alo"), NE)
                pe.wait_ge(s("e_ytok"), NE - 1)
                for v in range(2):
                    unit(unit_no(NE, v), split_slot(0, v), 4 + v, 1)
                pe.wait_ge(s("p_in"), 16)
                pe.wait_ge(s("e_xlo"), NE)
                for i in range(2):
                    for t in range(TT):
                        ins = turn(M[:, i, P * t:P * t + P], ptok[:, t, P * i:P * i + P], ident[:, :])
                ins.then_inc(s("p_turned"), 1)
                pe.wait_ge(s("pT_ready"), 1)
                pe.wait_ge(s("table_ready"), 1)
                nov = pe.value_load(ovt[0:1, OVB:OVB + 1], min_val=0, max_val=OVB)

                def block(j):
                    n, u = NE + j, 6 * NE + 6 * j
                    pe.wait_ge(s("xg_in0"), 8 * NE + 16 + 16 * j)
                    pe.wait_ge(s("e_xlo"), n)
                    turn_xg(0)
                    pe.wait_ge(s("e_xlo"), n + 1)
                    pe.wait_ge(s("e_sg"), n)
                    pe.wait_ge(s("e_act"), n)
                    for v in range(4):
                        unit(u + v, v, v, 0)
                    pe.wait_ge(s("e_act"), n + 1)
                    pe.wait_ge(s("e_alo"), n)
                    turn_act(0)
                    pe.wait_ge(s("e_alo"), n + 1)
                    pe.wait_ge(s("e_ytok"), n)
                    for v in (4, 5):
                        unit(u + v, v % 4, v, 0)
                further_blocks(pe, nov, block)
                pe.wait_ge(s("rows_done"), 1)
                mm(M[:, 3, 0:1], ones[:, :], ones[:, 0:1], start=True, stop=True).then_inc(s("experts_done"), 1)
                for t in range(TT):
                    pe.wait_ge(s("comb_ready"), t + 1)
                    if t >= 2:
                        pe.wait_ge(s("x_new"), 40 + 2 * (t - 1))
                    o = pj[:, 2 * (t % 2):2 * (t % 2) + 2, :].rearrange("p a b -> p (a b)")
                    for i in range(DT):
                        ins = turn(o[:, P * i:P * i + P], yg[:, t, 0, P * i:P * i + P], ident[:, :])
                    ins.then_inc(s("combined"), 1)

            def ssd_hook(k, n, slot):
                if k == "ssd_x":
                    if slot == 1:
                        ssd_a1(n)
                        if n:
                            ssd_ynorm(n - 1)
                    elif slot == 3:
                        ssd_csb(n, 0)
                        ssd_csb(n, 1)
                        ssd_a2(n)
                elif k == "ssd_bc":
                    if slot == 1:
                        ssd_states(n)
                    elif slot == 2:
                        ssd_ydiag(n, 0)
                        ssd_csb(n, 2)
                    elif slot == 3:
                        ssd_ydiag(n, 1)
                        ssd_csb(n, 3)
                elif slot == 0:
                    ssd_ydiag(n, 2)
                elif slot == 1:
                    ssd_ydiag(n, 3)
                    ssd_ecs(n)
                elif slot == 2:
                    ssd_yoff(n)

            def hook(k, j, slot):
                n = j - 1
                if k in ("ssd_x", "ssd_bc", "ssd_z"):
                    if n >= 0:
                        ssd_hook(k, n, slot)
                    elif (k, slot) == ("ssd_x", 0):
                        ssd_head_turn()
                    elif (k, slot) == ("ssd_bc", 1):
                        ssd_head_sums()
                    if k == "ssd_z" and j == SG - 1 and slot == 3:
                        for k_ in ("ssd_x", "ssd_bc", "ssd_z"):
                            for sl in range(4):
                                ssd_hook(k_, j, sl)
                        ssd_ynorm(j)
                elif (k, j) in HG_HOOKS and slot in HG_HOOKS[k, j]:
                    for step_of, n in HG_HOOKS[k, j][slot]:
                        (hg_scores, hg_dstate, hg_out, hg_norm)[step_of](n)

            HG_HOOKS = {("hg_og", 0): {3: [(0, 0)]}, ("hg_og", 1): {1: [(1, 0)], 3: [(2, 0)]},
                        ("hg_f", 1): {0: [(3, 0)], 3: [(0, 1)]}, ("hg_q", 1): {1: [(1, 1)], 3: [(2, 1)]},
                        ("gate_a", 0): {0: [(3, 1)]},
                        ("gate_a", 1): {0: [(0, 2)], 2: [(1, 2)]}, ("up_a", 1): {0: [(2, 2)], 1: [(3, 2)]},
                        ("gate_b", 0): {1: [(0, 3)], 2: [(1, 3)], 3: [(2, 3)]}, ("up_b", 0): {0: [(3, 3)]}}

            pe.wait_ge(s("const_ready"), 1)
            pe.wait_ge(s("params_in"), 16 * 13)
            for t in range(4):
                n = P if t < 3 else C_END - 3 * P
                ins = turn(M[:, 0, P * t:P * t + n], stage[0:n, t, :], ident[0:n, 0:n])
            ins.then_inc(s("params_turned"), 1)
            pe.wait_ge(s("x_in"), 16)
            for i in range(DT):
                if i >= 4:
                    pe.wait_ge(s("x_new"), i - 3)
                for t in range(TT):
                    ins = turn(pj[:, i % 4, P * t:P * t + P], xtok[:, t, P * i:P * i + P], ident[:, :])
                ins.then_inc(s("x_turned"), 1)
            pe.wait_ge(s("x_new"), 8)
            pe.wait_ge(s("cols_ready"), 1)
            for u in ada_at[0]:
                ada_sum(u)
            step(0)
            for g, G in enumerate(groups):
                if g >= 2:
                    pe.wait_ge(*read_out(g - 2))
                if g:
                    for u in ada_at.get(g, ()):
                        ada_sum(u)
                if G["kind"] == "ssd_x" and G["j"] == 0:
                    ssd_head()
                sem, base = G.get("wait", (None, 0))
                if G.get("tok"):
                    if sem:
                        pe.wait_ge(s(sem), base + DT)
                    token_products(g, G)
                else:
                    for n_sub, (q, k0, k1) in enumerate(G["subs"]):
                        pe.wait_ge(s("hi_ready"), q + 1)
                        pe.wait_ge(s("lo_ready"), q + 1)
                        for k in range(k0, k1):
                            if sem in ("mid_ready", "ya_ready"):
                                pe.wait_ge(s(sem), base + k // 2 + 1)
                            elif sem:
                                pe.wait_ge(s(sem), base + (0 if sem == "pt_ready" else k) + 1)
                            products(g, G, k, q, k0, n_sub, k == k1 - 1)
                            if k % 2:
                                hook(G["kind"], G["j"], k // 2)
                if (G["kind"], G["j"]) == ("gm_u", 0):
                    turn_wsp()
                elif (G["kind"], G["j"]) == ("hg_i", 1):
                    gm_mix()
                if g in step_after:
                    step(step_after[g])
                    if step_after[g] == 5:
                        moe_program()
                        step(6)
            step(7)
            pe.wait_ge(s("fin_ready"), 8)
            for t in range(TT):
                if t >= 2:
                    pe.wait_ge(s("otok_odd" if t % 2 else "otok_even"), 1)
                o = pj[:, 2 * (t % 2):2 * (t % 2) + 2, :].rearrange("p a b -> p (a b)")
                for i in range(DT):
                    ins = turn(o[:, P * i:P * i + P], y[:, i, P * t:P * t + P], ident[:, :])
                ins.then_inc(s("o_turned"), 1)


_INS = ("x", "c", "ada_w", "ada_b", "norm_g", "a_w_in", "a_conv_w", "a_w_out", "m_w_in", "m_conv_w", "m_conv_b",
        "m_dt_bias", "m_a_log", "m_d", "m_norm_g", "m_w_out", "f_w_in", "f_w_out", "p_2", "g_mix_2", "w_in_2",
        "gm_ln_g_2", "gm_ln_b_2", "gm_w_sp_2", "gm_b_sp_2", "w_up_a_2", "hg_lb_param_2", "hg_norm_g_2", "w_up_b_2",
        "w_out_2", "g_ffn_2", "w_grp_2", "w_exp_2", "w1_2", "w3_2", "w2_2", "g_ple_2", "w_pg_2", "w_ple_2", "g_final_2")


def kernel(**inputs):
    import numpy as _np
    import concourse.bacc as _bacc
    from concourse import mybir as _mybir
    from concourse.bass_utils import run_bass_kernel_spmd as _run

    nc = _bacc.Bacc("TRN2", target_bir_lowering=False, num_devices=1)
    arrays, args = {}, {}
    for name in _INS:
        a = _np.ascontiguousarray(inputs[name])
        arrays[f"in_{name}_dram"] = a
        args[name] = nc.dram_tensor(f"in_{name}_dram", a.shape, _mybir.dt.from_np(a.dtype), kind="ExternalInput").ap()
    out = nc.dram_tensor("out_0_dram", (1, T, D), F32, kind="ExternalOutput").ap()
    build(nc, args, out)
    r = _run(nc, [arrays], core_ids=[0])
    return r.results[0]["out_0_dram"]
```
